# Optimizing a Trainium2 kernel written in Bass

```python
import jax, jax.numpy as jnp
from jax import lax
import numpy as np

D_MODEL = 1024
BATCH = 1
SEQ = 128
DEPTH = 2
DEC_BATCH = 1
DEC_SEQ = 256
PAST_LEN = 128

GRID_W = 64
NA_HEADS = 8
NA_HEAD_DIM = 64
NA_WIDTH = NA_HEADS * NA_HEAD_DIM
WIN_R = 8
WIN_C = 16
NA_QB = WIN_C
NA_KBW = 2 * WIN_C
CTX_QBLOCK = 128
NEG_INF = -1e30
RET_HEADS = 4
RET_DK = 64
RET_DV = 128
RET_QK_WIDTH = RET_HEADS * RET_DK
RET_V_WIDTH = RET_HEADS * RET_DV
RET_CHUNK = 64
RET_GN_EPS = 1e-5
ROPE_BASE = 10000.0
RWKV_HEADS = 8
RWKV_N = 64
RWKV_WIDTH = RWKV_HEADS * RWKV_N
RWKV_LORA_W = 64
RWKV_LORA_A = 64
RWKV_LORA_G = 128
RWKV_DECAY_SCALE = 0.606531
RWKV_GN_EPS = 64e-5
RWKV_SIZES = (RWKV_WIDTH, RWKV_WIDTH, RWKV_WIDTH, RWKV_LORA_W, RWKV_LORA_W, RWKV_LORA_A, RWKV_LORA_A, RWKV_LORA_G)
RWKV_SHIFT_WIDTH = 3 * RWKV_WIDTH + 2 * RWKV_LORA_W + 2 * RWKV_LORA_A + RWKV_LORA_G
N_BRANCH = 3
BRANCH_WIDTH = 512
IN_SIZES = (NA_WIDTH, NA_WIDTH, NA_WIDTH, RET_QK_WIDTH, RET_QK_WIDTH, RET_V_WIDTH, RET_V_WIDTH,
            RWKV_SHIFT_WIDTH, D_MODEL, D_MODEL, D_MODEL)
P_IN = 3 * NA_WIDTH + 2 * RET_QK_WIDTH + 2 * RET_V_WIDTH + RWKV_SHIFT_WIDTH + N_BRANCH * D_MODEL
PEER_HEADS = 8
PEER_NKEYS = 128
PEER_N_EXPERTS = PEER_NKEYS * PEER_NKEYS
PEER_DK = 128
PEER_TOPK = 16
PEER_TOK_BLOCK = 128
LN_EPS = 1e-5
DEEPNORM_ALPHA = (2 * DEPTH) ** 0.25
DEEPNORM_BETA = (8 * DEPTH) ** -0.25

kernel_name = 'hybrid_natten_retnet_rwkv7_peer_diffusion_step'

def _split_points(sizes):
    return [int(s) for s in np.cumsum(sizes)[:-1]]

def flip(t):
    return t[:, ::-1]

def layer_norm(x, g=None, b=None):
    xf = x.astype(jnp.float32)
    mu = jnp.mean(xf, -1, keepdims=True)
    var = jnp.mean(jnp.square(xf - mu), -1, keepdims=True)
    y = (xf - mu) * lax.rsqrt(var + LN_EPS)
    if g is not None:
        y = y * g.astype(jnp.float32) + b.astype(jnp.float32)
    return y.astype(x.dtype)

def head_norm(x, g, b, eps):
    bsz, t_len, nh, n = x.shape
    xf = x.astype(jnp.float32)
    mu = jnp.mean(xf, -1, keepdims=True)
    var = jnp.mean(jnp.square(xf - mu), -1, keepdims=True)
    y = ((xf - mu) * lax.rsqrt(var + eps)).reshape(bsz, t_len, nh * n)
    return y * g.astype(jnp.float32) + b.astype(jnp.float32)

def centered_shift(z, mu):
    zp = jnp.pad(z, ((0, 0), (1, 1), (0, 0)))
    return z + mu * (0.5 * (zp[:, :-2] + zp[:, 2:]) - z)

def axial_rope(x):
    t_len, d = x.shape[1], x.shape[-1]
    half, quarter = d // 2, d // 4
    pos = jnp.arange(t_len)
    freqs = 1.0 / (ROPE_BASE ** (jnp.arange(quarter, dtype=jnp.float32) / quarter))
    xf = x.astype(jnp.float32)

    def rot(part, p_axis):
        ang = p_axis.astype(jnp.float32)[:, None] * freqs[None, :]
        cos, sin = jnp.cos(ang)[None, :, None, :], jnp.sin(ang)[None, :, None, :]
        p1, p2 = part[..., :quarter], part[..., quarter:]
        return jnp.concatenate([p1 * cos - p2 * sin, p1 * sin + p2 * cos], axis=-1)

    out = jnp.concatenate([rot(xf[..., :half], pos // GRID_W), rot(xf[..., half:], pos % GRID_W)], axis=-1)
    return out.astype(x.dtype)

def ctx_attention(q, k, v):
    bsz, l_len, nh, dh = q.shape
    nb = l_len // CTX_QBLOCK
    kt, vt = k.transpose(0, 2, 1, 3), v.transpose(0, 2, 1, 3)
    qblocks = q.reshape(bsz, nb, CTX_QBLOCK, nh, dh).transpose(1, 0, 3, 2, 4)

    def blk(qb):
        s = jnp.einsum('bhqd,bhkd->bhqk', qb, kt).astype(jnp.float32) * dh ** -0.5
        p = jax.nn.softmax(s, axis=-1).astype(v.dtype)
        return jnp.einsum('bhqk,bhkd->bhqd', p, vt)

    o = lax.map(blk, qblocks)
    return o.transpose(1, 0, 3, 2, 4).reshape(bsz, l_len, nh * dh)

def na_latent(q, k, v, ctx_k, ctx_v, rpb):
    bsz, t_len, nh, dh = q.shape
    rows = t_len // GRID_W
    kr = min(WIN_R, rows)
    ncb = GRID_W // NA_QB
    scale = dh ** -0.5

    def grid(z):
        return z.reshape(bsz, rows, GRID_W, nh, dh).transpose(0, 3, 1, 2, 4)

    qg, kg, vg = grid(q), grid(k), grid(v)
    r_ar = jnp.arange(rows)
    row_idx = jnp.clip(r_ar - kr // 2, 0, rows - kr)[:, None] + jnp.arange(kr)[None, :]
    cb_start = jnp.clip(jnp.arange(ncb) * NA_QB - WIN_C // 2, 0, GRID_W - NA_KBW)
    col_idx = cb_start[:, None] + jnp.arange(NA_KBW)[None, :]
    nw = kr * NA_KBW

    def gather(z):
        zb = z[:, :, row_idx[:, :, None, None], col_idx[None, None, :, :]]
        return zb.transpose(0, 1, 2, 4, 3, 5, 6).reshape(bsz, nh, rows, ncb, nw, dh)

    kb, vb = gather(kg), gather(vg)
    qb = qg.reshape(bsz, nh, rows, ncb, NA_QB, dh)
    q_col = jnp.arange(GRID_W).reshape(ncb, NA_QB)
    q_start = jnp.clip(q_col - WIN_C // 2, 0, GRID_W - WIN_C)
    rel = col_idx[:, None, :] - q_start[:, :, None]
    valid = (rel >= 0) & (rel < WIN_C)
    valid = jnp.broadcast_to(valid[:, :, None, :], (ncb, NA_QB, kr, NA_KBW)).reshape(ncb, NA_QB, nw)
    dr_i = row_idx - r_ar[:, None] + WIN_R - 1
    dc_i = jnp.clip(col_idx[:, None, :] - q_col[:, :, None], -(WIN_C - 1), WIN_C - 1) + WIN_C - 1
    bias = rpb.astype(jnp.float32)[:, dr_i[:, None, None, :, None], dc_i[None, :, :, None, :]]
    bias = bias.reshape(nh, rows, ncb, NA_QB, nw)
    s_win = jnp.einsum('bhrcqd,bhrckd->bhrcqk', qb, kb).astype(jnp.float32) * scale + bias[None]
    s_win = jnp.where(valid[None, None, None], s_win, NEG_INF)
    s_ctx = jnp.einsum('bhrcqd,bhld->bhrcql', qb, ctx_k).astype(jnp.float32) * scale
    p = jax.nn.softmax(jnp.concatenate([s_win, s_ctx], axis=-1), axis=-1).astype(v.dtype)
    o = (jnp.einsum('bhrcqk,bhrckd->bhrcqd', p[..., :nw], vb)
         + jnp.einsum('bhrcql,bhld->bhrcqd', p[..., nw:], ctx_v))
    return o.reshape(bsz, nh, rows, GRID_W, dh).transpose(0, 2, 3, 1, 4).reshape(bsz, t_len, nh * dh)

def retention_scan(q, k, v, gamma, s0):
    bsz, t_len, nh, dk = q.shape
    dv = v.shape[-1]
    c = RET_CHUNK
    n = t_len // c
    lg = jnp.log(gamma)
    i = jnp.arange(c, dtype=jnp.float32)
    diff = i[:, None] - i[None, :]
    mask = jnp.where(diff >= 0, jnp.exp(jnp.maximum(diff, 0.0)[None] * lg[:, None, None]), 0.0)
    q_dec = jnp.exp((i + 1.0)[:, None] * lg[None, :])[None, :, :, None]
    k_dec = jnp.exp((c - 1.0 - i)[:, None] * lg[None, :])[None, :, :, None]
    c_dec = jnp.exp(c * lg)[None, :, None, None]

    def to_chunks(z):
        return z.astype(jnp.float32).reshape(bsz, n, c, nh, z.shape[-1]).transpose(1, 0, 2, 3, 4)

    def step(s, inp):
        qc, kc, vc = inp
        att = jnp.einsum('bihd,bjhd->bhij', qc, kc) * mask
        o = jnp.einsum('bhij,bjhv->bihv', att, vc) + jnp.einsum('bihd,bhdv->bihv', qc * q_dec, s)
        s = s * c_dec + jnp.einsum('bjhd,bjhv->bhdv', kc * k_dec, vc)
        return s, o

    s_fin, o = lax.scan(step, s0.astype(jnp.float32), (to_chunks(q), to_chunks(k), to_chunks(v)))
    return o.transpose(1, 0, 2, 3, 4).reshape(bsz, t_len, nh, dv), s_fin

def rwkv7_scan(r, w, k, v, kk, a, s0):
    def tm(z):
        return jnp.moveaxis(z.astype(jnp.float32), 1, 0)

    def step(s, inp):
        r_t, w_t, k_t, v_t, kk_t, a_t = inp
        sk = jnp.einsum('bhvk,bhk->bhv', s, kk_t)
        s = s * w_t[:, :, None, :] - sk[..., None] * (kk_t * a_t)[:, :, None, :] + v_t[..., None] * k_t[:, :, None, :]
        return s, jnp.einsum('bhvk,bhk->bhv', s, r_t)

    s_fin, o = lax.scan(step, s0.astype(jnp.float32), (tm(r), tm(w), tm(k), tm(v), tm(kk), tm(a)))
    return jnp.moveaxis(o, 0, 1), s_fin

def token_mix(h, p, ctx):
    bsz, t_len, _ = h.shape
    f32 = jnp.float32
    lat = ctx is not None

    def heads(t, nh):
        return t.reshape(bsz, t_len, nh, -1)

    z = h @ p['w_in']
    (q_na, k_na, v_na, q_rt, k_rt, v_rt, g_rt, z_rw, g_a, g_b, g_c) = jnp.split(z, _split_points(IN_SIZES), axis=-1)

    q_na, k_na, v_na = heads(q_na, NA_HEADS), heads(k_na, NA_HEADS), heads(v_na, NA_HEADS)
    if lat:
        o_na = na_latent(q_na, k_na, v_na, ctx[0], ctx[1], p['na_rpb'])
    else:
        o_na = ctx_attention(q_na, k_na, v_na)

    q_rt, k_rt, v_rt = heads(q_rt, RET_HEADS), heads(k_rt, RET_HEADS), heads(v_rt, RET_HEADS)
    if lat:
        q_rt, k_rt = axial_rope(q_rt), axial_rope(k_rt)
        s_ret0 = ctx[2]
    else:
        s_ret0 = jnp.zeros((bsz, 2, RET_HEADS, RET_DK, RET_DV), f32)
    k_rt = k_rt * RET_DK ** -0.5
    gam = jax.nn.sigmoid(p['ret_decay_logit'].astype(f32))
    o_f, s_f = retention_scan(q_rt, k_rt, v_rt, gam[0], s_ret0[:, 0])
    o_b, s_b = retention_scan(flip(q_rt), flip(k_rt), flip(v_rt), gam[1], s_ret0[:, 1])
    o_rt = (head_norm(o_f + flip(o_b), p['ret_gn_w'], p['ret_gn_b'], RET_GN_EPS)
            * jax.nn.silu(g_rt.astype(f32))).astype(h.dtype)

    z_rw = centered_shift(z_rw, p['rwkv_mu'])
    r_c, k_c, v_c, wl_f, wl_b, al_f, al_b, gl = jnp.split(z_rw, _split_points(RWKV_SIZES), axis=-1)
    g_rw = jax.nn.sigmoid(gl) @ p['rwkv_g_up']
    kk = heads((k_c * p['rwkv_k_k']).astype(f32), RWKV_HEADS)
    kk = kk * lax.rsqrt(jnp.maximum(jnp.sum(kk * kk, -1, keepdims=True), 1e-24))
    r_h, v_h, k_h = heads(r_c, RWKV_HEADS), heads(v_c, RWKV_HEADS), heads(k_c, RWKV_HEADS)
    s_rw0 = ctx[3] if lat else jnp.zeros((bsz, 2, RWKV_HEADS, RWKV_N, RWKV_N), f32)
    outs, states = [], []
    for d, (wl, al) in enumerate(((wl_f, al_f), (wl_b, al_b))):
        w = jnp.exp(-RWKV_DECAY_SCALE * jax.nn.sigmoid((p['rwkv_w0'][d] + jnp.tanh(wl) @ p['rwkv_w_up'][d]).astype(f32)))
        a = jax.nn.sigmoid((p['rwkv_a0'][d] + al @ p['rwkv_a_up'][d]).astype(f32))
        k_d = k_c.astype(f32) * (1.0 + (a - 1.0) * p['rwkv_k_a'].astype(f32))
        seq = (r_h, heads(w, RWKV_HEADS), heads(k_d, RWKV_HEADS), v_h, kk, heads(a, RWKV_HEADS))
        if d == 1:
            seq = tuple(flip(t) for t in seq)
        o, s = rwkv7_scan(*seq, s_rw0[:, d])
        outs.append(flip(o) if d == 1 else o)
        states.append(s)
    bonus = jnp.sum(r_h.astype(f32) * k_h.astype(f32) * p['rwkv_r_k'].astype(f32), -1, keepdims=True) * v_h.astype(f32)
    o_rw = ((head_norm(outs[0] + outs[1], p['rwkv_gn_w'], p['rwkv_gn_b'], RWKV_GN_EPS)
             + bonus.reshape(bsz, t_len, RWKV_WIDTH)) * g_rw.astype(f32)).astype(h.dtype)

    w_br = p['w_br']
    merged = (jax.nn.sigmoid(g_a) * (o_na @ w_br[0])
              + jax.nn.sigmoid(g_b) * (o_rt @ w_br[1])
              + jax.nn.sigmoid(g_c) * (o_rw @ w_br[2]))
    out = merged @ p['w_out']
    if lat:
        return out, None
    return out, (k_na.transpose(0, 2, 1, 3), v_na.transpose(0, 2, 1, 3),
                 jnp.stack([s_f, s_b], axis=1), jnp.stack(states, axis=1))

def peer(h, wq, keys, u, v):
    bsz, t_len, d = h.shape
    xs = h.reshape(-1, PEER_TOK_BLOCK, d)

    def blk(xb):
        n = xb.shape[0]
        q = (xb @ wq).reshape(n, PEER_HEADS, 2, PEER_DK // 2)
        s = jnp.einsum('nhpd,hpkd->nhpk', q, keys).astype(jnp.float32)
        ts, ti = lax.top_k(s, PEER_TOPK)
        cand = (ts[:, :, 0, :, None] + ts[:, :, 1, None, :]).reshape(n, PEER_HEADS, PEER_TOPK * PEER_TOPK)
        cidx = (ti[:, :, 0, :, None] * PEER_NKEYS + ti[:, :, 1, None, :]).reshape(n, PEER_HEADS, PEER_TOPK * PEER_TOPK)
        fs, fpos = lax.top_k(cand, PEER_TOPK)
        eidx = jnp.take_along_axis(cidx, fpos, axis=-1).reshape(n, PEER_HEADS * PEER_TOPK)
        g = jax.nn.softmax(fs, axis=-1).reshape(n, PEER_HEADS * PEER_TOPK)
        act = jax.nn.gelu(jnp.einsum('nkd,nd->nk', u[eidx], xb).astype(jnp.float32), approximate=False) * g
        return jnp.einsum('nk,nkd->nd', act.astype(xb.dtype), v[eidx])

    return lax.map(blk, xs).reshape(bsz, t_len, d)

def trunk_layer(x, mod, p, ctx):
    sh_a, sc_a, gt_a, sh_f, sc_f, gt_f = jnp.split(mod, 6, axis=-1)
    h = layer_norm(x) * (1.0 + sc_a) + sh_a
    t, new_ctx = token_mix(h, p, ctx)
    x = layer_norm(DEEPNORM_ALPHA * x + gt_a * t, p['ln_a_g'], p['ln_a_b'])
    h = layer_norm(x) * (1.0 + sc_f) + sh_f
    f = peer(h, p['peer_wq'], p['peer_keys'], p['peer_u'], p['peer_v'])
    x = layer_norm(DEEPNORM_ALPHA * x + gt_f * f, p['ln_f_g'], p['ln_f_b'])
    return x, new_ctx

def setup_inputs(seed: int = 0) -> dict:
    key = jax.random.key(seed)
    ks = iter(jax.random.split(key, 48))
    f32 = jnp.float32
    D = D_MODEL
    L = DEPTH

    def nrm(shape, scale):
        return jax.random.normal(next(ks), shape, f32) * scale

    ret_base = 1.0 - 2.0 ** (-5.0 - jnp.arange(RET_HEADS, dtype=f32))
    ret_logit = jnp.log(ret_base / (1.0 - ret_base))
    return {
        'x_prompt': nrm((BATCH, SEQ, D), 1.0),
        'x_sample': nrm((DEC_BATCH, DEC_SEQ, D), 1.0),
        'cache_na_k': nrm((DEC_BATCH, L, NA_HEADS, PAST_LEN, NA_HEAD_DIM), 1.0),
        'cache_na_v': nrm((DEC_BATCH, L, NA_HEADS, PAST_LEN, NA_HEAD_DIM), 1.0),
        'state_ret': nrm((DEC_BATCH, L, 2, RET_HEADS, RET_DK, RET_DV), 0.5),
        'state_rwkv': nrm((DEC_BATCH, L, 2, RWKV_HEADS, RWKV_N, RWKV_N), 0.5),
        'c': nrm((DEC_BATCH, D), 1.0),
        'c_ctx': nrm((D,), 1.0),
        'w_mod': nrm((L, D, 6 * D), D ** -0.5),
        'b_mod': nrm((L, 6 * D), 0.02),
        'w_in': nrm((L, D, P_IN), D ** -0.5),
        'na_rpb': nrm((L, NA_HEADS, 2 * WIN_R - 1, 2 * WIN_C - 1), 0.02),
        'ret_decay_logit': ret_logit[None, None, :] + nrm((L, 2, RET_HEADS), 0.1),
        'ret_gn_w': 1.0 + nrm((L, RET_V_WIDTH), 0.02),
        'ret_gn_b': nrm((L, RET_V_WIDTH), 0.02),
        'rwkv_mu': jax.random.uniform(next(ks), (L, RWKV_SHIFT_WIDTH), f32),
        'rwkv_w0': nrm((L, 2, RWKV_WIDTH), 0.5),
        'rwkv_w_up': nrm((L, 2, RWKV_LORA_W, RWKV_WIDTH), RWKV_LORA_W ** -0.5),
        'rwkv_a0': nrm((L, 2, RWKV_WIDTH), 0.5),
        'rwkv_a_up': nrm((L, 2, RWKV_LORA_A, RWKV_WIDTH), RWKV_LORA_A ** -0.5),
        'rwkv_g_up': nrm((L, RWKV_LORA_G, RWKV_WIDTH), RWKV_LORA_G ** -0.5),
        'rwkv_k_k': 0.85 + nrm((L, RWKV_WIDTH), 0.02),
        'rwkv_k_a': 1.0 + nrm((L, RWKV_WIDTH), 0.02),
        'rwkv_r_k': nrm((L, RWKV_HEADS, RWKV_N), 0.1),
        'rwkv_gn_w': 1.0 + nrm((L, RWKV_WIDTH), 0.02),
        'rwkv_gn_b': nrm((L, RWKV_WIDTH), 0.02),
        'w_br': nrm((L, N_BRANCH, BRANCH_WIDTH, D), BRANCH_WIDTH ** -0.5),
        'w_out': nrm((L, D, D), D ** -0.5 * DEEPNORM_BETA),
        'ln_a_g': 1.0 + nrm((L, D), 0.02),
        'ln_a_b': nrm((L, D), 0.02),
        'ln_f_g': 1.0 + nrm((L, D), 0.02),
        'ln_f_b': nrm((L, D), 0.02),
        'peer_wq': nrm((L, D, PEER_HEADS * PEER_DK), D ** -0.5),
        'peer_keys': nrm((L, PEER_HEADS, 2, PEER_NKEYS, PEER_DK // 2), (PEER_DK // 2) ** -0.5),
        'peer_u': nrm((L, PEER_N_EXPERTS, D), D ** -0.5),
        'peer_v': nrm((L, PEER_N_EXPERTS, D), (PEER_HEADS * PEER_TOPK) ** -0.5 * DEEPNORM_BETA),
    }

def reference(x_prompt, x_sample, cache_na_k, cache_na_v, state_ret, state_rwkv, c, c_ctx,
              w_mod, b_mod, w_in, na_rpb, ret_decay_logit, ret_gn_w, ret_gn_b,
              rwkv_mu, rwkv_w0, rwkv_w_up, rwkv_a0, rwkv_a_up, rwkv_g_up, rwkv_k_k, rwkv_k_a,
              rwkv_r_k, rwkv_gn_w, rwkv_gn_b, w_br, w_out, ln_a_g, ln_a_b, ln_f_g, ln_f_b,
              peer_wq, peer_keys, peer_u, peer_v):
    weights = {
        'w_in': w_in, 'na_rpb': na_rpb, 'ret_decay_logit': ret_decay_logit,
        'ret_gn_w': ret_gn_w, 'ret_gn_b': ret_gn_b, 'rwkv_mu': rwkv_mu, 'rwkv_w0': rwkv_w0,
        'rwkv_w_up': rwkv_w_up, 'rwkv_a0': rwkv_a0, 'rwkv_a_up': rwkv_a_up, 'rwkv_g_up': rwkv_g_up,
        'rwkv_k_k': rwkv_k_k, 'rwkv_k_a': rwkv_k_a, 'rwkv_r_k': rwkv_r_k, 'rwkv_gn_w': rwkv_gn_w,
        'rwkv_gn_b': rwkv_gn_b, 'w_br': w_br, 'w_out': w_out, 'ln_a_g': ln_a_g, 'ln_a_b': ln_a_b,
        'ln_f_g': ln_f_g, 'ln_f_b': ln_f_b, 'peer_wq': peer_wq, 'peer_keys': peer_keys,
        'peer_u': peer_u, 'peer_v': peer_v,
    }
    y_prompt, y_sample = x_prompt, x_sample
    nk_list, nv_list, sr_list, sw_list = [], [], [], []
    for l in range(DEPTH):
        p = {name: arr[l] for name, arr in weights.items()}
        mod_ctx = (jax.nn.silu(c_ctx) @ w_mod[l] + b_mod[l])[None, None, :]
        y_prompt, (nk, nv, sr, sw) = trunk_layer(y_prompt, mod_ctx, p, None)
        nk_list.append(nk)
        nv_list.append(nv)
        sr_list.append(sr)
        sw_list.append(sw)
        mod_lat = (jax.nn.silu(c) @ w_mod[l] + b_mod[l])[:, None, :]
        y_sample, _ = trunk_layer(y_sample, mod_lat, p,
                                  (cache_na_k[:, l], cache_na_v[:, l], state_ret[:, l], state_rwkv[:, l]))
    dt = x_prompt.dtype
    new_na_k = jnp.stack(nk_list, axis=1).astype(dt)
    new_na_v = jnp.stack(nv_list, axis=1).astype(dt)
    new_state_ret = jnp.stack(sr_list, axis=1).astype(dt)
    new_state_rwkv = jnp.stack(sw_list, axis=1).astype(dt)
    return (y_prompt, y_sample, new_na_k, new_na_v, new_state_ret, new_state_rwkv)


_drawn_inputs = setup_inputs


def setup_inputs(seed=0):
    import zlib

    import numpy as np

    out = dict(_drawn_inputs(seed))
    spreads = {}
    factors = {'cache_na_k': 3.118,
     'cache_na_v': 2.857,
     'state_ret': 3.787,
     'state_rwkv': 8.0,
     'na_rpb': 200.0,
     'ret_gn_w': 8.0,
     'ret_gn_b': 8.0,
     'rwkv_k_k': 3.083,
     'rwkv_gn_w': 8.0,
     'rwkv_gn_b': 8.0,
     'peer_wq': 3.236,
     'peer_keys': 3.237,
     'peer_u': 3.649,
     'peer_v': 3.23}
    for name, (base, spread) in spreads.items():
        noise = np.random.default_rng([zlib.crc32(name.encode()), seed]).standard_normal(out[name].shape)
        drawn = base * np.exp(spread * noise) if base else spread * noise
        out[name] = __import__('jax').numpy.asarray(drawn.astype(out[name].dtype))
    for name, factor in factors.items():
        out[name] = (out[name] * factor).astype(out[name].dtype)
    return out
```

```python
from contextlib import ExitStack

import numpy as np

import concourse.bass as bass
from concourse import mybir

ALU = mybir.AluOpType
ACT = mybir.ActivationFunctionType
F32 = mybir.dt.float32
U32 = mybir.dt.uint32
X_AXIS = mybir.AxisListType.X

P = 128
D = 1024
KT = D // P
DEPTH = 2
NT = 3
T = NT * P
NSEQ = 2
TOK = (slice(0, 128), slice(128, 384))
GRID_W = 64
WIN_C = 16
HN = 8
DH = 64
RH = 4
RWH = 8
C = 64
NCH = T // C
LEVELS = 6
TOPK = 16
PH = 8
NKEYS = 128
ALPHA = float((2 * DEPTH) ** 0.25)
EPS = 1e-5
RWKV_EPS = 64e-5
DECAY = -0.606531
NQ = 4
QUART = NKEYS // NQ
SETN = T // QUART

Q_NA, K_NA, V_NA, Q_RT, K_RT, V_RT, G_RT, R_RW, K_RW, V_RW, W_RW, A_RW, GL_RW = (
    0, 4, 8, 12, 14, 16, 20, 24, 28, 32, 36, 37, 38)
NZ = 39
Z_FULL = 9
GATE_COL = NZ * P
RING = 4096

PARAMS = (("rwkv_mu", 15), ("rwkv_w0", 8), ("rwkv_a0", 8), ("rwkv_k_k", 4), ("rwkv_k_a", 4), ("rwkv_r_k", 4),
          ("rwkv_gn_w", 4), ("rwkv_gn_b", 4), ("ret_gn_w", 4), ("ret_gn_b", 4))
NPAR = sum(n for _, n in PARAMS)
PAR = {}
for _name, _n in PARAMS:
    PAR[_name] = sum(n for m, n in PARAMS[:[x for x, _ in PARAMS].index(_name)])


def shape_constants():
    p = np.arange(P)
    parts = {}
    parts["ident"] = np.eye(P)
    parts["iota"] = np.tile(np.arange(P), (P, 1))
    parts["headsum"] = (p[:, None] // 64 == p[None, :] // 64)
    d = p % 64
    half, within = d // 32, d % 32
    first = within < 16
    partner = np.where(first, p + 16, p - 16)
    swap = np.zeros((P, P))
    swap[partner, p] = np.where(first, -1.0, 1.0)
    parts["swap"] = swap
    pos = np.arange(256)
    freqs = (1.0 / (10000.0 ** (np.arange(16, dtype=np.float32) / np.float32(16)))).astype(np.float32)
    axis_pos = np.where(half[:, None] == 0, pos[None] // GRID_W, pos[None] % GRID_W).astype(np.float32)
    ang = (axis_pos * freqs[within % 16][:, None]).astype(np.float32)
    parts["cos"] = np.cos(ang)
    parts["sin"] = np.sin(ang)
    cq, ck = p % GRID_W, np.arange(GRID_W)
    start = np.clip(cq - WIN_C // 2, 0, GRID_W - WIN_C)
    rel = ck[None] - start[:, None]
    parts["window"] = np.where((rel >= 0) & (rel < WIN_C), 0.0, -1e30)
    diff = (p[None, :] - p[:, None]).astype(np.float32)
    parts["dist"] = np.abs(diff)
    parts["tri_f"] = diff >= 0
    parts["tri_b"] = diff <= 0
    parts["far_f"] = P + diff
    parts["far_b"] = P - diff
    parts["age_f"] = np.tile(pos + 1.0, (P, 1))
    parts["age_b"] = np.tile(256.0 - pos, (P, 1))
    parts["left"] = np.stack([127.0 - p, 1.0 * p], 1)
    s = (p % C)[:, None]
    t = np.arange(C)[None]
    parts["before"] = np.concatenate([s < t, s > t], 1)
    parts["upto"] = np.concatenate([s <= t, s >= t], 1)
    lv = []
    for j in range(LEVELS):
        b = 1 << j
        same = (s // (2 * b)) == (t // (2 * b))
        lv += [same & (s // b % 2 == 0) & (t // b % 2 == 1), same & (s // b % 2 == 1) & (t // b % 2 == 0)]
    parts["levels"] = np.concatenate(lv, 1)
    parts["carry"] = np.tile((np.arange(T) % C != 0), (P, 1))
    parts["eye64"] = np.tile(np.eye(C), (2, 1))
    parts["reverse"] = (p[:, None] // 64 == p[None, :] // 64) & (p[:, None] % 64 == 63 - p[None, :] % 64)
    where, cols, n = {}, [], 0
    for k, v in parts.items():
        cols.append(np.asarray(v, np.float32))
        where[k] = slice(n, n + v.shape[1])
        n += v.shape[1]
    return np.ascontiguousarray(np.concatenate(cols, 1)), where


CONSTS, WHERE = shape_constants()


def build(nc, a, out, upto=99):
    y_prompt, y_sample, new_na_k, new_na_v, new_state_ret, new_state_rwkv = out
    ctx = ExitStack()
    with ctx:
        def sb(name, shape, dt=F32):
            return ctx.enter_context(nc.sbuf_tensor(name, shape, dt))

        sems = {}

        def sem(name):
            if name not in sems:
                sems[name] = ctx.enter_context(nc.semaphore(name))
            return sems[name]

        const = sb("const", [P, WHERE["reverse"].start])
        X = sb("X", [P, NT, D])
        hT = sb("hT", [P, KT, T])
        gate = sb("gate", [P, 2, NSEQ, D])
        lnp = sb("lnp", [P, 2, D])
        ring = sb("ring", [P, 2, RING])
        arena = sb("arena", [P, 28672])
        modT = sb("modT", [P, 32, NSEQ])
        silT = sb("silT", [P, 16])
        par = sb("par", [P, NPAR])
        stat = sb("stat", [P, 40])
        decl = sb("decl", [P, 48])
        small = sb("small", [P, 72])
        ps = [ctx.enter_context(nc.psum_tensor(f"ps{i}", [P, 512], F32)) for i in range(8)]

        def K(name):
            return const[:, WHERE[name]]

        def area(at, n, **kw):
            v = arena[:, at:at + n]
            return v.rearrange(kw.pop("r"), **kw) if kw else v

        ident = K("ident")
        TL = T
        ZT = arena[:, 0:NZ * TL].rearrange("p (z t) -> p z t", t=TL)
        oT = arena[:, NZ * TL:(NZ + 12) * TL].rearrange("p (b z t) -> p b z t", b=3, t=TL)
        TMP = (NZ + 12) * TL

        block = ctx.enter_context(nc.Block())

        chain = {"dve": 0, "act": 0, "pool": 0}

        def linker(eng, key):
            def link(ins):
                chain[key] += 1
                ins.then_inc(sem(key + "_chain"), 1)
                eng.wait_ge(sem(key + "_chain"), chain[key])
            return link

        turns = {"dve": 0, "act": 0}

        def rsqrt(dve, link, ins, v, eps, op):
            link(ins)
            turns["dve"] += 1
            nc.vector.tensor_scalar(v, v, eps, None, op).then_inc(sem("square_ready"), 1)
            dve.wait_ge(sem("root_ready"), turns["dve"])
            link(nc.vector.reciprocal(v, v))

        def act_root(act, v):
            turns["act"] += 1
            act.wait_ge(sem("square_ready"), turns["act"])
            nc.scalar.activation(v, v, ACT.Sqrt).then_inc(sem("root_ready"), 1)

        NCHUNK = 12 + 10 + 6 + 3 + 2 + 2

        def chunk_source(l, c):
            if c < 12:
                return a["w_mod"][l].rearrange("(k p) n -> p k n", p=P)[:, :, 512 * c:512 * (c + 1)], KT, 512
            c -= 12
            w_in = a["w_in"][l].rearrange("(k p) n -> p k n", p=P)
            if c < 10:
                w = 512 if c < Z_FULL else NZ * P - 512 * Z_FULL
                return w_in[:, :, 512 * c:512 * c + w], KT, w
            c -= 10
            if c < 6:
                return w_in[:, :, GATE_COL + 512 * c:GATE_COL + 512 * (c + 1)], KT, 512
            c -= 6
            if c < 3:
                return a["w_br"][l, c].rearrange("(k p) n -> p k n", p=P), 4, D
            c -= 3
            w = a["w_out"] if c < 2 else a["peer_wq"]
            c %= 2
            return w[l].rearrange("(k p) n -> p k n", p=P)[:, :, 512 * c:512 * (c + 1)], KT, 512

        def slot(c, k, w):
            return ring[:, c % 2, 0:k * w].rearrange("p (k n) -> p k n", k=k)

        def chunk_no(l, c):
            return l * NCHUNK + c

        def chunk_here(eng, l, c):
            n = chunk_no(l, c)
            eng.wait_ge(sem(f"chunk_in{n % 2}"), 16 * (n // 2 + 1))
            _, k, w = chunk_source(l, c)
            return slot(n, k, w)

        def chunk_released(eng, n):
            l, c = divmod(n, NCHUNK)
            if c < 12:
                eng.wait_ge(sem("mod_mm"), 12 * l + c + 1)
            elif c < 22:
                eng.wait_ge(sem("proj"), NZ * l + min(4 * (c - 12) + 4, NZ))
            elif c < 28:
                eng.wait_ge(sem("gate_mm"), 24 * l + 4 * (c - 22) + 4)
            elif c < 31:
                eng.wait_ge(sem("branch_mm"), 8 * (3 * l + c - 28) + 8)
            elif c < 33:
                eng.wait_ge(sem("out_mm"), NT * (2 * l + c - 31) + NT)
            else:
                eng.wait_ge(sem("query_mm"), 4 * (2 * l + c - 33) + 4)

        G = arena[:, 0:2 * QUART * T].rearrange("p (i n) -> p i n", n=T)
        U_AT = 2 * QUART * T
        ublk = [arena[:, U_AT + b * D:U_AT + (b + 1) * D] for b in range(2)]
        vblk = [arena[:, U_AT + (2 + b) * D:U_AT + (3 + b) * D] for b in range(2)]
        ringf = ring[:, :, :].rearrange("p a n -> p (a n)")
        uT = [ringf[:, b * D:(b + 1) * D].rearrange("p (k e) -> p k e", k=KT) for b in range(2)]
        at = 2 * D
        Wg = [ringf[:, at + b * T:at + (b + 1) * T] for b in range(2)]
        ge = ringf[:, at + 2 * T:at + 3 * T]
        IJG = ringf[:, at + 3 * T:at + 6 * T].rearrange("p (a n) -> p a n", a=3)
        at += 6 * T
        E2 = [ringf[:, at + b * SETN * P:at + (b + 1) * SETN * P].rearrange("p (n j) -> p n j", j=P) for b in range(2)]
        at += 2 * SETN * P
        E1 = [ringf[:, at + b * T:at + (b + 1) * T].rearrange("p (n i) -> p n i", i=QUART) for b in range(2)]
        assert at + 2 * T <= 2 * RING

        def sp_experts(sp, l):
            base = l * NKEYS

            def load_u(i, b):
                if not isinstance(i, int) or base + i >= 2:
                    sp.wait_ge(sem("u_used"), i + (base - 1))
                sp.dma_start(ublk[b], a["peer_u"][l, bass.ds(i * P, P), :]).then_inc(sem(f"u_in{b}"), 16)

            def load_v(i, b):
                if not isinstance(i, int) or base + i >= 2:
                    sp.wait_ge(sem("v_used"), i + (base - 1))
                sp.dma_start(vblk[b], a["peer_v"][l, bass.ds(i * P, P), :]).then_inc(sem(f"v_in{b}"), 16)

            if upto < 7:
                return
            sp.wait_ge(sem("select_done"), l + 1)
            for b in range(2):
                load_u(b, b)
            for b in range(2):
                load_v(b, b)
            for b in range(2):
                load_u(2 + b, b)
            with sp.Fori(0, NKEYS // 2 - 2) as pair:
                for b in range(2):
                    load_u(pair * 2 + (4 + b), b)
                    load_v(pair * 2 + (2 + b), b)
            for b in range(2):
                load_v(NKEYS - 2 + b, b)

        STAGE = TMP
        crow = area(STAGE, 128)
        prow = area(STAGE + 128, 128)
        bmod = area(STAGE + 256, 6144)

        par_srcs = {
            "rwkv_mu": lambda l: a["rwkv_mu"][l].rearrange("(z p) -> z p", p=P),
            "rwkv_w0": lambda l: a["rwkv_w0"][l].rearrange("d (z p) -> (d z) p", p=P),
            "rwkv_a0": lambda l: a["rwkv_a0"][l].rearrange("d (z p) -> (d z) p", p=P),
            "rwkv_r_k": lambda l: a["rwkv_r_k"][l].rearrange("(z h) n -> z (h n)", h=2),
        }
        for nm in ("rwkv_k_k", "rwkv_k_a", "rwkv_gn_w", "rwkv_gn_b", "ret_gn_w", "ret_gn_b"):
            par_srcs[nm] = lambda l, nm=nm: a[nm][l].rearrange("(z p) -> z p", p=P)

        NB = TMP
        bias = area(NB, 4096, r="p (u k) -> p u k", u=16)
        ckin = area(NB + 4096, 512)
        cvin = area(NB + 4608, 512)
        ckT = area(NB + 5120, 512, r="p (z t) -> p z t", z=4)
        vtok = area(NB + 5632, 1536, r="p (t f) -> p t f", t=3)
        ktok0 = area((NZ + 8) * T, 512)
        Sx = [area(NB + 7168 + b * T, T) for b in range(2)]
        PT = [area(NB + 7936 + b * T, T).rearrange("p (j q) -> p j q", j=3) for b in range(2)]
        reverse = area(NB + 8704, P)
        assert NB + 8704 + P <= 28672

        def ln_rows(pool, l, g, b, which):
            n = 2 * l + which
            if which == 0:
                pool.wait_ge(sem("rw_gate"), l + 1)
            else:
                pool.wait_ge(sem("x_done"), n * NT)
            pool.dma_start(lnp[:, 0, :], a[g][l:l + 1, :].to_broadcast([P, D])).then_inc(sem("ln_in"), 16)
            pool.dma_start(lnp[:, 1, :], a[b][l:l + 1, :].to_broadcast([P, D])).then_inc(sem("ln_in"), 16)

        mrow = area(STAGE + 256 + 6144, 1024, r="p (b n) -> p b n", b=2)
        sil_tmp = area(STAGE + 256 + 6144 + 1024, 32)

        def pe_cond(pe):
            pe.wait_ge(sem("const_in"), 16)
            pe.wait_ge(sem("c_in"), 32)
            nc.tensor.transpose(ps[0][:, 0:16], crow[0:16, :], ident[0:16, 0:16]).then_inc(sem("cond_T"), 1)

        def act_cond(act):
            act.wait_ge(sem("cond_T"), 1)
            nc.scalar.activation(sil_tmp[:, 0:16], ps[0][:, 0:16], ACT.Sigmoid).then_inc(sem("cond_sig"), 1)

        def dve_cond(dve):
            dve.wait_ge(sem("cond_sig"), 1)
            nc.vector.tensor_tensor(silT[:, :].rearrange("p (k s) -> p s k", s=2),
                                    ps[0][:, 0:16].rearrange("p (s k) -> p s k", s=2),
                                    sil_tmp[:, 0:16].rearrange("p (s k) -> p s k", s=2),
                                    ALU.mult).then_inc(sem("cond_sil"), 1)

        def pe_mod(pe, l):
            if l == 0:
                pe.wait_ge(sem("cond_sil"), 1)
            pe.wait_ge(sem("param_in"), 16 * (len(PARAMS) + 2) * (l + 1))
            if l:
                pe.wait_ge(sem("x_done"), 2 * l * NT)
            nc.tensor.transpose(ps[4][:, 0:NPAR], prow[0:NPAR, :], ident[0:NPAR, 0:NPAR]).then_inc(sem("par_T"), 1)
            def finish(c):
                pe.wait_ge(sem("mod_row"), 12 * l + c + 1)
                if c >= 2:
                    pe.wait_ge(sem("mod_out"), 12 * l + c - 1)
                part = c // 2
                dst = ps[2 + c % 2]
                if part in (2, 5):
                    for s in range(NSEQ):
                        d = dst if s == 0 else ps[5 + c % 2]
                        ins = nc.tensor.matmul(d[:, :], K("ident")[0:2, s:s + 1].to_broadcast([2, P]),
                                               mrow[0:2, c % 2, :], start=True, stop=True)
                else:
                    for j in range(4):
                        ins = nc.tensor.transpose(dst[:, 2 * j:2 * j + 2], mrow[0:2, c % 2, P * j:P * (j + 1)],
                                                  ident[0:2, 0:2])
                ins.then_inc(sem("mod_spread"), 1)
            for c in range(12):
                w = chunk_here(pe, l, c)
                if c >= 2:
                    pe.wait_ge(sem("mod_row"), 12 * l + c - 1)
                for k in range(KT):
                    ins = nc.tensor.matmul(ps[c % 2][0:2, :], silT[:, 2 * k:2 * k + 2], w[:, k, :],
                                           start=(k == 0), stop=(k == KT - 1))
                ins.then_inc(sem("mod_mm"), 1)
                if c:
                    finish(c - 1)
            finish(11)

        def dve_mod(dve, l):
            dve.wait_ge(sem("param_in"), 16 * (len(PARAMS) + 2) * (l + 1))
            dve.wait_ge(sem("par_T"), l + 1)
            nc.vector.tensor_copy(par[:, :], ps[4][:, 0:NPAR]).then_inc(sem("par_ready"), 1)
            for c in range(12):
                dve.wait_ge(sem("mod_mm"), 12 * l + c + 1)
                if c >= 2:
                    dve.wait_ge(sem("mod_spread"), 12 * l + c - 1)
                nc.vector.tensor_tensor(mrow[0:2, c % 2, :], ps[c % 2][0:2, :], bmod[0:2, 512 * c:512 * (c + 1)],
                                        ALU.add).then_inc(sem("mod_row"), 1)
                if c:
                    dve_mod_out(dve, l, c - 1)
            dve_mod_out(dve, l, 11)

        def dve_mod_out(dve, l, c):
            dve.wait_ge(sem("mod_spread"), 12 * l + c + 1)
            part = c // 2
            if part in (2, 5):
                w = 0 if part == 2 else 1
                cols = slice(512 * (c % 2), 512 * (c % 2) + 512)
                nc.vector.tensor_copy(gate[:, w, 0, cols], ps[2 + c % 2][:, :])
                nc.vector.tensor_copy(gate[:, w, 1, cols], ps[5 + c % 2][:, :]).then_inc(sem("mod_out"), 1)
            else:
                j = (0, 1, None, 2, 3)[part]
                nc.vector.tensor_scalar(modT[:, 8 * j + 4 * (c % 2):8 * j + 4 * (c % 2) + 4, :],
                                        ps[2 + c % 2][:, 0:8].rearrange("p (z s) -> p z s", s=2),
                                        1.0 if j % 2 else 0.0, None, ALU.add).then_inc(sem("mod_out"), 1)

        XN = TMP

        def xnorm(t):
            return area(XN + D * (t % 2), D)

        def dve_layer_norm(dve, link, dst, src):
            for i in range(2):
                nc.vector.bn_stats(stat[:, 6 * i:6 * i + 6], src[:, 512 * i:512 * (i + 1)]).then_inc(sem("dve_chain"), 1)
                chain["dve"] += 1
            dve.wait_ge(sem("dve_chain"), chain["dve"])
            rsqrt(dve, link, nc.vector.bn_aggr(stat[:, 12:14], stat[:, 0:12]), stat[:, 13:14], EPS, ALU.add)
            return nc.vector.tensor_scalar(dst, src, stat[:, 12:13], stat[:, 13:14], ALU.subtract, ALU.mult)

        def act_norm_roots(act):
            for t in range(NT):
                act_root(act, stat[:, 13:14])

        def dve_norm(dve, link, n):
            if n == 0:
                dve.wait_ge(sem("x_in"), 32)
            if n % 2 == 0:
                dve.wait_ge(sem("mod_out"), 12 * (n // 2 + 1))
            for t in range(NT):
                if t == 2:
                    dve.wait_ge(sem("norm_T"), 6 * n + 2)
                dve_layer_norm(dve, link, xnorm(t), X[:, t, :]).then_inc(sem("normed"), 1)
                dve.wait_ge(sem("normed"), NT * n + t + 1)

        def pe_norm(pe, n):
            for t in range(NT):
                pe.wait_ge(sem("normed"), NT * n + t + 1)
                for hh in range(2):
                    q = 2 * t + hh
                    if q >= 4:
                        pe.wait_ge(sem("h_ready"), 6 * n + q - 3)
                    for k in range(4):
                        ins = nc.tensor.transpose(ps[q % 4][:, P * k:P * (k + 1)],
                                                  xnorm(t)[:, P * (4 * hh + k):P * (4 * hh + k + 1)], ident)
                    ins.then_inc(sem("norm_T"), 1)

        def act_norm(act, n):
            act_norm_roots(act)
            act.wait_ge(sem("mod_out"), 12 * (n // 2 + 1))
            if n % 2:
                act.wait_ge(sem("gate_mm"), 24 * (n // 2 + 1))
            elif n:
                act.wait_ge(sem("hidden"), NKEYS * (n // 2))
            for t in range(NT):
                s = min(t, 1)
                for hh in range(2):
                    q = 2 * t + hh
                    act.wait_ge(sem("norm_T"), 6 * n + q + 1)
                    for k in range(4):
                        kk = 4 * hh + k
                        j = 16 * (n % 2)
                        ins = nc.scalar.activation(hT[:, kk, P * t:P * (t + 1)], ps[q % 4][:, P * k:P * (k + 1)],
                                                   ACT.Identity, bias=modT[:, j + kk, s:s + 1],
                                                   scale=modT[:, j + 8 + kk, s:s + 1])
                    ins.then_inc(sem("h_ready"), 1)

        def out_wait(eng, q, act_sem, dve_sem):
            eng.wait_ge(sem(act_sem if q % 2 == 0 else dve_sem), q // 2 + 1)

        def pe_proj(pe, l):
            pe.wait_ge(sem("h_ready"), 6 * (2 * l + 1))
            if l == 0:
                pe.wait_ge(sem("mod_out"), 12)
            for z in range(NZ):
                c, j = divmod(z, 4)
                if j == 0:
                    w = chunk_here(pe, l, 12 + c)
                q = NZ * l + z
                if z in BIAS_AT:
                    pe_bias(pe, l, BIAS_AT.index(z))
                if z >= 4:
                    out_wait(pe, q - 4, "z_act", "z_dve")
                for k in range(KT):
                    ins = nc.tensor.matmul(ps[4 + z % 4][:, 0:T], w[:, k, P * j:P * (j + 1)], hT[:, k, :],
                                           start=(k == 0), stop=(k == KT - 1))
                ins.then_inc(sem("proj"), 1)

        def act_proj(act, l):
            for z in range(NZ):
                q = NZ * l + z
                if q % 2 == 0:
                    act.wait_ge(sem("proj"), q + 1)
                    nc.scalar.activation(ZT[:, z, :], ps[4 + z % 4][:, 0:T], ACT.Copy).then_inc(sem("z_act"), 1)

        def dve_proj(dve, l):
            for z in range(NZ):
                q = NZ * l + z
                if z - 2 in BIAS_AT:
                    dve_bias(dve, l, BIAS_AT.index(z - 2))
                if q % 2:
                    dve.wait_ge(sem("proj"), q + 1)
                    nc.vector.tensor_copy(ZT[:, z, :], ps[4 + z % 4][:, 0:T]).then_inc(sem("z_dve"), 1)

        BIAS_AT = (22, 30)

        def pe_bias(pe, l, half):
            pe.wait_ge(sem("bias_in"), 16 * 33 * (l + 1))
            if half:
                pe.wait_ge(sem("bias_ready"), 2 * l + 1)
            for i in range(4):
                at = NB + 512 * (4 * half + i)
                ins = nc.tensor.matmul(ps[i][:, :], reverse, arena[:, at:at + 512], start=True, stop=True)
            ins.then_inc(sem("bias_turned"), 1)

        def dve_bias(dve, l, half):
            dve.wait_ge(sem("bias_turned"), 2 * l + half + 1)
            for i in range(4):
                at = NB + 512 * (4 * half + i)
                ins = nc.vector.tensor_tensor(arena[:, at:at + 512].rearrange("p (a b) -> p a b", b=GRID_W),
                                              ps[i][:, :].rearrange("p (a b) -> p a b", b=GRID_W),
                                              K("window").rearrange("p (o b) -> p o b", o=1).to_broadcast([P, 8, GRID_W]),
                                              ALU.add)
            ins.then_inc(sem("bias_ready"), 1)

        def z_ready(eng, l):
            n = NZ * (l + 1)
            eng.wait_ge(sem("z_act"), (n + 1) // 2)
            eng.wait_ge(sem("z_dve"), n // 2)

        NU = HN * NT
        astat = stat[:, :]

        def width(n):
            return P if n % NT == 0 else T

        def pool_na(pool, l):
            pool.wait_ge(sem("mod_out"), 12 * (l + 1))
            pool.wait_ge(sem("norm_T"), 6 * (2 * l + 1))
            pool.dma_start(ckin.rearrange("p (h d) -> p h d", h=HN),
                           a["cache_na_k"][0, l].rearrange("h t d -> t h d")).then_inc(sem("na_in"), 16)
            pool.dma_start(cvin.rearrange("p (h d) -> p h d", h=HN),
                           a["cache_na_v"][0, l].rearrange("h t d -> t h d")).then_inc(sem("na_in"), 16)
            pool.dma_start(reverse, a["consts"][:, WHERE["reverse"]]).then_inc(sem("bias_in"), 16)
            rpb = a["na_rpb"]
            for h in range(HN):
                for tq in range(2):
                    for r in range(2):
                        at = ((l * HN + h) * 15 + 7 - (2 * tq + r)) * 31 + 15 - 63
                        pool.dma_start(bias[64 * r:64 * r + 64, 2 * h + tq, :].rearrange("p (a b) -> p a b", a=4),
                                       bass.AP(rpb.tensor, at, [[1, 64], [31, 4], [1, 64]])).then_inc(sem("bias_in"), 16)

        def pool_na_out(pool, l):
            pool.wait_ge(sem("na_tok"), 5 * (l + 1))
            pool.dma_start(new_na_k[0, l].rearrange("h t d -> t h d"),
                           ktok0.rearrange("p (h d) -> p h d", h=HN)).then_inc(sem("stored"), 16)
            pool.dma_start(new_na_v[0, l].rearrange("h t d -> t h d"),
                           vtok[:, 0, :].rearrange("p (h d) -> p h d", h=HN)).then_inc(sem("stored"), 16)

        def pe_na(pe, l):
            z_ready(pe, l)
            pe.wait_ge(sem("bias_ready"), 2 * (l + 1))
            pe.wait_ge(sem("na_in"), 32 * (l + 1))
            for z in range(4):
                ins = nc.tensor.transpose(ps[0][:, P * z:P * (z + 1)], ckin[:, P * z:P * (z + 1)], ident)
            ins.then_inc(sem("na_T"), 1)
            for t in range(NT):
                for z in range(4):
                    ins = nc.tensor.transpose(ps[1 + t][:, P * z:P * (z + 1)], ZT[:, V_NA + z, P * t:P * (t + 1)], ident)
                ins.then_inc(sem("na_T"), 1)
            for z in range(4):
                ins = nc.tensor.transpose(ps[4][:, P * z:P * (z + 1)], ZT[:, K_NA + z, 0:P], ident)
            ins.then_inc(sem("na_T"), 1)
            pe.wait_ge(sem("na_tok"), 5 * (l + 1))

            def scores(n):
                h, t = divmod(n, NT)
                rows = slice(64 * (h % 2), 64 * (h % 2) + 64)
                if n >= 3:
                    pe.wait_ge(sem("na_biased"), NU * l + n - 2)
                bank = ps[2 * (h % 2) + n % 2]
                q = ZT[rows, Q_NA + h // 2, P * t:P * (t + 1)]
                if t == 0:
                    ins = nc.tensor.matmul(bank[:, 0:P], q, ZT[rows, K_NA + h // 2, 0:P], start=True, stop=True)
                else:
                    nc.tensor.matmul(bank[:, 0:256], q, ZT[rows, K_NA + h // 2, P:T], start=True, stop=True)
                    ins = nc.tensor.matmul(bank[:, 256:T], q, ckT[rows, h // 2, :], start=True, stop=True)
                ins.then_inc(sem("na_scores"), 1)

            def turn(n):
                pe.wait_ge(sem("na_prob"), NU * l + n + 1)
                if n >= 2:
                    pe.wait_ge(sem("na_PT"), NU * l + n - 1)
                for j in range(width(n) // P):
                    ins = nc.tensor.transpose(ps[4 + n % 2][:, P * j:P * (j + 1)], Sx[n % 2][:, P * j:P * (j + 1)], ident)
                ins.then_inc(sem("na_turned"), 1)

            def values(n):
                h, t = divmod(n, NT)
                pe.wait_ge(sem("na_PT"), NU * l + n + 1)
                if n % 6 == 0 and n >= 12:
                    pe.wait_ge(sem("na_out"), 4 * l + n // 6 - 1)
                dst = ps[6 + (h // 2) % 2][64 * (h % 2):64 * (h % 2) + 64, P * t:P * (t + 1)]
                cols = slice(64 * h, 64 * h + 64)
                if t == 0:
                    ins = nc.tensor.matmul(dst, vtok[:, 0, cols], PT[n % 2][:, 0, :], start=True, stop=True)
                else:
                    for j, v in enumerate((vtok[:, 1, cols], vtok[:, 2, cols], cvin[:, cols])):
                        ins = nc.tensor.matmul(dst, v, PT[n % 2][:, j, :], start=(j == 0), stop=(j == 2))
                ins.then_inc(sem("na_values"), 1)

            for n in range(NU + 2):
                if n < NU:
                    scores(n)
                if 1 <= n <= NU:
                    turn(n - 1)
                if n >= 2:
                    values(n - 2)

        def act_na(act, l):
            for i, dst in enumerate([ckT.rearrange("p z t -> p (z t)"), vtok[:, 0, :], vtok[:, 1, :], vtok[:, 2, :], ktok0]):
                act.wait_ge(sem("na_T"), 5 * l + i + 1)
                nc.scalar.activation(dst, ps[i][:, :], ACT.Copy).then_inc(sem("na_tok"), 1)
            for n in range(NU + 2):
                if n < NU:
                    act.wait_ge(sem("na_max"), NU * l + n + 1)
                    s = Sx[n % 2][:, 0:width(n)]
                    nc.scalar.activation(s, s, ACT.Exp, bias=small[:, n:n + 1], accum_out=small[:, 24 + n:25 + n])\
                        .then_inc(sem("na_exp"), 1)
                if n >= 2:
                    m = n - 2
                    act.wait_ge(sem("na_turned"), NU * l + m + 1)
                    if m >= 2:
                        act.wait_ge(sem("na_values"), NU * l + m - 1)
                    w = width(m)
                    nc.scalar.activation(PT[m % 2].rearrange("p j q -> p (j q)")[:, 0:w], ps[4 + m % 2][:, 0:w],
                                         ACT.Copy).then_inc(sem("na_PT"), 1)
                if n % 6 == 1 and n >= 7:
                    act_na_out(act, l, (n - 7) // 6)

        def act_na_out(act, l, z):
            act.wait_ge(sem("na_values"), NU * l + 6 * z + 6)
            nc.scalar.activation(oT[:, 0, z, :], ps[6 + z % 2][:, 0:T], ACT.Copy).then_inc(sem("na_out"), 1)

        def dve_na(dve, link, l):
            dve.wait_ge(sem("bias_ready"), 2 * (l + 1))
            for n in range(NU + 1):
                if n < NU:
                    h, t = divmod(n, NT)
                    dve.wait_ge(sem("na_scores"), NU * l + n + 1)
                    if n >= 2:
                        dve.wait_ge(sem("na_turned"), NU * l + n - 1)
                    bank = ps[2 * (h % 2) + n % 2]
                    s = Sx[n % 2]
                    if t:
                        nc.vector.scalar_tensor_tensor(s[:, 0:256], bank[:, 0:256], DH ** -0.5, bias[:, 2 * h + t - 1, :],
                                                       ALU.mult, ALU.add)
                        nc.vector.tensor_scalar(s[:, 256:T], bank[:, 256:T], DH ** -0.5, None, ALU.mult)\
                            .then_inc(sem("na_biased"), 1)
                    else:
                        nc.vector.tensor_scalar(s[:, 0:P], bank[:, 0:P], DH ** -0.5, None, ALU.mult)\
                            .then_inc(sem("na_biased"), 1)
                    dve.wait_ge(sem("na_biased"), NU * l + n + 1)
                    nc.vector.tensor_reduce(small[:, n:n + 1], s[:, 0:width(n)], X_AXIS, ALU.max, negate=True)\
                        .then_inc(sem("na_max"), 1)
                if n:
                    m = n - 1
                    dve.wait_ge(sem("na_exp"), NU * l + m + 1)
                    link(nc.vector.reciprocal(small[:, 48 + m:49 + m], small[:, 24 + m:25 + m]))
                    s = Sx[m % 2][:, 0:width(m)]
                    nc.vector.tensor_scalar(s, s, small[:, 48 + m:49 + m], None, ALU.mult).then_inc(sem("na_prob"), 1)

        RA = TMP
        r_vtok = area(RA, 1536, r="p (t f) -> p t f", t=3)
        r_mask = area(RA + 1536, 2048, r="p (h k i) -> p h k i", h=4, k=4)
        r_qdec = area(RA + 3584, 1024, r="p (d z i) -> p d z i", d=2, z=2)
        r_s0 = area(RA + 4608, 512, r="p (z d v) -> p z d v", z=2, d=2)
        r_ktok = area(RA + 5120, 256)
        r_kleft = area(RA + 5376, 512, r="p (d h k) -> p d h k", d=2, h=4)
        r_on = area(RA + 5888, 1536, r="p (t f) -> p t f", t=3)
        r_sig = area(RA + 7424, 1536)
        r_att = arena[:, 0:2560]
        r_tmp = arena[:, 2560:2560 + 1536]
        r_sout = arena[:, 0:1024]
        nlg, ncol = decl[:, 0:8], decl[:, 8:12]

        def pool_ret(pool, l):
            pool.wait_ge(sem("na_out"), 4 * (l + 1))
            pool.wait_ge(sem("stored"), 16 * (7 * l + 2))
            st = a["state_ret"][0, l]
            for d in range(2):
                for z in range(2):
                    pool.dma_start(r_s0[:, z, d, :], st[d, 2 * z:2 * z + 2].rearrange("h k v -> (h k) v"))\
                        .then_inc(sem("ret_in"), 16)
            lg = a["ret_decay_logit"]
            pool.dma_start(nlg, bass.AP(lg.tensor, l * 8, [[0, P], [1, 8]])).then_inc(sem("ret_in"), 16)
            for q in range(2):
                for d in range(2):
                    for z in range(2):
                        pool.dma_start(ncol[64 * q:64 * q + 64, 2 * d + z:2 * d + z + 1],
                                       bass.AP(lg.tensor, l * 8 + 4 * d + 2 * z + q, [[0, 64], [1, 1]]))\
                            .then_inc(sem("ret_in"), 16)
        RET_IN = 16 * (4 + 1 + 8)

        def pool_ret_out(pool, l):
            pool.wait_ge(sem("ret_states"), 2 * (l + 1))
            pool.dma_start(new_state_ret[0, l].rearrange("d h k v -> k (d h) v"),
                           r_sout[0:64, :].rearrange("p (g v) -> p g v", g=8)).then_inc(sem("stored"), 16)

        def pe_ret(pe, l):
            pe.wait_ge(sem("na_out"), 4 * (l + 1))
            for i in range(4):
                ins = nc.tensor.matmul(ps[i][:, 0:256], K("swap"), ZT[:, Q_RT + i, P:T], start=True, stop=True)
            ins.then_inc(sem("ret_swap"), 1)
            for t in range(NT):
                for z in range(4):
                    ins = nc.tensor.transpose(ps[4 + t][:, P * z:P * (z + 1)], ZT[:, V_RT + z, P * t:P * (t + 1)], ident)
                ins.then_inc(sem("ret_T"), 1)
            pe.wait_ge(sem("ret_rope"), l + 1)
            for z in range(2):
                ins = nc.tensor.transpose(ps[7][:, P * z:P * (z + 1)], ZT[:, K_RT + z, 0:P], ident)
            ins.then_inc(sem("ret_T"), 1)
            pe.wait_ge(sem("ret_tok"), 4 * l + 2)
            for h in range(RH):
                rows = slice(64 * (h % 2), 64 * (h % 2) + 64)
                q, k = ZT[rows, Q_RT + h // 2, :], ZT[rows, K_RT + h // 2, :]
                for j in range(2):
                    nc.tensor.matmul(ps[h][:, 256 * j:256 * (j + 1)], k[:, P * (1 + j):P * (2 + j)], q[:, P:T],
                                     start=True, stop=True)
                ins = nc.tensor.matmul(ps[4 + h % 2][:, P * (h // 2):P * (h // 2) + P], k[:, 0:P], q[:, 0:P],
                                       start=True, stop=True)
            ins.then_inc(sem("ret_scores"), 1)
            pe.wait_ge(sem("ret_kleft"), l + 1)
            pe.wait_ge(sem("ret_tok"), 4 * l + 4)
            pe.wait_ge(sem("ret_att"), l + 1)
            pe.wait_ge(sem("ret_qdec"), l + 1)
            for t in range(NT):
                bank = ps[(6, 7, 0)[t]]
                for h in range(RH):
                    rows = slice(64 * (h % 2), 64 * (h % 2) + 64)
                    dst = bank[:, P * h:P * (h + 1)]
                    v = slice(P * h, P * (h + 1))
                    if t == 0:
                        ins = nc.tensor.matmul(dst, r_att[:, 2048 + P * h:2048 + P * (h + 1)], r_vtok[:, 0, v],
                                               start=True, stop=True)
                        continue
                    i = P * (t - 1)
                    for j in range(2):
                        at = 512 * h + 256 * j + i
                        nc.tensor.matmul(dst, r_att[:, at:at + P], r_vtok[:, 1 + j, v], start=(j == 0), stop=False)
                    if h:
                        pe.wait_ge(sem("ret_head"), 6 * l + 3 * (t - 1) + h)
                    for d in range(2):
                        ins = nc.tensor.matmul(dst, r_qdec[rows, d, h // 2, i:i + P], r_s0[rows, h // 2, d, :],
                                               start=False, stop=(d == 1))
                    if h < RH - 1:
                        ins.then_inc(sem("ret_head"), 1)
                ins.then_inc(sem("ret_o"), 1)
            for d in range(2):
                for h in range(RH):
                    ins = nc.tensor.matmul(ps[4 + d][0:64, P * h:P * (h + 1)], r_kleft[:, d, h, :],
                                           r_vtok[:, 0, P * h:P * (h + 1)], start=True, stop=True)
                ins.then_inc(sem("ret_S"), 1)
            for t in range(NT):
                pe.wait_ge(sem("ret_normed"), NT * l + t + 1)
                for h in range(RH):
                    ins = nc.tensor.transpose(ps[1 + t][:, P * h:P * (h + 1)], r_on[:, t, P * h:P * (h + 1)], ident)
                ins.then_inc(sem("ret_oT"), 1)

        def act_ret(act, link, l):
            act.wait_ge(sem("ret_in"), RET_IN * (l + 1))
            link(nc.scalar.activation(decl[:, 12:24], decl[:, 0:12], ACT.Exp, scale=-1.0))
            nc.scalar.activation(decl[:, 24:36], decl[:, 12:24], ACT.Ln, bias=1.0).then_inc(sem("ret_ln"), 1)
            for t in range(2):
                act.wait_ge(sem("ret_T"), 4 * l + t + 1)
                nc.scalar.activation(r_vtok[:, t, :], ps[4 + t][:, :], ACT.Copy).then_inc(sem("ret_tok"), 1)
            act.wait_ge(sem("ret_T"), 4 * l + 4)
            nc.scalar.activation(r_vtok[:, 2, :], ps[6][:, :], ACT.Copy).then_inc(sem("ret_tok"), 1)
            nc.scalar.activation(r_ktok, ps[7][:, 0:256], ACT.Copy).then_inc(sem("ret_tok"), 1)
            act.wait_ge(sem("ret_lg"), l + 1)
            for h in range(RH):
                f, b = decl[:, 36 + h:37 + h], decl[:, 40 + h:41 + h]
                nc.scalar.activation(r_mask[:, h, 0, :], K("dist"), ACT.Exp, scale=f)
                nc.scalar.activation(r_mask[:, h, 3, :], K("dist"), ACT.Exp, scale=b)
                nc.scalar.activation(r_mask[:, h, 1, :], K("far_f"), ACT.Exp, scale=f)
                ins = nc.scalar.activation(r_mask[:, h, 2, :], K("far_b"), ACT.Exp, scale=b)
            ins.then_inc(sem("ret_exp"), 1)
            for d in range(2):
                for z in range(2):
                    n = 44 + 2 * d + z
                    ins = nc.scalar.activation(r_qdec[:, d, z, :], K("age_b" if d else "age_f"), ACT.Exp,
                                               scale=decl[:, n:n + 1])
            ins.then_inc(sem("ret_exp"), 1)
            for d in range(2):
                for h in range(RH):
                    n = 4 * d + h
                    ins = nc.scalar.activation(small[:, n:n + 1], K("left")[:, d:d + 1], ACT.Exp,
                                               scale=decl[:, 36 + n:37 + n])
            ins.then_inc(sem("ret_exp"), 1)
            nc.scalar.activation(r_sig, ZT[:, G_RT:G_RT + 4, :].rearrange("p z t -> p (z t)"), ACT.Sigmoid)\
                .then_inc(sem("ret_sig"), 1)
            for t in range(NT):
                act_root(act, stat[:, 32:40].rearrange("p (h s) -> p h s", s=2)[:, :, 1])
            for d in range(2):
                act.wait_ge(sem("ret_S"), 2 * l + d + 1)
                if d == 0:
                    act.wait_ge(sem("ret_o"), NT * (l + 1))
                nc.scalar.activation(r_sout[0:64, 512 * d:512 * (d + 1)], ps[4 + d][0:64, :], ACT.Copy)\
                    .then_inc(sem("ret_states"), 1)
            for t in range(NT):
                act.wait_ge(sem("ret_oT"), NT * l + t + 1)
                for h in range(RH):
                    w, b = PAR["ret_gn_w"] + h, PAR["ret_gn_b"] + h
                    ins = nc.scalar.activation(oT[:, 1, h, P * t:P * (t + 1)], ps[1 + t][:, P * h:P * (h + 1)],
                                               ACT.Identity, bias=par[:, b:b + 1], scale=par[:, w:w + 1])
                ins.then_inc(sem("ret_affine"), 1)

        def dve_ret(dve, link, l):
            dve.wait_ge(sem("na_out"), 4 * (l + 1))
            qk = ZT[:, Q_RT:Q_RT + 4, P:T]
            rt = r_tmp[:, 0:1024].rearrange("p (z t) -> p z t", z=4)
            def wide(name):
                return K(name).rearrange("p (o t) -> p o t", o=1).to_broadcast([P, 4, 256])
            link(nc.vector.tensor_tensor(rt, qk, wide("cos"), ALU.mult))
            dve.wait_ge(sem("ret_swap"), l + 1)
            for i in range(4):
                ins = nc.vector.tensor_tensor(qk[:, i, :], ps[i][:, 0:256], K("sin"), ALU.mult)
            link(ins)
            link(nc.vector.tensor_tensor(qk, qk, rt, ALU.add))
            kk = ZT[:, K_RT:K_RT + 2, :]
            nc.vector.tensor_scalar(kk, kk, DH ** -0.5, None, ALU.mult).then_inc(sem("ret_rope"), 1)
            dve.wait_ge(sem("ret_ln"), l + 1)
            nc.vector.tensor_scalar(decl[:, 36:48], decl[:, 24:36], -1.0, None, ALU.mult).then_inc(sem("ret_lg"), 1)
            dve.wait_ge(sem("ret_exp"), 3 * l + 1)
            def tri(name):
                return K(name).rearrange("p (o i) -> p o i", o=1).to_broadcast([P, 4, P])
            nc.vector.tensor_tensor(r_mask[:, :, 0, :], r_mask[:, :, 0, :], tri("tri_f"), ALU.mult)
            link(nc.vector.tensor_tensor(r_mask[:, :, 3, :], r_mask[:, :, 3, :], tri("tri_b"), ALU.mult))
            link(nc.vector.tensor_tensor(r_mask[:, :, 0, :], r_mask[:, :, 0, :], r_mask[:, :, 3, :], ALU.add))
            link(nc.vector.tensor_copy(r_mask[:, :, 3, :], r_mask[:, :, 0, :]))
            dve.wait_ge(sem("ret_exp"), 3 * l + 2)
            q = ZT[:, Q_RT:Q_RT + 2, P:T]
            nc.vector.tensor_tensor(r_qdec[:, 0, :, :], r_qdec[:, 0, :, :], q, ALU.mult)
            nc.vector.tensor_tensor(r_qdec[:, 1, :, :], r_qdec[:, 1, :, :], q, ALU.mult).then_inc(sem("ret_qdec"), 1)
            dve.wait_ge(sem("ret_exp"), 3 * l + 3)
            dve.wait_ge(sem("ret_tok"), 4 * (l + 1))
            for d in range(2):
                for h in range(RH):
                    n = 4 * d + h
                    ins = nc.vector.tensor_scalar(r_kleft[:, d, h, :], r_ktok[:, 64 * h:64 * h + 64], small[:, n:n + 1],
                                                  None, ALU.mult)
            ins.then_inc(sem("ret_kleft"), 1)
            dve.wait_ge(sem("ret_scores"), l + 1)
            for h in range(RH):
                nc.vector.tensor_tensor(r_att[:, 512 * h:512 * (h + 1)], ps[h][:, :],
                                        r_mask[:, h, :, :].rearrange("p k i -> p (k i)"), ALU.mult)
                ins = nc.vector.tensor_tensor(r_att[:, 2048 + P * h:2048 + P * (h + 1)],
                                              ps[4 + h % 2][:, P * (h // 2):P * (h // 2) + P], r_mask[:, h, 0, :], ALU.mult)
            ins.then_inc(sem("ret_att"), 1)
            dve.wait_ge(sem("ret_sig"), l + 1)
            g = ZT[:, G_RT:G_RT + 4, :].rearrange("p z t -> p (z t)")
            link(nc.vector.tensor_tensor(r_sig, r_sig, g, ALU.mult))
            for t in range(NT):
                dve.wait_ge(sem("ret_o"), NT * l + t + 1)
                bank = ps[(6, 7, 0)[t]]
                for h in range(RH):
                    ins = nc.vector.bn_stats(stat[:, 6 * h:6 * h + 6], bank[:, P * h:P * (h + 1)])
                link(ins)
                for h in range(RH):
                    ins = nc.vector.bn_aggr(stat[:, 32 + 2 * h:34 + 2 * h], stat[:, 6 * h:6 * h + 6])
                rsqrt(dve, link, ins, stat[:, 32:40].rearrange("p (h s) -> p h s", s=2)[:, :, 1], EPS, ALU.add)
                for h in range(RH):
                    ins = nc.vector.tensor_scalar(r_on[:, t, P * h:P * (h + 1)], bank[:, P * h:P * (h + 1)],
                                                  stat[:, 32 + 2 * h:33 + 2 * h], stat[:, 33 + 2 * h:34 + 2 * h],
                                                  ALU.subtract, ALU.mult)
                ins.then_inc(sem("ret_normed"), 1)
            dve.wait_ge(sem("ret_affine"), NT * (l + 1))
            o = oT[:, 1, :, :].rearrange("p z t -> p (z t)")
            nc.vector.tensor_tensor(o, o, r_sig, ALU.mult).then_inc(sem("ret_done"), 1)

        ZW = T * 4

        def tiles4(at):
            return arena[:, at:at + ZW].rearrange("p (z t) -> p z t", t=T)

        w_QR = [arena[:, at:at + 2 * ZW].rearrange("p (x z t) -> p x z t", x=2, t=T) for at in (0, TMP)]
        w_K = [tiles4(2 * ZW), tiles4(TMP + 2 * ZW)]
        w_B = [tiles4(3 * ZW), tiles4(TMP + 3 * ZW)]
        w_kk = tiles4(4 * ZW)
        w_LW = tiles4(5 * ZW)
        w_L = tiles4(TMP + 4 * ZW)
        w_E = oT[:, 2, :, :]
        shift = arena[:, TMP:TMP + 15 * T].rearrange("p (z t) -> p z t", t=T)
        r_, k_, v_ = ZT[:, R_RW:R_RW + 4, :], ZT[:, K_RW:K_RW + 4, :], ZT[:, V_RW:V_RW + 4, :]
        w_up, a_up, g_up = lnp[:, 0, 0:512], lnp[:, 0, 512:1024], lnp[:, 1, 0:512]
        w_ends = small[:, 0:48].rearrange("p (d z c) -> p d z c", d=2, z=4)
        w_tot = small[:, 48:72]

        def unit(i):
            at = 4 * ZW + 512 * i if i < 12 else (TMP + 5 * ZW + 512 * (i - 12) if i < 14 else W_RW * T)
            return arena[:, at:at + 512]
        u_A, u_M, u_G, u_RK, u_RB, u_X, u_Y, u_T, u_K, u_B, u_V, u_I, u_S, u_in, u_out = (unit(i) for i in range(15))
        w_O = w_L
        w_Oc = arena[:, TMP + 4 * ZW:TMP + 5 * ZW].rearrange("p (c x) -> p c x", c=NCH)
        w_Og = arena[:, TMP + 4 * ZW:TMP + 5 * ZW].rearrange("p (g v) -> p g v", v=64)
        w_sq = arena[:, 4 * ZW + 1024:4 * ZW + 2560].rearrange("p (g v) -> p g v", v=64)
        w_N = tiles4(4 * ZW + 2560)

        def flat(v):
            return v.rearrange("p z t -> p (z t)")

        def pcol(name, z):
            return par[:, PAR[name] + z:PAR[name] + z + 1]

        def both(name, d=None):
            m = K(name)[:, 64 * d:64 * d + 64].rearrange("p (o t) -> p o t", o=1)
            return m.to_broadcast([P, 4, 64])

        STEPS = [(0, 1), (1, 0), (2, 5), (3, 4), (4, 3), (5, 2)]
        NS = len(STEPS)

        def pool_rwkv(pool, l):
            if l:
                pool.wait_ge(sem("x_done"), 2 * l * NT)
            pool.dma_start(w_up, a["rwkv_w_up"][l].rearrange("d r n -> (d r) n")).then_inc(sem("rw_in"), 16)
            pool.dma_start(a_up, a["rwkv_a_up"][l].rearrange("d r n -> (d r) n")).then_inc(sem("rw_in"), 16)
            pool.dma_start(g_up, a["rwkv_g_up"][l]).then_inc(sem("rw_in"), 16)
            pool.wait_ge(sem("rw_shift"), l + 1)
            for d in range(2):
                st = a["state_rwkv"][0, l, d].rearrange("(z q) v k -> q v z k", q=2)
                for q in range(2):
                    pool.dma_start(u_in[64 * q:64 * q + 64, 256 * d:256 * d + 256].rearrange("p (z k) -> p z k", z=4),
                                   st[q]).then_inc(sem("rw_state_in"), 16)

        def pool_rwkv_out(pool, l):
            pool.wait_ge(sem("rw_out"), l + 1)
            for d in range(2):
                st = new_state_rwkv[0, l, d].rearrange("(z q) v k -> q v z k", q=2)
                for q in range(2):
                    pool.dma_start(st[q], u_out[64 * q:64 * q + 64, 256 * d:256 * d + 256]
                                   .rearrange("p (z k) -> p z k", z=4)).then_inc(sem("stored"), 16)

        def heads(fn):
            for d in range(2):
                for z in range(4):
                    for q in range(2):
                        rows = slice(64 * q, 64 * q + 64)
                        ins = fn(d, z, rows, slice(256 * d + 64 * z, 256 * d + 64 * z + 64))
            return ins

        def pe_rwkv(pe, l):
            pe.wait_ge(sem("rw_sq"), 2 * l + 1)
            for z in range(4):
                ins = nc.tensor.matmul(ps[z][:, 0:T], K("headsum"), w_E[:, z, :], start=True, stop=True)
            ins.then_inc(sem("rw_sums"), 1)
            pe.wait_ge(sem("rw_in"), 48 * (l + 1))
            pe.wait_ge(sem("rw_tanh"), l + 1)
            pe.wait_ge(sem("rw_kk"), l + 1)
            for d in range(2):
                rows = slice(64 * d, 64 * d + 64)
                if d:
                    pe.wait_ge(sem("rw_sig"), 2 * l + 1)
                for z in range(4):
                    nc.tensor.matmul(ps[z][:, 0:T], w_up[rows, P * z:P * (z + 1)], ZT[rows, W_RW, :], start=True, stop=True)
                for z in range(4):
                    ins = nc.tensor.matmul(ps[4 + z][:, 0:T], a_up[rows, P * z:P * (z + 1)], ZT[rows, A_RW, :],
                                           start=True, stop=True)
                ins.then_inc(sem("rw_lora"), 1)
            pe.wait_ge(sem("rw_sq"), 2 * l + 2)
            pe.wait_ge(sem("rw_sig"), 2 * l + 2)
            for z in range(4):
                ins = nc.tensor.matmul(ps[4 + z][:, 0:T], K("headsum"), w_L[:, z, :], start=True, stop=True)
            ins.then_inc(sem("rw_sums"), 1)
            pe.wait_ge(sem("rw_ready"), l + 1)
            for s, chunks in enumerate(STEPS):
                pe_rwkv_step(pe, l, NS * l + s, chunks)
                if s == 1:
                    pe.wait_ge(sem("rw_state"), (NS + 1) * l + s + 1)
                    heads(lambda d, z, rows, g: nc.tensor.matmul(ps[7][rows, g], u_S[rows, g], K("eye64")[rows, :],
                                                                 start=True, stop=True)).then_inc(sem("rw_turn"), 1)
                    pe.wait_ge(sem("rw_state_in"), 64 * (l + 1))
                    heads(lambda d, z, rows, g: nc.tensor.matmul(ps[6][rows, g], u_in[rows, g], K("eye64")[rows, :],
                                                                 start=True, stop=True)).then_inc(sem("rw_turn"), 1)
            pe.wait_ge(sem("rw_O"), l + 1)
            for z in range(4):
                for c in range(NCH):
                    for q in range(2):
                        rows = slice(64 * q, 64 * q + 64)
                        ins = nc.tensor.matmul(ps[z][rows, 64 * c:64 * c + 64], w_Oc[rows, c, 64 * z:64 * z + 64],
                                               K("eye64")[rows, :], start=True, stop=True)
            ins.then_inc(sem("rw_OT"), 1)
            for z in range(4):
                ins = nc.tensor.matmul(ps[4 + z][:, 0:T], g_up[:, P * z:P * (z + 1)], ZT[:, GL_RW, :], start=True, stop=True)
            ins.then_inc(sem("rw_gate"), 1)

        def pe_rwkv_step(pe, l, m, chunks):
            n = (NS + 1) * l + m % NS + (1 if m % NS >= 2 else 0)
            tok = [slice(C * c, C * c + C) for c in chunks]
            if m % NS:
                pe.wait_ge(sem("rw_state"), n)
            if m % NS == 2:
                pe.wait_ge(sem("rw_out"), l + 1)
            for bank, src in ((0, w_B), (2, w_K)):
                for d in range(2):
                    for z in range(4):
                        for q in range(2):
                            rows = slice(64 * q, 64 * q + 64)
                            ins = nc.tensor.matmul(ps[bank + d][rows, P * z:P * (z + 1)].rearrange("p (x t) -> p x t", x=2),
                                                   src[d][rows, z, tok[d]], w_QR[d][rows, :, z, tok[d]],
                                                   start=True, stop=True)
                ins.then_inc(sem("rw_pairs"), 1)
            for bank, src in ((4, w_K), (5, w_B), (6, (v_, v_))):
                ins = heads(lambda d, z, rows, g: nc.tensor.matmul(ps[bank][rows, g], src[d][rows, z, tok[d]],
                                                                   K("eye64")[rows, :], start=True, stop=True))
            ins.then_inc(sem("rw_pairs"), 1)
            pe.wait_ge(sem("rw_masked"), 2 * m + 2)
            pe.wait_ge(sem("rw_tok"), 2 * m + 2)

            def rhs(d, z, rows, g):
                nc.tensor.matmul(ps[2][rows, g], w_QR[d][rows, 0, z, tok[d]], u_S[rows, g], start=True, stop=False)
                return nc.tensor.matmul(ps[2][rows, g], u_G[rows, g], u_V[rows, g], start=False, stop=True)
            heads(rhs).then_inc(sem("rw_rhs"), 1)
            for j in range(LEVELS):
                pe.wait_ge(sem("rw_M"), LEVELS * m + j + 1)
                if j:
                    pe.wait_ge(sem("rw_XY"), LEVELS * m + j)
                heads(lambda d, z, rows, g: nc.tensor.matmul(ps[7][rows, g], u_M[rows, g], (u_X if j else u_I)[rows, g],
                                                             start=True, stop=True)).then_inc(sem("rw_T"), 1)
                if j:
                    pe.wait_ge(sem("rw_Tc"), (LEVELS - 1) * m + j)
                    ins = heads(lambda d, z, rows, g: nc.tensor.matmul(ps[0][rows, g], u_T[rows, g], u_Y[rows, g],
                                                                       start=True, stop=True))
                    if j < LEVELS - 1:
                        ins = heads(lambda d, z, rows, g: nc.tensor.matmul(ps[1][rows, g], u_Y[rows, g], u_T[rows, g],
                                                                           start=True, stop=True))
                    ins.then_inc(sem("rw_XYp"), 1)
            pe.wait_ge(sem("rw_XY"), LEVELS * (m + 1))
            pe.wait_ge(sem("rw_rhsc"), m + 1)
            heads(lambda d, z, rows, g: nc.tensor.matmul(ps[3][rows, g], u_Y[rows, g], u_T[rows, g],
                                                         start=True, stop=True)).then_inc(sem("rw_alpha"), 1)
            pe.wait_ge(sem("rw_alphac"), m + 1)

            def outp(d, z, rows, g):
                nc.tensor.matmul(ps[4][rows, g], w_QR[d][rows, 1, z, tok[d]], u_S[rows, g], start=True, stop=False)
                nc.tensor.matmul(ps[4][rows, g], u_RK[rows, g], u_V[rows, g], start=False, stop=False)
                return nc.tensor.matmul(ps[4][rows, g], u_RB[rows, g], u_M[rows, g], start=False, stop=True)
            heads(outp).then_inc(sem("rw_o"), 1)

            def state(d, z, rows, g):
                nc.tensor.matmul(ps[5][rows, g], u_K[rows, g], u_V[rows, g], start=True, stop=False)
                return nc.tensor.matmul(ps[5][rows, g], u_B[rows, g], u_M[rows, g], start=False, stop=True)
            heads(state).then_inc(sem("rw_S"), 1)

        def act_rwkv(act, link, l):
            act.wait_ge(sem("rw_shift"), l + 1)
            nc.scalar.activation(ZT[:, W_RW, :], ZT[:, W_RW, :], ACT.Tanh).then_inc(sem("rw_tanh"), 1)
            act_root(act, flat(w_L))
            for d in range(2):
                act.wait_ge(sem("rw_lora"), 2 * l + d + 1)
                if d:
                    act.wait_ge(sem("rw_prep"), 2 * l + 1)
                for z in range(4):
                    nc.scalar.activation(w_LW[:, z, :], ps[z][:, 0:T], ACT.Sigmoid, bias=pcol("rwkv_w0", 4 * d + z))
                for z in range(4):
                    ins = nc.scalar.activation(w_E[:, z, :], ps[4 + z][:, 0:T], ACT.Sigmoid, bias=pcol("rwkv_a0", 4 * d + z))
                ins.then_inc(sem("rw_sig"), 1)
                act.wait_ge(sem("rw_L"), 2 * l + d + 1)
                incl, excl = (w_L, w_LW) if d == 0 else (w_LW, w_L)
                ends = incl.rearrange("p z (c t) -> p z c t", t=C)[:, :, :, C - 1 if d == 0 else 0]
                nc.scalar.activation(w_ends[:, d, :, :], ends, ACT.Exp)
                nc.scalar.activation(flat(w_QR[d][:, 1, :, :]), flat(incl), ACT.Exp)
                link(nc.scalar.activation(flat(excl), flat(excl), ACT.Exp))
                nc.scalar.activation(flat(incl), flat(incl), ACT.Exp, scale=-1.0).then_inc(sem("rw_exp"), 1)
            nc.scalar.activation(ZT[:, GL_RW, :], ZT[:, GL_RW, :], ACT.Sigmoid).then_inc(sem("rw_gl"), 1)
            for s in range(NS):
                m = NS * l + s
                act.wait_ge(sem("rw_pairs"), 3 * m + 1)
                for d in range(2):
                    ins = nc.scalar.activation(u_A[:, 256 * d:256 * (d + 1)].rearrange("p (z t) -> p z t", z=4),
                                               ps[d][:, :].rearrange("p (z x t) -> p z x t", z=4, x=2)[:, :, 0, :], ACT.Copy)
                ins.then_inc(sem("rw_tok"), 1)
                act.wait_ge(sem("rw_pairs"), 3 * m + 3)
                nc.scalar.activation(u_K, ps[4][:, :], ACT.Copy)
                nc.scalar.activation(u_B, ps[5][:, :], ACT.Copy)
                nc.scalar.activation(u_V, ps[6][:, :], ACT.Copy).then_inc(sem("rw_tok"), 1)
                for j in range(1, LEVELS):
                    act.wait_ge(sem("rw_T"), LEVELS * m + j + 1)
                    nc.scalar.activation(u_T, ps[7][:, :], ACT.Copy).then_inc(sem("rw_Tc"), 1)
                act.wait_ge(sem("rw_rhs"), m + 1)
                act.wait_ge(sem("rw_XYp"), (LEVELS - 1) * (m + 1))
                nc.scalar.activation(u_T, ps[2][:, :], ACT.Copy).then_inc(sem("rw_rhsc"), 1)
                act.wait_ge(sem("rw_alpha"), m + 1)
                nc.scalar.activation(u_M, ps[3][:, :], ACT.Copy, scale=-1.0).then_inc(sem("rw_alphac"), 1)
                if s == 1:
                    act.wait_ge(sem("rw_turn"), 2 * l + 1)
                    nc.scalar.activation(u_out, ps[7][:, :], ACT.Copy).then_inc(sem("rw_out"), 1)
            act_root(act, w_tot)
            act.wait_ge(sem("rw_OT"), l + 1)
            for z in range(4):
                ins = nc.scalar.activation(w_N[:, z, :], ps[z][:, 0:T], ACT.Identity, bias=pcol("rwkv_gn_b", z),
                                           scale=pcol("rwkv_gn_w", z))
            ins.then_inc(sem("rw_affine"), 1)

        def dve_rwkv(dve, link, l):
            zz = ZT[:, R_RW:NZ, :]
            dve.wait_ge(sem("stored"), 16 * (7 * l + 3))
            link(nc.vector.tensor_tensor(shift[:, :, 1:T - 1], zz[:, :, 0:T - 2], zz[:, :, 2:T], ALU.add))
            for at, of in ((0, 1), (P - 1, P - 2), (P, P + 1), (T - 1, T - 2)):
                ins = nc.vector.tensor_copy(shift[:, :, at:at + 1], zz[:, :, of:of + 1])
            link(ins)
            link(nc.vector.scalar_tensor_tensor(flat(shift), flat(shift), 0.5, flat(zz), ALU.mult, ALU.subtract))
            for z in range(15):
                ins = nc.vector.scalar_tensor_tensor(zz[:, z, :], shift[:, z, :], pcol("rwkv_mu", z), zz[:, z, :],
                                                     ALU.mult, ALU.add)
            ins.then_inc(sem("rw_shift"), 1)
            dve.wait_ge(sem("rw_shift"), l + 1)
            for z in range(4):
                ins = nc.vector.tensor_scalar(w_kk[:, z, :], k_[:, z, :], pcol("rwkv_k_k", z), None, ALU.mult)
            link(ins)
            nc.vector.tensor_tensor(w_E, w_kk, w_kk, ALU.mult).then_inc(sem("rw_sq"), 1)
            dve.wait_ge(sem("rw_sums"), 2 * l + 1)
            for z in range(4):
                ins = nc.vector.tensor_copy(w_L[:, z, :], ps[z][:, 0:T])
            rsqrt(dve, link, ins, flat(w_L), 1e-24, ALU.max)
            nc.vector.tensor_tensor(w_kk, w_kk, w_L, ALU.mult).then_inc(sem("rw_kk"), 1)
            dve.wait_ge(sem("rw_kk"), l + 1)
            for d in range(2):
                incl, excl = (w_L, w_LW) if d == 0 else (w_LW, w_L)
                dve.wait_ge(sem("rw_sig"), 2 * l + d + 1)
                link(nc.vector.tensor_scalar(flat(w_LW), flat(w_LW), DECAY, None, ALU.mult))
                for z in range(4):
                    ins = nc.vector.tensor_tensor_scan(w_L[:, z, :], K("carry"), w_LW[:, z, :], 0.0, ALU.mult, ALU.add)
                link(ins)
                if d == 0:
                    nc.vector.tensor_tensor(w_LW, w_L, w_LW, ALU.subtract).then_inc(sem("rw_L"), 1)
                else:
                    Lg = flat(w_L).rearrange("p (g t) -> p g t", t=C)
                    link(nc.vector.tensor_copy(w_tot, Lg[:, :, C - 1]))
                    link(nc.vector.tensor_tensor(Lg, w_tot.rearrange("p (g o) -> p g o", o=1).to_broadcast([P, 24, C]), Lg,
                                                 ALU.subtract))
                    nc.vector.tensor_tensor(w_LW, w_L, w_LW, ALU.add).then_inc(sem("rw_L"), 1)
                nc.vector.tensor_tensor(w_B[d], w_kk, w_E, ALU.mult)
                for z in range(4):
                    ins = nc.vector.tensor_scalar(w_K[d][:, z, :], w_E[:, z, :], -1.0, pcol("rwkv_k_a", z), ALU.add, ALU.mult)
                link(ins)
                link(nc.vector.scalar_tensor_tensor(flat(w_K[d]), flat(w_K[d]), 1.0, flat(k_), ALU.add, ALU.mult))
                dve.wait_ge(sem("rw_exp"), 2 * l + d + 1)
                nc.vector.tensor_tensor(w_QR[d][:, 0, :, :], w_kk, excl, ALU.mult)
                nc.vector.tensor_tensor(w_QR[d][:, 1, :, :], w_QR[d][:, 1, :, :], r_, ALU.mult)
                nc.vector.tensor_tensor(w_K[d], w_K[d], incl, ALU.mult)
                nc.vector.tensor_tensor(w_B[d], w_B[d], incl, ALU.mult).then_inc(sem("rw_prep"), 1)
                dve.wait_ge(sem("rw_prep"), 2 * l + d + 1)
            link(nc.vector.tensor_tensor(w_L, r_, k_, ALU.mult))
            for z in range(4):
                ins = nc.vector.tensor_scalar(w_L[:, z, :], w_L[:, z, :], pcol("rwkv_r_k", z), None, ALU.mult)
            ins.then_inc(sem("rw_sq"), 1)
            dve.wait_ge(sem("rw_sums"), 2 * l + 2)
            for z in range(4):
                nc.vector.tensor_tensor(w_E[:, z, :], ps[4 + z][:, 0:T], v_[:, z, :], ALU.mult)
            nc.vector.memset(u_S, 0.0)
            nc.vector.memset(w_Og, 0.0)
            nc.vector.tensor_copy(u_I.rearrange("p (g t) -> p g t", t=C),
                                  K("eye64").rearrange("p (o t) -> p o t", o=1).to_broadcast([P, 8, C]))\
                .then_inc(sem("rw_ready"), 1)
            dve.wait_ge(sem("rw_ready"), l + 1)
            for s, chunks in enumerate(STEPS):
                dve_rwkv_step(dve, link, l, NS * l + s, chunks)
                if s == 1:
                    dve.wait_ge(sem("rw_turn"), 2 * l + 2)
                    nc.vector.tensor_copy(u_S, ps[6][:, :]).then_inc(sem("rw_state"), 1)
            def wide(v):
                return v.rearrange("p (g o) -> p g o", o=1).to_broadcast([P, 24, C])
            link(nc.vector.tensor_reduce(w_tot, w_Og, X_AXIS, ALU.add))
            link(nc.vector.tensor_scalar(w_tot, w_tot, 1.0 / C, None, ALU.mult))
            link(nc.vector.tensor_tensor(w_Og, w_Og, wide(w_tot), ALU.subtract))
            link(nc.vector.tensor_tensor(w_sq, w_Og, w_Og, ALU.mult))
            link(nc.vector.tensor_reduce(w_tot, w_sq, X_AXIS, ALU.add))
            rsqrt(dve, link, nc.vector.tensor_scalar(w_tot, w_tot, 1.0 / C, None, ALU.mult), w_tot, RWKV_EPS, ALU.add)
            nc.vector.tensor_tensor(w_Og, w_Og, wide(w_tot), ALU.mult).then_inc(sem("rw_O"), 1)
            dve.wait_ge(sem("rw_affine"), l + 1)
            link(nc.vector.tensor_tensor(w_E, w_E, w_N, ALU.add))
            dve.wait_ge(sem("rw_gate"), l + 1)
            for z in range(4):
                ins = nc.vector.tensor_tensor(w_E[:, z, :], w_E[:, z, :], ps[4 + z][:, 0:T], ALU.mult)
            ins.then_inc(sem("rw_done"), 1)

        def dve_rwkv_step(dve, link, l, m, chunks):
            def part(u, d):
                return u[:, 256 * d:256 * (d + 1)].rearrange("p (z t) -> p z t", z=4)

            def scores(bank, x):
                return ps[bank][:, :].rearrange("p (z x t) -> p z x t", z=4, x=2)[:, :, x, :]
            dve.wait_ge(sem("rw_pairs"), 3 * m + 2)
            for d in range(2):
                nc.vector.tensor_tensor(part(u_G, d), scores(2 + d, 0), both("before", d), ALU.mult)
            for d in range(2):
                ins = nc.vector.tensor_tensor(part(u_RK, d), scores(2 + d, 1), both("upto", d), ALU.mult)
            ins.then_inc(sem("rw_masked"), 1)
            dve.wait_ge(sem("rw_tok"), 2 * m + 1)
            for d in range(2):
                ins = nc.vector.tensor_tensor(part(u_RB, d), scores(d, 1), both("upto", d), ALU.mult)
            ins.then_inc(sem("rw_masked"), 1)
            for j in range(LEVELS):
                if j:
                    dve.wait_ge(sem("rw_T"), LEVELS * m + j)
                for d in range(2):
                    lv = K("levels")[:, P * j + 64 * d:P * j + 64 * d + 64].rearrange("p (o t) -> p o t", o=1)
                    ins = nc.vector.tensor_tensor(part(u_M, d), part(u_A, d), lv.to_broadcast([P, 4, 64]), ALU.mult)
                ins.then_inc(sem("rw_M"), 1)
                if j == 0:
                    dve.wait_ge(sem("rw_M"), LEVELS * m + 1)
                    nc.vector.tensor_tensor(u_Y, u_I, u_M, ALU.subtract)
                    dve.wait_ge(sem("rw_T"), LEVELS * m + 1)
                    nc.vector.tensor_tensor(u_X, u_I, ps[7][:, :], ALU.subtract).then_inc(sem("rw_XY"), 1)
                    dve.wait_ge(sem("rw_XY"), LEVELS * m + 1)
                else:
                    dve.wait_ge(sem("rw_XYp"), (LEVELS - 1) * m + j)
                    ins = nc.vector.tensor_tensor(u_Y, u_Y, ps[0][:, :], ALU.subtract)
                    if j < LEVELS - 1:
                        ins = nc.vector.tensor_tensor(u_X, u_X, ps[1][:, :], ALU.subtract)
                    ins.then_inc(sem("rw_XY"), 1)
                    dve.wait_ge(sem("rw_XY"), LEVELS * m + j + 1)
            dve.wait_ge(sem("rw_o"), m + 1)
            for d in range(2):
                o = w_Oc[:, chunks[d], :]
                link(nc.vector.tensor_tensor(o, o, ps[4][:, 256 * d:256 * (d + 1)], ALU.add))
            dve.wait_ge(sem("rw_S"), m + 1)
            link(nc.vector.tensor_tensor(u_X, u_S, ps[5][:, :], ALU.add))
            for d in range(2):
                e = w_ends[:, d, :, chunks[d]].rearrange("p (z o) -> p z o", o=1).to_broadcast([P, 4, 64])
                ins = nc.vector.tensor_tensor(part(u_S, d), part(u_X, d), e, ALU.mult)
            ins.then_inc(sem("rw_state"), 1)
            dve.wait_ge(sem("rw_state"), m + l + 1 + (1 if m % NS >= 2 else 0))

        g_T = arena[:, 0:24 * T].rearrange("p (z t) -> p z t", t=T)
        merged = arena[:, 24 * T:32 * T].rearrange("p (z t) -> p z t", t=T)
        m_tmp = [arena[:, TMP + T * b:TMP + T * (b + 1)] for b in range(2)]
        res_tmp = [arena[:, TMP + 1024 + 512 * b:TMP + 1536 + 512 * b] for b in range(2)]

        def pe_merge(pe, l):
            for z in range(24):
                if z % 4 == 0:
                    w = chunk_here(pe, l, 22 + z // 4)
                if z == 0:
                    pe.wait_ge(sem("rw_affine"), l + 1)
                if z >= 4:
                    pe.wait_ge(sem("gate_act"), 24 * l + z - 3)
                for k in range(KT):
                    ins = nc.tensor.matmul(ps[z % 4][:, 0:T], w[:, k, P * (z % 4):P * (z % 4) + P], hT[:, k, :],
                                           start=(k == 0), stop=(k == KT - 1))
                ins.then_inc(sem("gate_mm"), 1)
            pe.wait_ge(sem("rw_done"), l + 1)
            for b in range(3):
                w = chunk_here(pe, l, 28 + b)
                for z in range(8):
                    n = 8 * b + z
                    if n >= 4:
                        pe.wait_ge(sem("branch_dve"), 24 * l + n - 3)
                    for k in range(4):
                        ins = nc.tensor.matmul(ps[4 + n % 4][:, 0:T], w[:, k, P * z:P * (z + 1)], oT[:, b, k, :],
                                               start=(k == 0), stop=(k == 3))
                    ins.then_inc(sem("branch_mm"), 1)
            pe.wait_ge(sem("merged"), 8 * (l + 1))
            pe.wait_ge(sem("gate_act"), 24 * (l + 1))
            for c in range(2):
                w = chunk_here(pe, l, 31 + c)
                for t in range(NT):
                    n = NT * c + t
                    if n >= 4:
                        pe.wait_ge(sem("res_dve"), 6 * l + n - 3)
                    for k in range(KT):
                        ins = nc.tensor.matmul(ps[n % 4][:, :], merged[:, k, P * t:P * (t + 1)], w[:, k, :],
                                               start=(k == 0), stop=(k == KT - 1))
                    ins.then_inc(sem("out_mm"), 1)

        def act_merge(act, l):
            act.wait_ge(sem("rw_ready"), l + 1)
            act.wait_ge(sem("rw_done"), l + 1)
            for z in range(24):
                act.wait_ge(sem("gate_mm"), 24 * l + z + 1)
                nc.scalar.activation(g_T[:, z, :], ps[z % 4][:, 0:T], ACT.Sigmoid).then_inc(sem("gate_act"), 1)
            act_norm_roots(act)

        def dve_merge(dve, link, l):
            for n in range(24):
                b, z = divmod(n, 8)
                dve.wait_ge(sem("branch_mm"), 24 * l + n + 1)
                dve.wait_ge(sem("gate_act"), 24 * l + n + 1)
                bank = ps[4 + n % 4][:, 0:T]
                if b == 0:
                    nc.vector.tensor_tensor(merged[:, z, :], bank, g_T[:, n, :], ALU.mult).then_inc(sem("branch_dve"), 1)
                    continue
                nc.vector.tensor_tensor(m_tmp[n % 2], bank, g_T[:, n, :], ALU.mult).then_inc(sem("branch_dve"), 1)
                dve.wait_ge(sem("branch_dve"), 24 * l + n + 1)
                ins = nc.vector.tensor_tensor(merged[:, z, :], merged[:, z, :], m_tmp[n % 2], ALU.add)
                if b == 2:
                    ins.then_inc(sem("merged"), 1)
                else:
                    link(ins)
            for n in range(6):
                c, t = divmod(n, NT)
                dve.wait_ge(sem("out_mm"), 6 * l + n + 1)
                dve_residual(dve, link, ps[n % 4], 0, t, c, "res_dve", 6 * l + n + 1)
            dve_out_norm(dve, link, l, 0)

        def dve_residual(dve, link, bank, which, t, c, done, value):
            cols = slice(512 * c, 512 * (c + 1))
            x = X[:, t, cols]
            tmp = res_tmp[(t + c) % 2]
            nc.vector.tensor_tensor(tmp, bank[:, :], gate[:, which, min(t, 1), cols], ALU.mult).then_inc(sem(done), 1)
            dve.wait_ge(sem(done), value)
            link(nc.vector.scalar_tensor_tensor(x, x, ALPHA, tmp, ALU.mult, ALU.add))

        def dve_out_norm(dve, link, l, which):
            n = 2 * l + which
            for t in range(NT):
                link(dve_layer_norm(dve, link, X[:, t, :], X[:, t, :]))
                if t == 0:
                    dve.wait_ge(sem("ln_in"), 32 * (n + 1))
                link(nc.vector.tensor_tensor(X[:, t, :], X[:, t, :], lnp[:, 0, :], ALU.mult))
                nc.vector.tensor_tensor(X[:, t, :], X[:, t, :], lnp[:, 1, :], ALU.add).then_inc(sem("x_done"), 1)
                dve.wait_ge(sem("x_done"), NT * n + t + 1)

        q_T = arena[:, 0:8 * T].rearrange("p (h t) -> p h t", t=T)
        keys_in = arena[:, 3072:4096].rearrange("p (h x) -> p h x", h=PH)
        keys_T = arena[:, 4096:5120].rearrange("p (h k) -> p h k", h=PH)
        sc = [arena[:, 5120 + 2048 * b:7168 + 2048 * b].rearrange("p (s h k) -> p s h k", s=2, h=PH) for b in range(2)]
        cand = arena[:, 9216:11264].rearrange("p (h a b) -> p h a b", h=PH, a=TOPK)
        eq = arena[:, 11264:13312]
        TOP = 13312

        def tops(at, n, dt=F32):
            v = arena[:, TOP + at:TOP + at + n]
            return v if dt is F32 else v.bitcast(dt)
        ts_ = tops(0, 256).rearrange("p (s h k) -> p s h k", s=2, h=PH)
        ti_ = tops(256, 256, U32).rearrange("p (s h k) -> p s h k", s=2, h=PH)
        tif = tops(512, 256).rearrange("p (s h k) -> p s h k", s=2, h=PH)
        fs_ = tops(768, 128).rearrange("p (h k) -> p h k", h=PH)
        fp_ = tops(896, 128, U32).rearrange("p (h k) -> p h k", h=PH)
        fi_ = tops(1024, 256, U32).rearrange("p (s x) -> p s x", s=2)
        ff_ = tops(1280, 256).rearrange("p (s x) -> p s x", s=2)
        ijg = [tops(1536 + 384 * b, 384).rearrange("p (s x) -> p s x", s=3) for b in range(2)]
        fsum = small[:, 0:8]
        LOW = -3.0e38

        def pool_keys(pool, l):
            pool.wait_ge(sem("x_done"), NT * (2 * l + 1))
            pool.dma_start(keys_in.rearrange("p h (s d) -> p h s d", s=2),
                           a["peer_keys"][l].rearrange("h s k d -> k h s d")).then_inc(sem("keys_in"), 16)

        def pe_select(pe, l):
            pe.wait_ge(sem("h_ready"), 6 * (2 * l + 2))
            for h in range(PH):
                if h % 4 == 0:
                    w = chunk_here(pe, l, 33 + h // 4)
                if h >= 4:
                    pe.wait_ge(sem("query_act"), 8 * l + h - 3)
                for k in range(KT):
                    ins = nc.tensor.matmul(ps[4 + h % 4][:, 0:T], w[:, k, P * (h % 4):P * (h % 4) + P], hT[:, k, :],
                                           start=(k == 0), stop=(k == KT - 1))
                ins.then_inc(sem("query_mm"), 1)
            pe.wait_ge(sem("keys_in"), 16 * (l + 1))
            for h in range(PH):
                ins = nc.tensor.transpose(ps[h // 4][:, P * (h % 4):P * (h % 4) + P], keys_in[:, h, :], ident)
                if h % 4 == 3:
                    ins.then_inc(sem("keys_turned"), 1)
            pe.wait_ge(sem("query_act"), 8 * (l + 1))
            pe.wait_ge(sem("keys_act"), 2 * (l + 1))
            for t in range(NT):
                if t == 2:
                    pe.wait_ge(sem("score_act"), 4 * (NT * l + t - 1))
                for s in range(2):
                    rows = slice(64 * s, 64 * s + 64)
                    for h in range(PH):
                        ins = nc.tensor.matmul(ps[4 * (t % 2) + 2 * s + h // 4][:, P * (h % 4):P * (h % 4) + P],
                                               q_T[rows, h, P * t:P * (t + 1)], keys_T[rows, h, :], start=True, stop=True)
                        if h % 4 == 3:
                            ins.then_inc(sem("score_mm"), 1)
            for t in range(NT):
                pe.wait_ge(sem("chosen"), NT * l + t + 1)
                for i in range(3):
                    ins = nc.tensor.transpose(ps[5 + t][:, P * i:P * (i + 1)], ijg[t % 2][:, i, :], ident)
                ins.then_inc(sem("chosen_T"), 1)

        def act_select(act, l):
            act.wait_ge(sem("x_done"), NT * (2 * l + 1))
            for h in range(PH):
                act.wait_ge(sem("query_mm"), 8 * l + h + 1)
                nc.scalar.activation(q_T[:, h, :], ps[4 + h % 4][:, 0:T], ACT.Copy).then_inc(sem("query_act"), 1)
            for i in range(2):
                act.wait_ge(sem("keys_turned"), 2 * l + i + 1)
                nc.scalar.activation(keys_T[:, 4 * i:4 * i + 4, :].rearrange("p h k -> p (h k)"), ps[i][:, :], ACT.Copy)\
                    .then_inc(sem("keys_act"), 1)
            for t in range(NT):
                if t == 2:
                    act.wait_ge(sem("topped"), NT * l + 1)
                for i in range(4):
                    act.wait_ge(sem("score_mm"), 4 * (NT * l + t) + i + 1)
                    nc.scalar.activation(sc[t % 2][:, i // 2, 4 * (i % 2):4 * (i % 2) + 4, :].rearrange("p h k -> p (h k)"),
                                         ps[4 * (t % 2) + i][:, :], ACT.Copy).then_inc(sem("score_act"), 1)
                if t:
                    act_softmax(act, l, t - 1)
            act_softmax(act, l, 2)

        def act_softmax(act, l, t):
            act.wait_ge(sem("final_tops"), NT * l + t + 1)
            nc.scalar.activation(fs_, fs_, ACT.Exp).then_inc(sem("final_exp"), 1)
            act.wait_ge(sem("chosen_T"), NT * l + t + 1)
            nc.scalar.activation(IJG[:, :, P * t:P * (t + 1)], ps[5 + t][:, 0:3 * P].rearrange("p (i n) -> p i n", i=3),
                                 ACT.Copy).then_inc(sem("ijg"), 1)

        def dve_top16(link, link_all, values, vals, idxs):
            n = len(values)
            for half in range(2):
                for i in range(n):
                    ins = nc.vector.max(vals[i][:, 8 * half:8 * half + 8], values[i])
                link(ins)
                for i in range(n):
                    ins = nc.vector.max_index(idxs[i][:, 8 * half:8 * half + 8], vals[i][:, 8 * half:8 * half + 8], values[i])
                link(ins)
                if half == 0:
                    for i in range(n):
                        ins = nc.vector.match_replace(values[i], vals[i][:, 0:8], values[i], LOW)
                    link(ins)

        def dve_select(dve, link, l):
            for t in range(NT):
                dve.wait_ge(sem("score_act"), 4 * (NT * l + t + 1))
                s_t = sc[t % 2]
                groups = [(s, h) for s in range(2) for h in range(PH)]
                dve_top16(link, None, [s_t[:, s, h, :] for s, h in groups], [ts_[:, s, h, :] for s, h in groups],
                          [ti_[:, s, h, :] for s, h in groups])
                nc.vector.tensor_copy(tif, ti_).then_inc(sem("topped"), 1)
                link(nc.vector.tensor_tensor(
                    cand, ts_[:, 0, :, :].rearrange("p h (a o) -> p h a o", o=1).to_broadcast([P, PH, TOPK, TOPK]),
                    ts_[:, 1, :, :].rearrange("p h (o b) -> p h o b", o=1).to_broadcast([P, PH, TOPK, TOPK]), ALU.add))
                dve_top16(link, None, [cand[:, h, :, :].rearrange("p a b -> p (a b)") for h in range(PH)],
                          [fs_[:, h, :] for h in range(PH)], [fp_[:, h, :] for h in range(PH)])
                link(nc.vector.tensor_copy(fsum.rearrange("p (h o) -> p h o", o=1), fs_[:, :, 0:1]))
                nc.vector.tensor_tensor(fs_, fs_, fsum.rearrange("p (h o) -> p h o", o=1).to_broadcast([P, PH, TOPK]),
                                        ALU.subtract).then_inc(sem("final_tops"), 1)
                fpf = fp_.rearrange("p h k -> p (h k)")
                nc.vector.tensor_scalar(fi_[:, 0, :], fpf, 4, None, ALU.logical_shift_right)
                link(nc.vector.tensor_scalar(fi_[:, 1, :], fpf, 15, None, ALU.bitwise_and))
                link(nc.vector.tensor_copy(ff_, fi_))
                out = ijg[t % 2]
                if t == 2:
                    dve.wait_ge(sem("chosen_T"), NT * l + 1)
                for s in range(2):
                    e3 = eq.rearrange("p (x a) -> p x a", a=TOPK)
                    e4 = eq.rearrange("p (h k a) -> p h k a", h=PH, k=TOPK)
                    link(nc.vector.tensor_tensor(
                        e3, ff_[:, s, :].rearrange("p (x o) -> p x o", o=1).to_broadcast([P, P, TOPK]),
                        K("iota")[:, 0:TOPK].rearrange("p (o a) -> p o a", o=1).to_broadcast([P, P, TOPK]), ALU.is_equal))
                    link(nc.vector.tensor_tensor(
                        e4, e4, tif[:, s, :, :].rearrange("p h (o a) -> p h o a", o=1).to_broadcast([P, PH, TOPK, TOPK]),
                        ALU.mult))
                    link(nc.vector.tensor_reduce(out[:, s, :], e3, X_AXIS, ALU.add))
                dve.wait_ge(sem("final_exp"), NT * l + t + 1)
                link(nc.vector.tensor_reduce(fsum, fs_, X_AXIS, ALU.add))
                link(nc.vector.reciprocal(fsum, fsum))
                nc.vector.tensor_tensor(out[:, 2, :].rearrange("p (h k) -> p h k", h=PH), fs_,
                                        fsum.rearrange("p (h o) -> p h o", o=1).to_broadcast([P, PH, TOPK]),
                                        ALU.mult).then_inc(sem("chosen"), 1)
                dve.wait_ge(sem("chosen"), NT * l + t + 1)
            dve.wait_ge(sem("ijg"), NT * (l + 1))
            dve.wait_ge(sem("ijg"), NT * (l + 1))
            nc.vector.tensor_copy(stat[:, 0:1], IJG[:, 0, 0:1]).then_inc(sem("select_done"), 1)

        def pe_gates(pe, s, b, bank):
            pe.wait_ge(sem("onehot"), s + 1)
            for n in range(SETN):
                ins = nc.tensor.matmul(bank[:, QUART * n:QUART * (n + 1)], E2[b][:, n, :], E1[b][:, n, :],
                                       start=True, stop=True)
            ins.then_inc(sem("gate_psum"), 1)

        def dve_onehot(dve, Q, n0, b):
            for n in range(SETN):
                tok = bass.ds(n0 + n, 1)
                nc.vector.tensor_scalar(E2[b][:, n, :], K("iota"), IJG[:, 1, tok], IJG[:, 2, tok], ALU.is_equal, ALU.mult)
            nc.vector.tensor_tensor(
                E1[b], K("iota")[:, QUART * Q:QUART * (Q + 1)].rearrange("p (o i) -> p o i", o=1)
                .to_broadcast([P, SETN, QUART]),
                IJG[:, 0, bass.ds(n0, SETN)].rearrange("p (n o) -> p n o", o=1).to_broadcast([P, SETN, QUART]),
                ALU.is_equal).then_inc(sem("onehot"), 1)

        def act_store(act, s, Q, n0, bank):
            act.wait_ge(sem("gate_psum"), s + 1)
            nc.scalar.activation(G[:, QUART * (Q % 2):QUART * (Q % 2 + 1), bass.ds(n0, SETN)],
                                 bank[:, 0:T].rearrange("p (n i) -> p i n", i=QUART), ACT.Copy).then_inc(sem("gate_set"), 1)

        def pe_first_gates(pe, base):
            for s in range(2):
                pe_gates(pe, base + s, s, ps[6 + s])
            with pe.Fori(1, QUART // 2) as pair:
                for s in range(2):
                    pe.wait_ge(sem("gate_set"), pair * 2 + (base + s - 1))
                    pe_gates(pe, pair * 2 + (base + s), s, ps[6 + s])
            pe.wait_ge(sem("gate_set"), base + QUART)

        def dve_first_gates(dve, base):
            for s in range(2):
                dve_onehot(dve, 0, SETN * s, s)
            with dve.Fori(1, QUART // 2) as pair:
                for s in range(2):
                    dve.wait_ge(sem("gate_psum"), pair * 2 + (base + s - 1))
                    dve_onehot(dve, 0, pair * (2 * SETN) + SETN * s, s)

        def act_first_gates(act, base):
            with act.Fori(0, QUART // 2) as pair:
                for s in range(2):
                    act_store(act, pair * 2 + (base + s), 0, pair * (2 * SETN) + SETN * s, ps[6 + s])

        def steps(eng, run):
            n = QUART // 2
            for Q in range(NQ):
                first, last = Q == 0, Q == NQ - 1
                if first:
                    run(Q, 0, 0)
                with eng.Fori(1 if first else 0, n - 1 if last else n) as pair:
                    run(Q, pair * 2, None)
                if last:
                    run(Q, QUART - 2, QUART - 2)

        def pe_experts(pe, base):
            def turn_a(g, b):
                pe.wait_ge(sem(f"u_in{b}"), g * 8 + (16 - 8 * b))
                for k in range(4):
                    ins = nc.tensor.transpose(ps[7][:, P * k:P * (k + 1)], ublk[b][:, P * k:P * (k + 1)], ident)
                ins.then_inc(sem("turn_a"), 1)

            def turn_b(g, b):
                pe.wait_ge(sem("uT_a"), g + 1)
                for k in range(4):
                    ins = nc.tensor.transpose(ps[7][:, P * k:P * (k + 1)], ublk[b][:, P * (k + 4):P * (k + 5)], ident)
                ins.then_inc(sem("u_used"), 1)

            def hidden(g, b, bank_used):
                pe.wait_ge(sem("uT_b"), g + 1)
                if bank_used:
                    pe.wait_ge(sem("gelu"), g)
                for k in range(KT):
                    ins = nc.tensor.matmul(ps[6][:, 0:T], uT[b][:, k, :], hT[:, k, :], start=(k == 0), stop=(k == KT - 1))
                ins.then_inc(sem("hidden"), 1)

            def value(b, part, start=False, stop=False):
                for t, c in ((0, 0), (0, 1), (1, 0), (1, 1), (2, 0), (2, 1))[3 * part:3 * part + 3]:
                    ins = nc.tensor.matmul(ps[2 * t + c][:, :], Wg[b][:, P * t:P * (t + 1)], vblk[b][:, 512 * c:512 * (c + 1)],
                                           start=start, stop=stop)
                return ins

            def value_ready(g, b):
                pe.wait_ge(sem(f"v_in{b}"), g * 8 + (16 - 8 * b))
                pe.wait_ge(sem("weighted"), g + 1)

            turn_a(base, 0)
            turn_b(base, 0)

            def run(Q, k, peeled):
                for j in range(2):
                    g = k + (base + QUART * Q + j)
                    begin = peeled == 0 and j == 0
                    end = peeled == QUART - 2 and j == 1
                    if not end:
                        if not begin and Q < NQ - 1:
                            pe.wait_ge(sem("gate_set"), g + QUART)
                        else:
                            if j == 0 and Q == NQ - 1:
                                pe.wait_ge(sem("gate_set"), base + NQ * QUART)
                            pe.wait_ge(sem("uT_b"), g + 1)
                        turn_a(g + 1, 1 - j)
                    hidden(g, j, not begin)
                    if not end:
                        turn_b(g + 1, 1 - j)
                    first = peeled == 0 and j == 1
                    if not begin:
                        value_ready(g - 1, 1 - j)
                        value(1 - j, 0, start=first)
                    if Q < NQ - 1:
                        pe.wait_ge(sem("uT_b"), g + 2)
                        pe_gates(pe, g + QUART, j, ps[7])
                    if not begin:
                        value(1 - j, 1, start=first).then_inc(sem("v_used"), 1)
            steps(pe, run)
            end = base + NKEYS - 1
            value_ready(end, 1)
            value(1, 0, stop=True)
            value(1, 1, stop=True).then_inc(sem("v_used"), 1)

        def act_experts(act, base):
            def turn(g, b, buffer_used):
                act.wait_ge(sem("turn_a"), g + 1)
                if buffer_used:
                    act.wait_ge(sem("hidden"), g - 1)
                nc.scalar.activation(uT[b][:, 0:4, :].rearrange("p k e -> p (k e)"), ps[7][:, :], ACT.Copy)\
                    .then_inc(sem("uT_a"), 1)

            turn(base, 0, False)

            def run(Q, k, peeled):
                for j in range(2):
                    g = k + (base + QUART * Q + j)
                    begin = peeled == 0 and j == 0
                    if not (peeled == QUART - 2 and j == 1):
                        turn(g + 1, 1 - j, not begin)
                    act.wait_ge(sem("hidden"), g + 1)
                    if not begin:
                        act.wait_ge(sem("weighted"), g)
                    nc.scalar.activation(ge, ps[6][:, 0:T], ACT.Gelu).then_inc(sem("gelu"), 1)
                    if Q < NQ - 1:
                        act_store(act, g + QUART, Q + 1, k * SETN + SETN * j, ps[7])
            steps(act, run)

        def dve_experts(dve, base):
            def turn(g, b, buffer_used):
                dve.wait_ge(sem("u_used"), g + 1)
                if buffer_used:
                    dve.wait_ge(sem("hidden"), g - 1)
                nc.vector.tensor_copy(uT[b][:, 4:8, :].rearrange("p k e -> p (k e)"), ps[7][:, :]).then_inc(sem("uT_b"), 1)

            turn(base, 0, False)

            def run(Q, k, peeled):
                for j in range(2):
                    g = k + (base + QUART * Q + j)
                    if Q < NQ - 1:
                        dve.wait_ge(sem("gate_psum"), g + (QUART - 1))
                        dve_onehot(dve, Q + 1, k * SETN + SETN * j, j)
                    if not (peeled == QUART - 2 and j == 1):
                        turn(g + 1, 1 - j, not (peeled == 0 and j == 0))
                    if j == 0:
                        dve.wait_ge(sem("gate_set"), base + QUART * (Q + 1))
                    dve.wait_ge(sem("gelu"), g + 1)
                    if not peeled == 0:
                        dve.wait_ge(sem("v_used"), g - 1)
                    i = bass.ds(k + (QUART * (Q % 2) + j), 1)
                    nc.vector.tensor_tensor(Wg[j].rearrange("p (o n) -> p o n", o=1), ge.rearrange("p (o n) -> p o n", o=1),
                                            G[:, i, :], ALU.mult).then_inc(sem("weighted"), 1)
            steps(dve, run)

        def pe_peer(pe, l):
            pe_select(pe, l)
            pe.wait_ge(sem("select_done"), l + 1)
            pe_first_gates(pe, NKEYS * l)
            pe_experts(pe, NKEYS * l)

        def act_peer(act, l):
            act_select(act, l)
            act.wait_ge(sem("select_done"), l + 1)
            act_first_gates(act, NKEYS * l)
            act_experts(act, NKEYS * l)
            act_norm_roots(act)

        def dve_peer(dve, link, l):
            dve_select(dve, link, l)
            dve.wait_ge(sem("select_done"), l + 1)
            dve_first_gates(dve, NKEYS * l)
            dve_experts(dve, NKEYS * l)
            dve.wait_ge(sem("v_used"), NKEYS * (l + 1))
            for n in range(6):
                t, c = divmod(n, 2)
                dve_residual(dve, link, ps[n], 1, t, c, "peer_res", 6 * l + n + 1)
            dve_out_norm(dve, link, l, 1)
            dve.sem_inc(sem("peer_done"), 1)

        @block.sync
        def _(sp):
            sp.dma_start(const[:, :], a["consts"][:, 0:WHERE["reverse"].start]).then_inc(sem("const_in"), 16)
            sp.dma_start(X[:, 0, :], a["x_prompt"][0]).then_inc(sem("x_in"), 16)
            sp.dma_start(X[:, 1:3, :], a["x_sample"][0].rearrange("(t p) d -> p t d", p=P)).then_inc(sem("x_in"), 16)
            for l in range(DEPTH):
                if upto < 8 and l:
                    break
                for c in range(NCHUNK if upto >= 7 else (33 if upto >= 6 else 22)):
                    n = chunk_no(l, c)
                    if n >= 2:
                        chunk_released(sp, n - 2)
                    if l and c < 2:
                        sp.wait_ge(sem("peer_done"), l)
                    src, k, w = chunk_source(l, c)
                    sp.dma_start(slot(n, k, w), src).then_inc(sem(f"chunk_in{n % 2}"), 16)
                sp_experts(sp, l)

        @block.gpsimd
        def _(pool):
            pool.dma_start(crow[0:8, :], a["c_ctx"].rearrange("(k p) -> k p", p=P)).then_inc(sem("c_in"), 16)
            pool.dma_start(crow[8:16, :], a["c"][0].rearrange("(k p) -> k p", p=P)).then_inc(sem("c_in"), 16)
            for l in range(DEPTH):
                if upto < 8 and l:
                    break
                if l:
                    pool.wait_ge(sem("peer_done"), l)
                for nm, n in PARAMS:
                    pool.dma_start(prow[PAR[nm]:PAR[nm] + n, :], par_srcs[nm](l)).then_inc(sem("param_in"), 16)
                for s in range(2):
                    pool.dma_start(bmod[s:s + 1, :], a["b_mod"][l:l + 1, :]).then_inc(sem("param_in"), 16)
                if upto >= 3:
                    pool_na(pool, l)
                    pool_na_out(pool, l)
                if upto >= 4:
                    pool_ret(pool, l)
                    pool_ret_out(pool, l)
                if upto >= 5:
                    pool_rwkv(pool, l)
                    pool_rwkv_out(pool, l)
                if upto >= 6:
                    ln_rows(pool, l, "ln_a_g", "ln_a_b", 0)
                if upto >= 7:
                    pool_keys(pool, l)
                if upto >= 7:
                    ln_rows(pool, l, "ln_f_g", "ln_f_b", 1)
            if upto >= 8:
                pool.wait_ge(sem("x_done"), 2 * DEPTH * NT)
                pool.dma_start(y_prompt[0], X[:, 0, :]).then_inc(sem("stored"), 16)
                pool.dma_start(y_sample[0].rearrange("(t p) d -> p t d", p=P), X[:, 1:3, :]).then_inc(sem("stored"), 16)
            if upto >= 5:
                pool.wait_ge(sem("stored"), 16 * (DEPTH * 7 + 2) if upto >= 8 else 16 * 7)


        @block.tensor
        def _(pe):
            pe_cond(pe)
            for l in range(DEPTH):
                pe_mod(pe, l)
                pe_norm(pe, 2 * l)
                pe_proj(pe, l)
                if upto >= 3:
                    pe_na(pe, l)
                if upto >= 4:
                    pe_ret(pe, l)
                if upto >= 5:
                    pe_rwkv(pe, l)
                if upto >= 6:
                    pe_merge(pe, l)
                    pe_norm(pe, 2 * l + 1)
                if upto >= 7:
                    pe_peer(pe, l)
                if upto < 8:
                    break

        @block.scalar
        def _(act):
            link = linker(act, "act")
            act_cond(act)
            for l in range(DEPTH):
                act_norm(act, 2 * l)
                act_proj(act, l)
                if upto >= 3:
                    act_na(act, l)
                if upto >= 4:
                    act_ret(act, link, l)
                if upto >= 5:
                    act_rwkv(act, link, l)
                if upto >= 6:
                    act_merge(act, l)
                    act_norm(act, 2 * l + 1)
                if upto >= 7:
                    act_peer(act, l)
                if upto < 8:
                    break

        @block.vector
        def _(dve):
            link = linker(dve, "dve")
            dve_cond(dve)
            for l in range(DEPTH):
                dve_mod(dve, l)
                dve_norm(dve, link, 2 * l)
                dve_proj(dve, l)
                if upto >= 3:
                    dve_na(dve, link, l)
                if upto >= 4:
                    dve_ret(dve, link, l)
                if upto >= 5:
                    dve_rwkv(dve, link, l)
                if upto >= 6:
                    dve_merge(dve, link, l)
                    dve_norm(dve, link, 2 * l + 1)
                if upto >= 7:
                    dve_peer(dve, link, l)
                if upto < 8:
                    break


INS = ["x_prompt", "x_sample", "cache_na_k", "cache_na_v", "state_ret", "state_rwkv", "c", "c_ctx", "w_mod", "b_mod", "w_in",
       "na_rpb", "ret_decay_logit", "ret_gn_w", "ret_gn_b", "rwkv_mu", "rwkv_w0", "rwkv_w_up", "rwkv_a0", "rwkv_a_up",
       "rwkv_g_up", "rwkv_k_k", "rwkv_k_a", "rwkv_r_k", "rwkv_gn_w", "rwkv_gn_b", "w_br", "w_out", "ln_a_g", "ln_a_b",
       "ln_f_g", "ln_f_b", "peer_wq", "peer_keys", "peer_u", "peer_v"]
OUTS = [(1, 128, 1024), (1, 256, 1024), (1, 2, 8, 128, 64), (1, 2, 8, 128, 64), (1, 2, 2, 4, 64, 128), (1, 2, 2, 8, 64, 64)]


def kernel(**inputs):
    import concourse.bacc as bacc
    from concourse.bass_utils import run_bass_kernel_spmd

    nc = bacc.Bacc("TRN2", target_bir_lowering=False, num_devices=1)
    arrays, args = {}, {}
    for name in INS + ["consts"]:
        x = CONSTS if name == "consts" else np.ascontiguousarray(inputs[name])
        arrays[f"in_{name}"] = x
        args[name] = nc.dram_tensor(f"in_{name}", x.shape, mybir.dt.from_np(x.dtype), kind="ExternalInput").ap()
    outs = [nc.dram_tensor(f"out_{i}", s, F32, kind="ExternalOutput").ap() for i, s in enumerate(OUTS)]
    build(nc, args, outs)
    r = run_bass_kernel_spmd(nc, [arrays], core_ids=[0])
    return tuple(r.results[0][f"out_{i}"] for i in range(len(OUTS)))
```

```python
from contextlib import ExitStack

import numpy as np

import concourse.bass as bass
from concourse import mybir

ALU = mybir.AluOpType
ACT = mybir.ActivationFunctionType
F32 = mybir.dt.float32
U32 = mybir.dt.uint32
BF16 = mybir.dt.bfloat16
X_AXIS = mybir.AxisListType.X

P = 128
D = 1024
KT = D // P
DEPTH = 2
NT = 3
T = NT * P
NSEQ = 2
GRID_W = 64
WIN_C = 16
HN = 8
DH = 64
RH = 4
C = 64
NCH = T // C
LEVELS = 6
TOPK = 16
FULL = TOPK // 2
PH = 8
NKEYS = 128
ALPHA = float((2 * DEPTH) ** 0.25)
EPS = 1e-5
RWKV_EPS = 64e-5
DECAY = -0.606531
NQ = 4
QUART = NKEYS // NQ
SETN = T // QUART

Q_NA, K_NA, V_NA, Q_RT, K_RT, V_RT, G_RT, R_RW, K_RW, V_RW, W_RW, A_RW, GL_RW = (
    0, 4, 8, 12, 14, 16, 20, 24, 28, 32, 36, 37, 38)
NZ = 39
Z_FULL = 9
GATE_COL = NZ * P
RING = 4096

PARAMS = (("rwkv_mu", 15), ("rwkv_w0", 8), ("rwkv_a0", 8), ("rwkv_k_k", 4), ("rwkv_k_a", 4), ("rwkv_r_k", 4),
          ("rwkv_gn_w", 4), ("rwkv_gn_b", 4), ("ret_gn_w", 4), ("ret_gn_b", 4))
NPAR = sum(n for _, n in PARAMS)
PAR = {}
for _name, _n in PARAMS:
    PAR[_name] = sum(n for m, n in PARAMS[:[x for x, _ in PARAMS].index(_name)])


def shape_constants():
    p = np.arange(P)
    parts = {}
    parts["ident"] = np.eye(P)
    parts["iota"] = np.tile(np.arange(P), (P, 1))
    parts["headsum"] = (p[:, None] // 64 == p[None, :] // 64)
    d = p % 64
    half, within = d // 32, d % 32
    first = within < 16
    partner = np.where(first, p + 16, p - 16)
    swap = np.zeros((P, P))
    swap[partner, p] = np.where(first, -1.0, 1.0)
    parts["swap"] = swap
    pos = np.arange(256)
    freqs = (1.0 / (10000.0 ** (np.arange(16, dtype=np.float32) / np.float32(16)))).astype(np.float32)
    axis_pos = np.where(half[:, None] == 0, pos[None] // GRID_W, pos[None] % GRID_W).astype(np.float32)
    ang = (axis_pos * freqs[within % 16][:, None]).astype(np.float32)
    parts["cos"] = np.cos(ang)
    parts["sin"] = np.sin(ang)
    cq, ck = p % GRID_W, np.arange(GRID_W)
    start = np.clip(cq - WIN_C // 2, 0, GRID_W - WIN_C)
    rel = ck[None] - start[:, None]
    parts["window"] = np.where((rel >= 0) & (rel < WIN_C), 0.0, -1e30)
    diff = (p[None, :] - p[:, None]).astype(np.float32)
    parts["dist"] = np.abs(diff)
    parts["tri_f"] = diff >= 0
    parts["tri_b"] = diff <= 0
    parts["far_f"] = P + diff
    parts["far_b"] = P - diff
    parts["age_f"] = np.tile(pos + 1.0, (P, 1))
    parts["age_b"] = np.tile(256.0 - pos, (P, 1))
    parts["left"] = np.stack([127.0 - p, 1.0 * p], 1)
    s = (p % C)[:, None]
    t = np.arange(C)[None]
    parts["before"] = np.concatenate([s < t, s > t], 1)
    parts["upto"] = np.concatenate([s <= t, s >= t], 1)
    lv = []
    for j in range(LEVELS):
        b = 1 << j
        same = (s // (2 * b)) == (t // (2 * b))
        lv += [same & (s // b % 2 == 0) & (t // b % 2 == 1), same & (s // b % 2 == 1) & (t // b % 2 == 0)]
    parts["levels"] = np.concatenate(lv, 1)
    parts["carry"] = np.tile((np.arange(T) % C != 0), (P, 1))
    parts["eye64"] = np.tile(np.eye(C), (2, 1))
    parts["reverse"] = (p[:, None] // 64 == p[None, :] // 64) & (p[:, None] % 64 == 63 - p[None, :] % 64)
    where, cols, n = {}, [], 0
    for k, v in parts.items():
        cols.append(np.asarray(v, np.float32))
        where[k] = slice(n, n + v.shape[1])
        n += v.shape[1]
    return np.ascontiguousarray(np.concatenate(cols, 1)), where


CONSTS, WHERE = shape_constants()


def build(nc, a, out):
    y_prompt, y_sample, new_na_k, new_na_v, new_state_ret, new_state_rwkv = out
    ctx = ExitStack()
    with ctx:
        def sb(name, shape, dt=F32):
            return ctx.enter_context(nc.sbuf_tensor(name, shape, dt))

        sems = {}

        def sem(name):
            if name not in sems:
                sems[name] = ctx.enter_context(nc.semaphore(name))
            return sems[name]

        const = sb("const", [P, WHERE["reverse"].start])
        X = sb("X", [P, NT, D])
        hT = sb("hT", [P, KT, T])
        gate = sb("gate", [P, 2, NSEQ, D])
        lnp = sb("lnp", [P, 2, D])
        ring = sb("ring", [P, 2, RING])
        arena = sb("arena", [P, 28672])
        modT = sb("modT", [P, 32, NSEQ])
        silT = sb("silT", [P, 16])
        par = sb("par", [P, NPAR])
        stat = sb("stat", [P, 40])
        decl = sb("decl", [P, 48])
        small = sb("small", [P, 72])
        ps = [ctx.enter_context(nc.psum_tensor(f"ps{i}", [P, 512], F32)) for i in range(8)]

        def K(name):
            return const[:, WHERE[name]]

        def area(at, n, **kw):
            v = arena[:, at:at + n]
            return v.rearrange(kw.pop("r"), **kw) if kw else v

        ident = K("ident")
        TL = T
        ZT = arena[:, 0:NZ * TL].rearrange("p (z t) -> p z t", t=TL)
        oT = arena[:, NZ * TL:(NZ + 12) * TL].rearrange("p (b z t) -> p b z t", b=3, t=TL)
        TMP = (NZ + 12) * TL

        block = ctx.enter_context(nc.Block())

        chain = {"dve": 0, "act": 0, "pool": 0}

        def linker(eng, key):
            def link(ins):
                chain[key] += 1
                ins.then_inc(sem(key + "_chain"), 1)
                eng.wait_ge(sem(key + "_chain"), chain[key])
            return link

        turns = {"dve": 0, "act": 0}

        def rsqrt(dve, link, ins, v, eps, op):
            link(ins)
            turns["dve"] += 1
            nc.vector.tensor_scalar(v, v, eps, None, op).then_inc(sem("square_ready"), 1)
            dve.wait_ge(sem("root_ready"), turns["dve"])
            link(nc.vector.reciprocal(v, v))

        def act_root(act, v):
            turns["act"] += 1
            act.wait_ge(sem("square_ready"), turns["act"])
            nc.scalar.activation(v, v, ACT.Sqrt).then_inc(sem("root_ready"), 1)

        NCHUNK = 12 + 10 + 6 + 3 + 2 + 2

        def chunk_source(l, c):
            if c < 12:
                return a["w_mod"][l].rearrange("(k p) n -> p k n", p=P)[:, :, 512 * c:512 * (c + 1)], KT, 512
            c -= 12
            w_in = a["w_in"][l].rearrange("(k p) n -> p k n", p=P)
            if c < 10:
                w = 512 if c < Z_FULL else NZ * P - 512 * Z_FULL
                return w_in[:, :, 512 * c:512 * c + w], KT, w
            c -= 10
            if c < 6:
                return w_in[:, :, GATE_COL + 512 * c:GATE_COL + 512 * (c + 1)], KT, 512
            c -= 6
            if c < 3:
                return a["w_br"][l, c].rearrange("(k p) n -> p k n", p=P), 4, D
            c -= 3
            w = a["w_out"] if c < 2 else a["peer_wq"]
            c %= 2
            return w[l].rearrange("(k p) n -> p k n", p=P)[:, :, 512 * c:512 * (c + 1)], KT, 512

        def slot(c, k, w):
            return ring[:, c % 2, 0:k * w].rearrange("p (k n) -> p k n", k=k)

        def chunk_no(l, c):
            return l * NCHUNK + c

        def chunk_here(eng, l, c):
            n = chunk_no(l, c)
            eng.wait_ge(sem(f"chunk_in{n % 2}"), 16 * (n // 2 + 1))
            _, k, w = chunk_source(l, c)
            return slot(n, k, w)

        def chunk_released(eng, n):
            l, c = divmod(n, NCHUNK)
            if c < 12:
                eng.wait_ge(sem("mod_mm"), 12 * l + c + 1)
            elif c < 22:
                eng.wait_ge(sem("proj"), NZ * l + min(4 * (c - 12) + 4, NZ))
            elif c < 28:
                eng.wait_ge(sem("gate_mm"), 24 * l + 4 * (c - 22) + 4)
            elif c < 31:
                eng.wait_ge(sem("branch_mm"), 8 * (3 * l + c - 28) + 8)
            elif c < 33:
                eng.wait_ge(sem("out_mm"), NT * (2 * l + c - 31) + NT)
            else:
                eng.wait_ge(sem("query_mm"), 4 * (2 * l + c - 33) + 4)

        G = arena[:, 0:2 * QUART * T].rearrange("p (i n) -> p i n", n=T)
        U_AT = 2 * QUART * T
        ublk = [arena[:, U_AT + b * D:U_AT + (b + 1) * D] for b in range(2)]
        vblk = [arena[:, U_AT + (2 + b) * D:U_AT + (3 + b) * D] for b in range(2)]
        ringf = ring[:, :, :].rearrange("p a n -> p (a n)")
        uT = [ringf[:, b * D:(b + 1) * D].rearrange("p (k e) -> p k e", k=KT) for b in range(2)]
        at = 2 * D
        Wg = [ringf[:, at + b * T:at + (b + 1) * T] for b in range(2)]
        ge = ringf[:, at + 2 * T:at + 3 * T]
        chosen_ij = ringf[:, at + 3 * T:at + 4 * T].bitcast(BF16).rearrange("p (a n) -> p a n", a=2)
        chosen_g = ringf[:, at + 4 * T:at + 5 * T]
        at += 5 * T
        gate_parts = ringf[:, at:at + 3 * T // 2].bitcast(BF16).rearrange("p (n k) -> p n k", k=3)
        at += 3 * T // 2
        iota_bf = ringf[:, at:at + P // 2].bitcast(BF16)
        at += P // 2
        hot_i = [ringf[:, at + b * T // 2:at + (b + 1) * T // 2].bitcast(BF16).rearrange("p (n i) -> p n i", i=QUART)
                 for b in range(2)]
        at += T
        n = SETN * P // 2
        E2 = [ringf[:, at + b * n:at + (b + 1) * n].bitcast(BF16).rearrange("p (n j) -> p n j", j=P) for b in range(2)]
        at += 2 * n
        n = 3 * T // 2
        E1 = [ringf[:, at + b * n:at + (b + 1) * n].bitcast(BF16).rearrange("p (n k i) -> p n k i", k=3, i=QUART)
              for b in range(2)]
        assert at + 2 * n <= 2 * RING

        def sp_experts(sp, l):
            base = l * NKEYS

            def load_u(i, b):
                if not isinstance(i, int) or base + i >= 2:
                    sp.wait_ge(sem("u_used"), i + (base - 1))
                sp.dma_start(ublk[b], a["peer_u"][l, bass.ds(i * P, P), :]).then_inc(sem(f"u_in{b}"), 16)

            def load_v(i, b):
                if not isinstance(i, int) or base + i >= 2:
                    sp.wait_ge(sem("v_used"), i + (base - 1))
                sp.dma_start(vblk[b], a["peer_v"][l, bass.ds(i * P, P), :]).then_inc(sem(f"v_in{b}"), 16)

            sp.wait_ge(sem("select_done"), l + 1)
            for b in range(2):
                load_u(b, b)
            for b in range(2):
                load_v(b, b)
            for b in range(2):
                load_u(2 + b, b)
            with sp.Fori(0, NKEYS // 2 - 2) as pair:
                for b in range(2):
                    load_u(pair * 2 + (4 + b), b)
                    load_v(pair * 2 + (2 + b), b)
            for b in range(2):
                load_v(NKEYS - 2 + b, b)

        STAGE = TMP
        crow = area(STAGE, 128)
        prow = area(STAGE + 128, 128)
        bmod = area(STAGE + 256, 6144)

        par_srcs = {
            "rwkv_mu": lambda l: a["rwkv_mu"][l].rearrange("(z p) -> z p", p=P),
            "rwkv_w0": lambda l: a["rwkv_w0"][l].rearrange("d (z p) -> (d z) p", p=P),
            "rwkv_a0": lambda l: a["rwkv_a0"][l].rearrange("d (z p) -> (d z) p", p=P),
            "rwkv_r_k": lambda l: a["rwkv_r_k"][l].rearrange("(z h) n -> z (h n)", h=2),
        }
        for nm in ("rwkv_k_k", "rwkv_k_a", "rwkv_gn_w", "rwkv_gn_b", "ret_gn_w", "ret_gn_b"):
            par_srcs[nm] = lambda l, nm=nm: a[nm][l].rearrange("(z p) -> z p", p=P)

        NB = TMP
        bias = area(NB, 4096, r="p (u k) -> p u k", u=16)
        ckin = area(NB + 4096, 512)
        cvin = area(NB + 4608, 512)
        ckT = area(NB + 5120, 512, r="p (z t) -> p z t", z=4)
        vtok = area(NB + 5632, 1536, r="p (t f) -> p t f", t=3)
        ktok0 = area((NZ + 8) * T, 512)
        Sx = [area(NB + 7168 + b * T, T) for b in range(2)]
        PT = [area(NB + 7936 + b * T, T).rearrange("p (j q) -> p j q", j=3) for b in range(2)]
        reverse = area(NB + 8704, P)
        assert NB + 8704 + P <= 28672

        def ln_rows(pool, l, g, b, which):
            n = 2 * l + which
            if which == 0:
                pool.wait_ge(sem("rw_gate"), l + 1)
            else:
                pool.wait_ge(sem("x_done"), n * NT)
            pool.dma_start(lnp[:, 0, :], a[g][l:l + 1, :].to_broadcast([P, D])).then_inc(sem("ln_in"), 16)
            pool.dma_start(lnp[:, 1, :], a[b][l:l + 1, :].to_broadcast([P, D])).then_inc(sem("ln_in"), 16)

        mrow = area(STAGE + 256 + 6144, 1024, r="p (b n) -> p b n", b=2)
        sil_tmp = area(STAGE + 256 + 6144 + 1024, 32)

        def pe_cond(pe):
            pe.wait_ge(sem("const_in"), 16)
            pe.wait_ge(sem("c_in"), 32)
            nc.tensor.transpose(ps[0][:, 0:16], crow[0:16, :], ident[0:16, 0:16]).then_inc(sem("cond_T"), 1)

        def act_cond(act):
            act.wait_ge(sem("cond_T"), 1)
            nc.scalar.activation(sil_tmp[:, 0:16], ps[0][:, 0:16], ACT.Sigmoid).then_inc(sem("cond_sig"), 1)

        def dve_cond(dve):
            dve.wait_ge(sem("cond_sig"), 1)
            nc.vector.tensor_tensor(silT[:, :].rearrange("p (k s) -> p s k", s=2),
                                    ps[0][:, 0:16].rearrange("p (s k) -> p s k", s=2),
                                    sil_tmp[:, 0:16].rearrange("p (s k) -> p s k", s=2),
                                    ALU.mult).then_inc(sem("cond_sil"), 1)

        def pe_mod(pe, l):
            if l == 0:
                pe.wait_ge(sem("cond_sil"), 1)
            pe.wait_ge(sem("param_in"), 16 * (len(PARAMS) + 2) * (l + 1))
            if l:
                pe.wait_ge(sem("peer_res"), 6 * l)
            nc.tensor.transpose(ps[4][:, 0:NPAR], prow[0:NPAR, :], ident[0:NPAR, 0:NPAR]).then_inc(sem("par_T"), 1)
            def finish(c):
                pe.wait_ge(sem("mod_row"), 12 * l + c + 1)
                if c >= 2:
                    pe.wait_ge(sem("mod_out"), 12 * l + c - 1)
                part = c // 2
                dst = ps[2 + c % 2]
                if part in (2, 5):
                    for s in range(NSEQ):
                        d = dst if s == 0 else ps[5 + c % 2]
                        ins = nc.tensor.matmul(d[:, :], K("ident")[0:2, s:s + 1].to_broadcast([2, P]),
                                               mrow[0:2, c % 2, :], start=True, stop=True)
                else:
                    for j in range(4):
                        ins = nc.tensor.transpose(dst[:, 2 * j:2 * j + 2], mrow[0:2, c % 2, P * j:P * (j + 1)],
                                                  ident[0:2, 0:2])
                ins.then_inc(sem("mod_spread"), 1)
            for c in range(12):
                w = chunk_here(pe, l, c)
                if c >= 2:
                    pe.wait_ge(sem("mod_row"), 12 * l + c - 1)
                for k in range(KT):
                    ins = nc.tensor.matmul(ps[c % 2][0:2, :], silT[:, 2 * k:2 * k + 2], w[:, k, :],
                                           start=(k == 0), stop=(k == KT - 1))
                ins.then_inc(sem("mod_mm"), 1)
                if c:
                    finish(c - 1)
            finish(11)

        def dve_mod(dve, l):
            dve.wait_ge(sem("param_in"), 16 * (len(PARAMS) + 2) * (l + 1))
            dve.wait_ge(sem("par_T"), l + 1)
            nc.vector.tensor_copy(par[:, :], ps[4][:, 0:NPAR]).then_inc(sem("par_ready"), 1)
            for c in range(12):
                dve.wait_ge(sem("mod_mm"), 12 * l + c + 1)
                if c >= 2:
                    dve.wait_ge(sem("mod_spread"), 12 * l + c - 1)
                nc.vector.tensor_tensor(mrow[0:2, c % 2, :], ps[c % 2][0:2, :], bmod[0:2, 512 * c:512 * (c + 1)],
                                        ALU.add).then_inc(sem("mod_row"), 1)
                if c:
                    dve_mod_out(dve, l, c - 1)
            dve_mod_out(dve, l, 11)

        def dve_mod_out(dve, l, c):
            dve.wait_ge(sem("mod_spread"), 12 * l + c + 1)
            part = c // 2
            if part in (2, 5):
                w = 0 if part == 2 else 1
                cols = slice(512 * (c % 2), 512 * (c % 2) + 512)
                nc.vector.tensor_copy(gate[:, w, 0, cols], ps[2 + c % 2][:, :])
                nc.vector.tensor_copy(gate[:, w, 1, cols], ps[5 + c % 2][:, :]).then_inc(sem("mod_out"), 1)
            else:
                j = (0, 1, None, 2, 3)[part]
                nc.vector.tensor_scalar(modT[:, 8 * j + 4 * (c % 2):8 * j + 4 * (c % 2) + 4, :],
                                        ps[2 + c % 2][:, 0:8].rearrange("p (z s) -> p z s", s=2),
                                        1.0 if j % 2 else 0.0, None, ALU.add).then_inc(sem("mod_out"), 1)

        XN = TMP

        def xnorm(t):
            return area(XN + D * (t % 2), D)

        def dve_layer_norm(dve, link, dst, src):
            for i in range(2):
                nc.vector.bn_stats(stat[:, 6 * i:6 * i + 6], src[:, 512 * i:512 * (i + 1)]).then_inc(sem("dve_chain"), 1)
                chain["dve"] += 1
            dve.wait_ge(sem("dve_chain"), chain["dve"])
            rsqrt(dve, link, nc.vector.bn_aggr(stat[:, 12:14], stat[:, 0:12]), stat[:, 13:14], EPS, ALU.add)
            return nc.vector.tensor_scalar(dst, src, stat[:, 12:13], stat[:, 13:14], ALU.subtract, ALU.mult)

        def act_norm_roots(act):
            for t in range(NT):
                act_root(act, stat[:, 13:14])

        def dve_norm(dve, link, n):
            if n == 0:
                dve.wait_ge(sem("x_in"), 32)
            if n % 2 == 0:
                dve.wait_ge(sem("mod_out"), 12 * (n // 2 + 1))
            for t in range(NT):
                if t == 2:
                    dve.wait_ge(sem("norm_T"), 6 * n + 2)
                dve_layer_norm(dve, link, xnorm(t), X[:, t, :]).then_inc(sem("normed"), 1)
                dve.wait_ge(sem("normed"), NT * n + t + 1)

        def pe_norm(pe, n):
            for t in range(NT):
                pe.wait_ge(sem("normed"), NT * n + t + 1)
                for hh in range(2):
                    q = 2 * t + hh
                    if q >= 4:
                        pe.wait_ge(sem("h_ready"), 6 * n + q - 3)
                    for k in range(4):
                        ins = nc.tensor.transpose(ps[q % 4][:, P * k:P * (k + 1)],
                                                  xnorm(t)[:, P * (4 * hh + k):P * (4 * hh + k + 1)], ident)
                    ins.then_inc(sem("norm_T"), 1)

        def act_norm(act, n):
            act_norm_roots(act)
            act.wait_ge(sem("mod_out"), 12 * (n // 2 + 1))
            if n % 2:
                act.wait_ge(sem("gate_mm"), 24 * (n // 2 + 1))
            elif n:
                act.wait_ge(sem("hidden"), NKEYS * (n // 2))
            for t in range(NT):
                s = min(t, 1)
                for hh in range(2):
                    q = 2 * t + hh
                    act.wait_ge(sem("norm_T"), 6 * n + q + 1)
                    for k in range(4):
                        kk = 4 * hh + k
                        j = 16 * (n % 2)
                        ins = nc.scalar.activation(hT[:, kk, P * t:P * (t + 1)], ps[q % 4][:, P * k:P * (k + 1)],
                                                   ACT.Identity, bias=modT[:, j + kk, s:s + 1],
                                                   scale=modT[:, j + 8 + kk, s:s + 1])
                    ins.then_inc(sem("h_ready"), 1)

        def out_wait(eng, q, act_sem, dve_sem):
            eng.wait_ge(sem(act_sem if q % 2 == 0 else dve_sem), q // 2 + 1)

        def pe_proj(pe, l):
            pe.wait_ge(sem("h_ready"), 6 * (2 * l + 1))
            if l == 0:
                pe.wait_ge(sem("mod_out"), 12)
            for z in range(NZ):
                c, j = divmod(z, 4)
                if j == 0:
                    w = chunk_here(pe, l, 12 + c)
                q = NZ * l + z
                if z in BIAS_AT:
                    pe_bias(pe, l, BIAS_AT.index(z))
                if z >= 2:
                    out_wait(pe, q - 2, "z_act", "z_dve")
                for k in range(KT):
                    ins = nc.tensor.matmul(ps[6 + z % 2][:, 0:T], w[:, k, P * j:P * (j + 1)], hT[:, k, :],
                                           start=(k == 0), stop=(k == KT - 1))
                ins.then_inc(sem("proj"), 1)
                if z == NA_TILES - 1:
                    pe_na_start(pe, l)
                elif z >= NA_TILES:
                    pe_na_step(pe, l, z - NA_TILES)

        def act_proj(act, l):
            for z in range(NZ):
                q = NZ * l + z
                if q % 2 == 0:
                    act.wait_ge(sem("proj"), q + 1)
                    nc.scalar.activation(ZT[:, z, :], ps[6 + z % 2][:, 0:T], ACT.Copy).then_inc(sem("z_act"), 1)
                if z == NA_TILES - 1:
                    act_na_start(act, l)
                elif z >= NA_TILES:
                    act_na_step(act, l, z - NA_TILES)
            act_na_out(act, l, 3)

        def dve_proj(dve, link, l):
            for z in range(NZ):
                q = NZ * l + z
                if q % 2:
                    dve.wait_ge(sem("proj"), q + 1)
                    nc.vector.tensor_copy(ZT[:, z, :], ps[6 + z % 2][:, 0:T]).then_inc(sem("z_dve"), 1)
                if z in BIAS_AT:
                    dve_bias(dve, l, BIAS_AT.index(z))
                if z >= NA_TILES:
                    dve_na_step(dve, link, l, z - NA_TILES)
                if z > R_RW:
                    dve_shift(dve, link, l, z - 1)
            dve_shift(dve, link, l, NZ - 1)

        NA_TILES = 12
        BIAS_AT = (9, 11)

        def pe_bias(pe, l, half):
            pe.wait_ge(sem("bias_in"), 16 * 33 * (l + 1))
            if half:
                pe.wait_ge(sem("bias_ready"), 2 * l + 1)
            for i in range(4):
                at = NB + 512 * (4 * half + i)
                ins = nc.tensor.matmul(ps[i][:, :], reverse, arena[:, at:at + 512], start=True, stop=True)
            ins.then_inc(sem("bias_turned"), 1)

        def dve_bias(dve, l, half):
            dve.wait_ge(sem("bias_turned"), 2 * l + half + 1)
            for i in range(4):
                at = NB + 512 * (4 * half + i)
                ins = nc.vector.tensor_tensor(arena[:, at:at + 512].rearrange("p (a b) -> p a b", b=GRID_W),
                                              ps[i][:, :].rearrange("p (a b) -> p a b", b=GRID_W),
                                              K("window").rearrange("p (o b) -> p o b", o=1).to_broadcast([P, 8, GRID_W]),
                                              ALU.add)
            ins.then_inc(sem("bias_ready"), 1)

        def z_ready(eng, l, tiles=NZ):
            n = NZ * l + tiles
            eng.wait_ge(sem("z_act"), (n + 1) // 2)
            eng.wait_ge(sem("z_dve"), n // 2)

        NU = HN * NT

        def width(n):
            return P if n % NT == 0 else T

        def pool_na(pool, l):
            pool.wait_ge(sem("mod_out"), 12 * (l + 1))
            pool.wait_ge(sem("norm_T"), 6 * (2 * l + 1))
            pool.dma_start(ckin.rearrange("p (h d) -> p h d", h=HN),
                           a["cache_na_k"][0, l].rearrange("h t d -> t h d")).then_inc(sem("na_in"), 16)
            pool.dma_start(cvin.rearrange("p (h d) -> p h d", h=HN),
                           a["cache_na_v"][0, l].rearrange("h t d -> t h d")).then_inc(sem("na_in"), 16)
            pool.dma_start(reverse, a["consts"][:, WHERE["reverse"]]).then_inc(sem("bias_in"), 16)
            rpb = a["na_rpb"]
            for h in range(HN):
                for tq in range(2):
                    for r in range(2):
                        at = ((l * HN + h) * 15 + 7 - (2 * tq + r)) * 31 + 15 - 63
                        pool.dma_start(bias[64 * r:64 * r + 64, 2 * h + tq, :].rearrange("p (a b) -> p a b", a=4),
                                       bass.AP(rpb.tensor, at, [[1, 64], [31, 4], [1, 64]])).then_inc(sem("bias_in"), 16)

        def pool_na_out(pool, l):
            pool.wait_ge(sem("na_tok"), 5 * (l + 1))
            pool.dma_start(new_na_k[0, l].rearrange("h t d -> t h d"),
                           ktok0.rearrange("p (h d) -> p h d", h=HN)).then_inc(sem("stored"), 16)
            pool.dma_start(new_na_v[0, l].rearrange("h t d -> t h d"),
                           vtok[:, 0, :].rearrange("p (h d) -> p h d", h=HN)).then_inc(sem("stored"), 16)

        def pe_na_start(pe, l):
            z_ready(pe, l, NA_TILES)
            pe.wait_ge(sem("bias_ready"), 2 * (l + 1))
            pe.wait_ge(sem("na_in"), 32 * (l + 1))
            for z in range(4):
                ins = nc.tensor.transpose(ps[0][:, P * z:P * (z + 1)], ckin[:, P * z:P * (z + 1)], ident)
            ins.then_inc(sem("na_T"), 1)
            for t in range(NT):
                for z in range(4):
                    ins = nc.tensor.transpose(ps[1 + t][:, P * z:P * (z + 1)], ZT[:, V_NA + z, P * t:P * (t + 1)], ident)
                ins.then_inc(sem("na_T"), 1)
            for z in range(4):
                ins = nc.tensor.transpose(ps[4][:, P * z:P * (z + 1)], ZT[:, K_NA + z, 0:P], ident)
            ins.then_inc(sem("na_T"), 1)

        def pe_na_step(pe, l, n):
            if n == 0:
                pe.wait_ge(sem("na_tok"), 5 * (l + 1))
            if n < NU:
                h, t = divmod(n, NT)
                rows = slice(64 * (h % 2), 64 * (h % 2) + 64)
                if n:
                    pe.wait_ge(sem("na_biased"), NU * l + n)
                bank = ps[h % 2]
                q = ZT[rows, Q_NA + h // 2, P * t:P * (t + 1)]
                if t == 0:
                    ins = nc.tensor.matmul(bank[:, 0:P], q, ZT[rows, K_NA + h // 2, 0:P], start=True, stop=True)
                else:
                    nc.tensor.matmul(bank[:, 0:256], q, ZT[rows, K_NA + h // 2, P:T], start=True, stop=True)
                    ins = nc.tensor.matmul(bank[:, 256:T], q, ckT[rows, h // 2, :], start=True, stop=True)
                ins.then_inc(sem("na_scores"), 1)
            m = n - 2
            if 0 <= m < NU:
                pe.wait_ge(sem("na_prob"), NU * l + m + 1)
                if m >= 2:
                    pe.wait_ge(sem("na_PT"), NU * l + m - 1)
                for j in range(width(m) // P):
                    ins = nc.tensor.transpose(ps[(2, 5)[m % 2]][:, P * j:P * (j + 1)], Sx[m % 2][:, P * j:P * (j + 1)],
                                              ident)
                ins.then_inc(sem("na_turned"), 1)
            m = n - 3
            if m >= 0:
                h, t = divmod(m, NT)
                pe.wait_ge(sem("na_PT"), NU * l + m + 1)
                if m % 6 == 0 and m >= 12:
                    pe.wait_ge(sem("na_out"), 4 * l + m // 6 - 1)
                dst = ps[3 + (h // 2) % 2][64 * (h % 2):64 * (h % 2) + 64, P * t:P * (t + 1)]
                cols = slice(64 * h, 64 * h + 64)
                if t == 0:
                    ins = nc.tensor.matmul(dst, vtok[:, 0, cols], PT[m % 2][:, 0, :], start=True, stop=True)
                else:
                    for j, v in enumerate((vtok[:, 1, cols], vtok[:, 2, cols], cvin[:, cols])):
                        ins = nc.tensor.matmul(dst, v, PT[m % 2][:, j, :], start=(j == 0), stop=(j == 2))
                ins.then_inc(sem("na_values"), 1)

        def act_na_start(act, l):
            for i, dst in enumerate([ckT.rearrange("p z t -> p (z t)"), vtok[:, 0, :], vtok[:, 1, :], vtok[:, 2, :], ktok0]):
                act.wait_ge(sem("na_T"), 5 * l + i + 1)
                nc.scalar.activation(dst, ps[i][:, :], ACT.Copy).then_inc(sem("na_tok"), 1)

        def act_na_step(act, l, n):
            if n < NU:
                act.wait_ge(sem("na_max"), NU * l + n + 1)
                s = Sx[n % 2][:, 0:width(n)]
                nc.scalar.activation(s, s, ACT.Exp, bias=small[:, n:n + 1], accum_out=small[:, 24 + n:25 + n])\
                    .then_inc(sem("na_exp"), 1)
            m = n - 2
            if 0 <= m < NU:
                act.wait_ge(sem("na_turned"), NU * l + m + 1)
                if m >= 2:
                    act.wait_ge(sem("na_values"), NU * l + m - 1)
                w = width(m)
                nc.scalar.activation(PT[m % 2].rearrange("p j q -> p (j q)")[:, 0:w], ps[(2, 5)[m % 2]][:, 0:w],
                                     ACT.Copy).then_inc(sem("na_PT"), 1)
            if n >= 9 and (n - 9) % 6 == 0:
                act_na_out(act, l, (n - 9) // 6)

        def act_na_out(act, l, z):
            act.wait_ge(sem("na_values"), NU * l + 6 * z + 6)
            nc.scalar.activation(oT[:, 0, z, :], ps[3 + z % 2][:, 0:T], ACT.Copy).then_inc(sem("na_out"), 1)

        def dve_na_step(dve, link, l, n):
            if n == 0:
                dve.wait_ge(sem("bias_ready"), 2 * (l + 1))
            if n < NU:
                h, t = divmod(n, NT)
                dve.wait_ge(sem("na_scores"), NU * l + n + 1)
                if n >= 2:
                    dve.wait_ge(sem("na_turned"), NU * l + n - 1)
                bank = ps[h % 2]
                s = Sx[n % 2]
                if t:
                    nc.vector.scalar_tensor_tensor(s[:, 0:256], bank[:, 0:256], DH ** -0.5, bias[:, 2 * h + t - 1, :],
                                                   ALU.mult, ALU.add)
                    nc.vector.tensor_scalar(s[:, 256:T], bank[:, 256:T], DH ** -0.5, None, ALU.mult)\
                        .then_inc(sem("na_biased"), 1)
                else:
                    nc.vector.tensor_scalar(s[:, 0:P], bank[:, 0:P], DH ** -0.5, None, ALU.mult)\
                        .then_inc(sem("na_biased"), 1)
                dve.wait_ge(sem("na_biased"), NU * l + n + 1)
                nc.vector.tensor_reduce(small[:, n:n + 1], s[:, 0:width(n)], X_AXIS, ALU.max, negate=True)\
                    .then_inc(sem("na_max"), 1)
            m = n - 1
            if 0 <= m < NU:
                dve.wait_ge(sem("na_exp"), NU * l + m + 1)
                link(nc.vector.reciprocal(small[:, 48 + m:49 + m], small[:, 24 + m:25 + m]))
                s = Sx[m % 2][:, 0:width(m)]
                nc.vector.tensor_scalar(s, s, small[:, 48 + m:49 + m], None, ALU.mult).then_inc(sem("na_prob"), 1)

        RA = TMP
        r_vtok = area(RA, 1536, r="p (t f) -> p t f", t=3)
        r_mask = area(RA + 1536, 2048, r="p (h k i) -> p h k i", h=4, k=4)
        r_qdec = area(RA + 3584, 1024, r="p (d z i) -> p d z i", d=2, z=2)
        r_s0 = area(RA + 4608, 512, r="p (z d v) -> p z d v", z=2, d=2)
        r_ktok = area(RA + 5120, 256)
        r_kleft = area(RA + 5376, 512, r="p (d h k) -> p d h k", d=2, h=4)
        r_on = area(RA + 5888, 1536, r="p (t f) -> p t f", t=3)
        r_sig = area(RA + 7424, 1536)
        r_att = arena[:, 0:2560]
        r_tmp = arena[:, 2560:2560 + 1536]
        r_sout = arena[:, 0:1024]
        nlg, ncol = decl[:, 0:8], decl[:, 8:12]

        def pool_ret(pool, l):
            pool.wait_ge(sem("na_out"), 4 * (l + 1))
            pool.wait_ge(sem("stored"), 16 * (7 * l + 2))
            st = a["state_ret"][0, l]
            for d in range(2):
                for z in range(2):
                    pool.dma_start(r_s0[:, z, d, :], st[d, 2 * z:2 * z + 2].rearrange("h k v -> (h k) v"))\
                        .then_inc(sem("ret_in"), 16)

        def pool_decays(pool, l):
            lg = a["ret_decay_logit"]
            pool.dma_start(nlg, bass.AP(lg.tensor, l * 8, [[0, P], [1, 8]])).then_inc(sem("decay_in"), 16)
            for q in range(2):
                for d in range(2):
                    for z in range(2):
                        pool.dma_start(ncol[64 * q:64 * q + 64, 2 * d + z:2 * d + z + 1],
                                       bass.AP(lg.tensor, l * 8 + 4 * d + 2 * z + q, [[0, 64], [1, 1]]))\
                            .then_inc(sem("decay_in"), 16)

        def pool_ret_out(pool, l):
            pool.wait_ge(sem("ret_states"), 2 * (l + 1))
            pool.dma_start(new_state_ret[0, l].rearrange("d h k v -> k (d h) v"),
                           r_sout[0:64, :].rearrange("p (g v) -> p g v", g=8)).then_inc(sem("stored"), 16)

        def pe_ret(pe, l):
            z_ready(pe, l)
            pe.wait_ge(sem("na_out"), 4 * (l + 1))
            for i in range(4):
                ins = nc.tensor.matmul(ps[i][:, 0:256], K("swap"), ZT[:, Q_RT + i, P:T], start=True, stop=True)
            ins.then_inc(sem("ret_swap"), 1)
            for t in range(NT):
                for z in range(4):
                    ins = nc.tensor.transpose(ps[4 + t][:, P * z:P * (z + 1)], ZT[:, V_RT + z, P * t:P * (t + 1)], ident)
                ins.then_inc(sem("ret_T"), 1)
            pe.wait_ge(sem("ret_rope"), l + 1)
            for z in range(2):
                ins = nc.tensor.transpose(ps[7][:, P * z:P * (z + 1)], ZT[:, K_RT + z, 0:P], ident)
            ins.then_inc(sem("ret_T"), 1)
            pe.wait_ge(sem("ret_tok"), 4 * l + 2)
            for h in range(RH):
                rows = slice(64 * (h % 2), 64 * (h % 2) + 64)
                q, k = ZT[rows, Q_RT + h // 2, :], ZT[rows, K_RT + h // 2, :]
                for j in range(2):
                    nc.tensor.matmul(ps[h][:, 256 * j:256 * (j + 1)], k[:, P * (1 + j):P * (2 + j)], q[:, P:T],
                                     start=True, stop=True)
                ins = nc.tensor.matmul(ps[4 + h % 2][:, P * (h // 2):P * (h // 2) + P], k[:, 0:P], q[:, 0:P],
                                       start=True, stop=True)
            ins.then_inc(sem("ret_scores"), 1)
            pe.wait_ge(sem("ret_kleft"), l + 1)
            pe.wait_ge(sem("ret_tok"), 4 * l + 4)
            pe.wait_ge(sem("ret_att"), l + 1)
            pe.wait_ge(sem("ret_qdec"), l + 1)
            pe.wait_ge(sem("ret_in"), 16 * 4 * (l + 1))
            for t in range(NT):
                bank = ps[(6, 7, 0)[t]]
                for h in range(RH):
                    rows = slice(64 * (h % 2), 64 * (h % 2) + 64)
                    dst = bank[:, P * h:P * (h + 1)]
                    v = slice(P * h, P * (h + 1))
                    if t == 0:
                        ins = nc.tensor.matmul(dst, r_att[:, 2048 + P * h:2048 + P * (h + 1)], r_vtok[:, 0, v],
                                               start=True, stop=True)
                        continue
                    i = P * (t - 1)
                    for j in range(2):
                        at = 512 * h + 256 * j + i
                        nc.tensor.matmul(dst, r_att[:, at:at + P], r_vtok[:, 1 + j, v], start=(j == 0), stop=False)
                    if h:
                        pe.wait_ge(sem("ret_head"), 6 * l + 3 * (t - 1) + h)
                    for d in range(2):
                        ins = nc.tensor.matmul(dst, r_qdec[rows, d, h // 2, i:i + P], r_s0[rows, h // 2, d, :],
                                               start=False, stop=(d == 1))
                    if h < RH - 1:
                        ins.then_inc(sem("ret_head"), 1)
                ins.then_inc(sem("ret_o"), 1)
            for d in range(2):
                for h in range(RH):
                    ins = nc.tensor.matmul(ps[4 + d][0:64, P * h:P * (h + 1)], r_kleft[:, d, h, :],
                                           r_vtok[:, 0, P * h:P * (h + 1)], start=True, stop=True)
                ins.then_inc(sem("ret_S"), 1)
            for t in range(NT):
                pe.wait_ge(sem("ret_normed"), NT * l + t + 1)
                for h in range(RH):
                    ins = nc.tensor.transpose(ps[1 + t][:, P * h:P * (h + 1)], r_on[:, t, P * h:P * (h + 1)], ident)
                ins.then_inc(sem("ret_oT"), 1)

        def act_ret(act, link, l):
            act.wait_ge(sem("decay_in"), 16 * (1 + 8) * (l + 1))
            act.wait_ge(sem("stored"), 16 * (7 * l + 2))
            link(nc.scalar.activation(decl[:, 12:24], decl[:, 0:12], ACT.Exp, scale=-1.0))
            nc.scalar.activation(decl[:, 24:36], decl[:, 12:24], ACT.Ln, bias=1.0).then_inc(sem("ret_ln"), 1)
            for t in range(2):
                act.wait_ge(sem("ret_T"), 4 * l + t + 1)
                nc.scalar.activation(r_vtok[:, t, :], ps[4 + t][:, :], ACT.Copy).then_inc(sem("ret_tok"), 1)
            act.wait_ge(sem("ret_T"), 4 * l + 4)
            nc.scalar.activation(r_vtok[:, 2, :], ps[6][:, :], ACT.Copy).then_inc(sem("ret_tok"), 1)
            nc.scalar.activation(r_ktok, ps[7][:, 0:256], ACT.Copy).then_inc(sem("ret_tok"), 1)
            act.wait_ge(sem("ret_lg"), l + 1)
            for h in range(RH):
                f, b = decl[:, 36 + h:37 + h], decl[:, 40 + h:41 + h]
                nc.scalar.activation(r_mask[:, h, 0, :], K("dist"), ACT.Exp, scale=f)
                nc.scalar.activation(r_mask[:, h, 3, :], K("dist"), ACT.Exp, scale=b)
                nc.scalar.activation(r_mask[:, h, 1, :], K("far_f"), ACT.Exp, scale=f)
                ins = nc.scalar.activation(r_mask[:, h, 2, :], K("far_b"), ACT.Exp, scale=b)
            ins.then_inc(sem("ret_exp"), 1)
            for d in range(2):
                for z in range(2):
                    n = 44 + 2 * d + z
                    ins = nc.scalar.activation(r_qdec[:, d, z, :], K("age_b" if d else "age_f"), ACT.Exp,
                                               scale=decl[:, n:n + 1])
            ins.then_inc(sem("ret_exp"), 1)
            for d in range(2):
                for h in range(RH):
                    n = 4 * d + h
                    ins = nc.scalar.activation(small[:, n:n + 1], K("left")[:, d:d + 1], ACT.Exp,
                                               scale=decl[:, 36 + n:37 + n])
            ins.then_inc(sem("ret_exp"), 1)
            nc.scalar.activation(r_sig, ZT[:, G_RT:G_RT + 4, :].rearrange("p z t -> p (z t)"), ACT.Sigmoid)\
                .then_inc(sem("ret_sig"), 1)
            for t in range(NT):
                act_root(act, stat[:, 32:40].rearrange("p (h s) -> p h s", s=2)[:, :, 1])
            for d in range(2):
                act.wait_ge(sem("ret_S"), 2 * l + d + 1)
                if d == 0:
                    act.wait_ge(sem("ret_o"), NT * (l + 1))
                nc.scalar.activation(r_sout[0:64, 512 * d:512 * (d + 1)], ps[4 + d][0:64, :], ACT.Copy)\
                    .then_inc(sem("ret_states"), 1)
            for t in range(NT):
                act.wait_ge(sem("ret_oT"), NT * l + t + 1)
                for h in range(RH):
                    w, b = PAR["ret_gn_w"] + h, PAR["ret_gn_b"] + h
                    ins = nc.scalar.activation(oT[:, 1, h, P * t:P * (t + 1)], ps[1 + t][:, P * h:P * (h + 1)],
                                               ACT.Identity, bias=par[:, b:b + 1], scale=par[:, w:w + 1])
                ins.then_inc(sem("ret_affine"), 1)

        def dve_ret(dve, link, l):
            dve.wait_ge(sem("na_out"), 4 * (l + 1))
            dve.wait_ge(sem("stored"), 16 * (7 * l + 2))
            qk = ZT[:, Q_RT:Q_RT + 4, P:T]
            rt = r_tmp[:, 0:1024].rearrange("p (z t) -> p z t", z=4)
            def wide(name):
                return K(name).rearrange("p (o t) -> p o t", o=1).to_broadcast([P, 4, 256])
            link(nc.vector.tensor_tensor(rt, qk, wide("cos"), ALU.mult))
            dve.wait_ge(sem("ret_swap"), l + 1)
            for i in range(4):
                ins = nc.vector.tensor_tensor(qk[:, i, :], ps[i][:, 0:256], K("sin"), ALU.mult)
            link(ins)
            link(nc.vector.tensor_tensor(qk, qk, rt, ALU.add))
            kk = ZT[:, K_RT:K_RT + 2, :]
            nc.vector.tensor_scalar(kk, kk, DH ** -0.5, None, ALU.mult).then_inc(sem("ret_rope"), 1)
            dve.wait_ge(sem("ret_ln"), l + 1)
            nc.vector.tensor_scalar(decl[:, 36:48], decl[:, 24:36], -1.0, None, ALU.mult).then_inc(sem("ret_lg"), 1)
            dve.wait_ge(sem("ret_exp"), 3 * l + 1)
            def tri(name):
                return K(name).rearrange("p (o i) -> p o i", o=1).to_broadcast([P, 4, P])
            nc.vector.tensor_tensor(r_mask[:, :, 0, :], r_mask[:, :, 0, :], tri("tri_f"), ALU.mult)
            link(nc.vector.tensor_tensor(r_mask[:, :, 3, :], r_mask[:, :, 3, :], tri("tri_b"), ALU.mult))
            link(nc.vector.tensor_tensor(r_mask[:, :, 0, :], r_mask[:, :, 0, :], r_mask[:, :, 3, :], ALU.add))
            link(nc.vector.tensor_copy(r_mask[:, :, 3, :], r_mask[:, :, 0, :]))
            dve.wait_ge(sem("ret_exp"), 3 * l + 2)
            q = ZT[:, Q_RT:Q_RT + 2, P:T]
            nc.vector.tensor_tensor(r_qdec[:, 0, :, :], r_qdec[:, 0, :, :], q, ALU.mult)
            nc.vector.tensor_tensor(r_qdec[:, 1, :, :], r_qdec[:, 1, :, :], q, ALU.mult).then_inc(sem("ret_qdec"), 1)
            dve.wait_ge(sem("ret_exp"), 3 * l + 3)
            dve.wait_ge(sem("ret_tok"), 4 * (l + 1))
            for d in range(2):
                for h in range(RH):
                    n = 4 * d + h
                    ins = nc.vector.tensor_scalar(r_kleft[:, d, h, :], r_ktok[:, 64 * h:64 * h + 64], small[:, n:n + 1],
                                                  None, ALU.mult)
            ins.then_inc(sem("ret_kleft"), 1)
            dve.wait_ge(sem("ret_scores"), l + 1)
            for h in range(RH):
                nc.vector.tensor_tensor(r_att[:, 512 * h:512 * (h + 1)], ps[h][:, :],
                                        r_mask[:, h, :, :].rearrange("p k i -> p (k i)"), ALU.mult)
                ins = nc.vector.tensor_tensor(r_att[:, 2048 + P * h:2048 + P * (h + 1)],
                                              ps[4 + h % 2][:, P * (h // 2):P * (h // 2) + P], r_mask[:, h, 0, :], ALU.mult)
            ins.then_inc(sem("ret_att"), 1)
            dve_keys(dve, link, l)
            dve.wait_ge(sem("ret_sig"), l + 1)
            g = ZT[:, G_RT:G_RT + 4, :].rearrange("p z t -> p (z t)")
            link(nc.vector.tensor_tensor(r_sig, r_sig, g, ALU.mult))
            for t in range(NT):
                dve.wait_ge(sem("ret_o"), NT * l + t + 1)
                bank = ps[(6, 7, 0)[t]]
                for h in range(RH):
                    ins = nc.vector.bn_stats(stat[:, 6 * h:6 * h + 6], bank[:, P * h:P * (h + 1)])
                link(ins)
                for h in range(RH):
                    ins = nc.vector.bn_aggr(stat[:, 32 + 2 * h:34 + 2 * h], stat[:, 6 * h:6 * h + 6])
                rsqrt(dve, link, ins, stat[:, 32:40].rearrange("p (h s) -> p h s", s=2)[:, :, 1], EPS, ALU.add)
                for h in range(RH):
                    ins = nc.vector.tensor_scalar(r_on[:, t, P * h:P * (h + 1)], bank[:, P * h:P * (h + 1)],
                                                  stat[:, 32 + 2 * h:33 + 2 * h], stat[:, 33 + 2 * h:34 + 2 * h],
                                                  ALU.subtract, ALU.mult)
                ins.then_inc(sem("ret_normed"), 1)
            dve.wait_ge(sem("ret_affine"), NT * (l + 1))
            o = oT[:, 1, :, :].rearrange("p z t -> p (z t)")
            nc.vector.tensor_tensor(o, o, r_sig, ALU.mult).then_inc(sem("ret_done"), 1)

        ZW = T * 4

        def tiles4(at):
            return arena[:, at:at + ZW].rearrange("p (z t) -> p z t", t=T)

        w_QR = [arena[:, at:at + 2 * ZW].rearrange("p (x z t) -> p x z t", x=2, t=T) for at in (0, TMP)]
        w_K = [tiles4(2 * ZW), tiles4(TMP + 2 * ZW)]
        w_B = [tiles4(3 * ZW), tiles4(TMP + 3 * ZW)]
        w_kk = tiles4(4 * ZW)
        w_LW = tiles4(5 * ZW)
        w_L = tiles4(TMP + 4 * ZW)
        w_E = oT[:, 2, :, :]
        shift = lnp[:, 1, 512:512 + T]
        r_, k_, v_ = ZT[:, R_RW:R_RW + 4, :], ZT[:, K_RW:K_RW + 4, :], ZT[:, V_RW:V_RW + 4, :]
        w_up, a_up, g_up = lnp[:, 0, 0:512], lnp[:, 0, 512:1024], lnp[:, 1, 0:512]
        w_ends = small[:, 0:48].rearrange("p (d z c) -> p d z c", d=2, z=4)
        w_tot = small[:, 48:72]

        def unit(i):
            at = 4 * ZW + 512 * i if i < 12 else (TMP + 5 * ZW + 512 * (i - 12) if i < 14 else W_RW * T)
            return arena[:, at:at + 512]
        u_A, u_M, u_G, u_RK, u_RB, u_X, u_Y, u_T, u_K, u_B, u_V, u_M1, u_S, u_in, u_out = (unit(i) for i in range(15))
        u_Ms = (u_M, u_M1)
        w_Oc = arena[:, TMP + 4 * ZW:TMP + 5 * ZW].rearrange("p (c x) -> p c x", c=NCH)
        w_Og = arena[:, TMP + 4 * ZW:TMP + 5 * ZW].rearrange("p (g v) -> p g v", v=64)
        w_sq = arena[:, 4 * ZW + 1024:4 * ZW + 2560].rearrange("p (g v) -> p g v", v=64)
        w_N = tiles4(4 * ZW + 2560)

        def flat(v):
            return v.rearrange("p z t -> p (z t)")

        def pcol(name, z):
            return par[:, PAR[name] + z:PAR[name] + z + 1]

        def both(name, d=None):
            m = K(name)[:, 64 * d:64 * d + 64].rearrange("p (o t) -> p o t", o=1)
            return m.to_broadcast([P, 4, 64])

        STEPS = [(0, 1), (1, 0), (2, 5), (3, 4), (4, 3), (5, 2)]
        NS = len(STEPS)
        V_AT = [(u_V, False), (u_V, True), (u_V, False), (u_in, False), (u_in, True), (u_V, True)]

        def dve_shift(dve, link, l, z):
            q = NZ * l + z
            dve.wait_ge(sem("z_act" if q % 2 == 0 else "z_dve"), q // 2 + 1)
            v = ZT[:, z, :]
            nc.vector.tensor_tensor(shift[:, 1:T - 1], v[:, 0:T - 2], v[:, 2:T], ALU.add).then_inc(sem("rw_sides"), 1)
            dve.wait_ge(sem("rw_sides"), 15 * l + z - R_RW + 1)
            for at, of in ((0, 1), (P - 1, P - 2), (P, P + 1), (T - 1, T - 2)):
                ins = nc.vector.tensor_copy(shift[:, at:at + 1], v[:, of:of + 1])
            link(ins)
            link(nc.vector.scalar_tensor_tensor(shift, shift, 0.5, v, ALU.mult, ALU.subtract))
            nc.vector.scalar_tensor_tensor(v, shift, pcol("rwkv_mu", z - R_RW), v, ALU.mult, ALU.add)\
                .then_inc(sem("rw_shift"), 1)
            dve.wait_ge(sem("rw_shift"), 15 * l + z - R_RW + 1)

        def pool_rwkv(pool, l):
            if l:
                pool.wait_ge(sem("x_done"), 2 * l * NT)
            pool.dma_start(w_up, a["rwkv_w_up"][l].rearrange("d r n -> (d r) n")).then_inc(sem("rw_in"), 16)
            pool.dma_start(a_up, a["rwkv_a_up"][l].rearrange("d r n -> (d r) n")).then_inc(sem("rw_in"), 16)
            pool.dma_start(g_up, a["rwkv_g_up"][l]).then_inc(sem("rw_in"), 16)
            pool.wait_ge(sem("ret_done"), l + 1)
            for d in range(2):
                st = a["state_rwkv"][0, l, d].rearrange("(z q) v k -> q v z k", q=2)
                for q in range(2):
                    pool.dma_start(u_in[64 * q:64 * q + 64, 256 * d:256 * d + 256].rearrange("p (z k) -> p z k", z=4),
                                   st[q]).then_inc(sem("rw_state_in"), 16)

        def pool_rwkv_out(pool, l):
            pool.wait_ge(sem("rw_out"), l + 1)
            for d in range(2):
                st = new_state_rwkv[0, l, d].rearrange("(z q) v k -> q v z k", q=2)
                for q in range(2):
                    pool.dma_start(st[q], u_out[64 * q:64 * q + 64, 256 * d:256 * d + 256]
                                   .rearrange("p (z k) -> p z k", z=4)).then_inc(sem("stored"), 16)

        def level(m, j, d):
            return 2 * (LEVELS * m + j) + d + 1

        def later(m, j, d):
            return 2 * ((LEVELS - 1) * m + j - 1) + d + 1

        def heads(fn, dirs=(0, 1)):
            for d in dirs:
                for z in range(4):
                    for q in range(2):
                        rows = slice(64 * q, 64 * q + 64)
                        ins = fn(d, z, rows, slice(256 * d + 64 * z, 256 * d + 64 * z + 64))
            return ins

        def pe_rwkv(pe, l):
            pe.wait_ge(sem("rw_sq"), 2 * l + 1)
            pe.wait_ge(sem("ret_affine"), NT * (l + 1))
            for z in range(4):
                ins = nc.tensor.matmul(ps[z][:, 0:T], K("headsum"), w_E[:, z, :], start=True, stop=True)
            ins.then_inc(sem("rw_sums"), 1)
            pe.wait_ge(sem("rw_in"), 48 * (l + 1))
            for d in range(2):
                rows = slice(64 * d, 64 * d + 64)
                if d:
                    pe.wait_ge(sem("rw_sig"), 2 * l + 1)
                for z in range(4):
                    nc.tensor.matmul(ps[4 + z][:, 0:T], a_up[rows, P * z:P * (z + 1)], ZT[rows, A_RW, :],
                                     start=True, stop=True)
                if d == 0:
                    pe.wait_ge(sem("rw_norm"), l + 1)
                    pe.wait_ge(sem("rw_tanh"), l + 1)
                for z in range(4):
                    ins = nc.tensor.matmul(ps[z][:, 0:T], w_up[rows, P * z:P * (z + 1)], ZT[rows, W_RW, :],
                                           start=True, stop=True)
                ins.then_inc(sem("rw_lora"), 1)
            pe.wait_ge(sem("rw_sig"), 2 * l + 2)
            pe.wait_ge(sem("rw_ready"), l + 1)
            for s, chunks in enumerate(STEPS):
                pe_rwkv_step(pe, l, NS * l + s, chunks)
                if s == 1:
                    pe.wait_ge(sem("rw_state"), (NS + 1) * l + s + 1)
                    heads(lambda d, z, rows, g: nc.tensor.matmul(ps[7][rows, g], u_S[rows, g], K("eye64")[rows, :],
                                                                 start=True, stop=True)).then_inc(sem("rw_turn"), 1)
                    pe.wait_ge(sem("rw_state_in"), 64 * (l + 1))
                    heads(lambda d, z, rows, g: nc.tensor.matmul(ps[6][rows, g], u_in[rows, g], K("eye64")[rows, :],
                                                                 start=True, stop=True)).then_inc(sem("rw_turn"), 1)
            pe.wait_ge(sem("rw_state"), (NS + 1) * (l + 1))
            pe.wait_ge(sem("rw_sq"), 2 * l + 2)
            for z in range(4):
                ins = nc.tensor.matmul(ps[4 + z][:, 0:T], K("headsum"), w_E[:, z, :], start=True, stop=True)
            ins.then_inc(sem("rw_sums"), 1)
            pe.wait_ge(sem("rw_O"), l + 1)
            for z in range(4):
                for c in range(NCH):
                    for q in range(2):
                        rows = slice(64 * q, 64 * q + 64)
                        ins = nc.tensor.matmul(ps[z][rows, 64 * c:64 * c + 64], w_Oc[rows, c, 64 * z:64 * z + 64],
                                               K("eye64")[rows, :], start=True, stop=True)
            ins.then_inc(sem("rw_OT"), 1)
            pe.wait_ge(sem("rw_bonus"), l + 1)
            for z in range(4):
                ins = nc.tensor.matmul(ps[4 + z][:, 0:T], g_up[:, P * z:P * (z + 1)], ZT[:, GL_RW, :], start=True, stop=True)
            ins.then_inc(sem("rw_gate"), 1)

        def pe_rwkv_step(pe, l, m, chunks):
            n = (NS + 1) * l + m % NS + (1 if m % NS >= 2 else 0)
            tok = [slice(C * c, C * c + C) for c in chunks]
            for bank, src in ((0, w_B), (2, w_K)):
                for d in range(2):
                    for z in range(4):
                        for q in range(2):
                            rows = slice(64 * q, 64 * q + 64)
                            ins = nc.tensor.matmul(ps[bank + d][rows, P * z:P * (z + 1)].rearrange("p (x t) -> p x t", x=2),
                                                   src[d][rows, z, tok[d]], w_QR[d][rows, :, z, tok[d]],
                                                   start=True, stop=True)
                ins.then_inc(sem("rw_pairs"), 1)
            if m % NS:
                pe.wait_ge(sem("rw_state"), n)
            if m % NS == 2:
                pe.wait_ge(sem("rw_out"), l + 1)
            V, swapped = V_AT[m % NS]

            def v_at(d, z, rows):
                at = 256 * (1 - d if swapped else d) + 64 * z
                return V[rows, at:at + 64]
            for bank, src in ((4, w_K), (5, w_B)) + (() if swapped else ((6, (v_, v_)),)):
                ins = heads(lambda d, z, rows, g: nc.tensor.matmul(ps[bank][rows, g], src[d][rows, z, tok[d]],
                                                                   K("eye64")[rows, :], start=True, stop=True))
            ins.then_inc(sem("rw_pairs"), 1)
            pe.wait_ge(sem("rw_masked"), 2 * m + 2)
            pe.wait_ge(sem("rw_tok"), 2 * m + 2)

            def rhs(d, z, rows, g):
                nc.tensor.matmul(ps[2][rows, g], w_QR[d][rows, 0, z, tok[d]], u_S[rows, g], start=True, stop=False)
                return nc.tensor.matmul(ps[2][rows, g], u_G[rows, g], v_at(d, z, rows), start=False, stop=True)
            for j in range(LEVELS):
                M = u_Ms[j % 2]
                for d in range(2):
                    pe.wait_ge(sem("rw_M"), level(m, j, d))
                    if j:
                        pe.wait_ge(sem("rw_XY"), level(m, j - 1, d))
                    bank = ps[(7, 3)[d]]
                    heads(lambda d, z, rows, g: nc.tensor.matmul(bank[rows, g], M[rows, g],
                                                                 u_X[rows, g] if j else K("eye64")[rows, :],
                                                                 start=True, stop=True), (d,)).then_inc(sem("rw_T"), 1)
                if j == 0:
                    heads(rhs).then_inc(sem("rw_rhs"), 1)
                    continue
                for d in range(2):
                    pe.wait_ge(sem("rw_Tc"), later(m, j, d))
                    ins = heads(lambda d, z, rows, g: nc.tensor.matmul(ps[d][rows, C * z:C * (z + 1)], u_T[rows, g],
                                                                       u_Y[rows, g], start=True, stop=True), (d,))
                    if j < LEVELS - 1:
                        ins = heads(lambda d, z, rows, g: nc.tensor.matmul(ps[d][rows, 256 + C * z:256 + C * (z + 1)],
                                                                           u_Y[rows, g], u_T[rows, g],
                                                                           start=True, stop=True), (d,))
                    ins.then_inc(sem("rw_XYp"), 1)
            pe.wait_ge(sem("rw_rhsc"), m + 1)
            for d in range(2):
                pe.wait_ge(sem("rw_XY"), level(m, LEVELS - 1, d))
                bank = ps[(7, 3)[d]]
                heads(lambda d, z, rows, g: nc.tensor.matmul(bank[rows, g], u_Y[rows, g], u_A[rows, g],
                                                             start=True, stop=True), (d,)).then_inc(sem("rw_alpha"), 1)

            def outp(d, z, rows, g):
                nc.tensor.matmul(ps[4][rows, g], w_QR[d][rows, 1, z, tok[d]], u_S[rows, g], start=True, stop=False)
                nc.tensor.matmul(ps[4][rows, g], u_RK[rows, g], v_at(d, z, rows), start=False, stop=False)
                return nc.tensor.matmul(ps[4][rows, g], u_RB[rows, g], u_M[rows, g], start=False, stop=True)
            for d in range(2):
                pe.wait_ge(sem("rw_alphac"), 2 * m + d + 1)
                ins = heads(outp, (d,))
            ins.then_inc(sem("rw_o"), 1)

            def state(d, z, rows, g):
                nc.tensor.matmul(ps[5][rows, g], u_K[rows, g], v_at(d, z, rows), start=True, stop=False)
                return nc.tensor.matmul(ps[5][rows, g], u_B[rows, g], u_M[rows, g], start=False, stop=True)
            heads(state).then_inc(sem("rw_S"), 1)

        def act_rwkv(act, link, l):
            act.wait_ge(sem("rw_shift"), 15 * (l + 1))
            nc.scalar.activation(ZT[:, W_RW, :], ZT[:, W_RW, :], ACT.Tanh).then_inc(sem("rw_tanh"), 1)
            act.wait_ge(sem("rw_norm"), l + 1)
            nc.scalar.activation(flat(w_L), flat(w_L), ACT.Sqrt).then_inc(sem("rw_root"), 1)
            for d in range(2):
                act.wait_ge(sem("rw_lora"), 2 * l + d + 1)
                if d:
                    act.wait_ge(sem("rw_prep"), 2 * l + 1)
                for z in range(4):
                    nc.scalar.activation(w_LW[:, z, :], ps[z][:, 0:T], ACT.Sigmoid, bias=pcol("rwkv_w0", 4 * d + z))
                for z in range(4):
                    ins = nc.scalar.activation(w_E[:, z, :], ps[4 + z][:, 0:T], ACT.Sigmoid, bias=pcol("rwkv_a0", 4 * d + z))
                ins.then_inc(sem("rw_sig"), 1)
                act.wait_ge(sem("rw_L"), 2 * l + d + 1)
                incl, excl = (w_L, w_LW) if d == 0 else (w_LW, w_L)
                ends = incl.rearrange("p z (c t) -> p z c t", t=C)[:, :, :, C - 1 if d == 0 else 0]
                nc.scalar.activation(w_ends[:, d, :, :], ends, ACT.Exp, scale=DECAY)
                nc.scalar.activation(flat(w_QR[d][:, 1, :, :]), flat(incl), ACT.Exp, scale=DECAY)
                link(nc.scalar.activation(flat(excl), flat(excl), ACT.Exp, scale=DECAY))
                nc.scalar.activation(flat(incl), flat(incl), ACT.Exp, scale=-DECAY).then_inc(sem("rw_exp"), 1)
            nc.scalar.activation(ZT[:, GL_RW, :], ZT[:, GL_RW, :], ACT.Sigmoid).then_inc(sem("rw_gl"), 1)
            for s in range(NS):
                m = NS * l + s
                act.wait_ge(sem("rw_pairs"), 3 * m + 1)
                for d in range(2):
                    ins = nc.scalar.activation(u_A[:, 256 * d:256 * (d + 1)].rearrange("p (z t) -> p z t", z=4),
                                               ps[d][:, :].rearrange("p (z x t) -> p z x t", z=4, x=2)[:, :, 0, :], ACT.Copy)
                ins.then_inc(sem("rw_tok"), 1)
                act.wait_ge(sem("rw_pairs"), 3 * m + 3)
                nc.scalar.activation(u_K, ps[4][:, :], ACT.Copy)
                ins = nc.scalar.activation(u_B, ps[5][:, :], ACT.Copy)
                V, swapped = V_AT[s]
                if not swapped:
                    if s == 3:
                        act.wait_ge(sem("rw_turn"), 2 * (l + 1))
                    ins = nc.scalar.activation(V, ps[6][:, :], ACT.Copy)
                ins.then_inc(sem("rw_tok"), 1)
                for j in range(1, LEVELS):
                    for d in range(2):
                        g = slice(256 * d, 256 * (d + 1))
                        act.wait_ge(sem("rw_T"), level(m, j, d))
                        nc.scalar.activation(u_T[:, g], ps[(7, 3)[d]][:, g], ACT.Copy).then_inc(sem("rw_Tc"), 1)
                act.wait_ge(sem("rw_M"), level(m, LEVELS - 1, 1))
                act.wait_ge(sem("rw_rhs"), m + 1)
                nc.scalar.activation(u_A, ps[2][:, :], ACT.Copy).then_inc(sem("rw_rhsc"), 1)
                for d in range(2):
                    g = slice(256 * d, 256 * (d + 1))
                    act.wait_ge(sem("rw_alpha"), 2 * m + d + 1)
                    nc.scalar.activation(u_M[:, g], ps[(7, 3)[d]][:, g], ACT.Copy, scale=-1.0)\
                        .then_inc(sem("rw_alphac"), 1)
                if s == 1:
                    act.wait_ge(sem("rw_turn"), 2 * l + 1)
                    nc.scalar.activation(u_out, ps[7][:, :], ACT.Copy).then_inc(sem("rw_out"), 1)
            act_root(act, w_tot)
            act.wait_ge(sem("rw_OT"), l + 1)
            for z in range(4):
                ins = nc.scalar.activation(w_N[:, z, :], ps[z][:, 0:T], ACT.Identity, bias=pcol("rwkv_gn_b", z),
                                           scale=pcol("rwkv_gn_w", z))
            ins.then_inc(sem("rw_affine"), 1)

        def dve_keys(dve, link, l):
            dve.wait_ge(sem("rw_shift"), 15 * (l + 1))
            for z in range(4):
                ins = nc.vector.tensor_scalar(w_kk[:, z, :], k_[:, z, :], pcol("rwkv_k_k", z), None, ALU.mult)
            link(ins)
            nc.vector.tensor_tensor(w_E, w_kk, w_kk, ALU.mult).then_inc(sem("rw_sq"), 1)

        def dve_rwkv(dve, link, l):
            dve.wait_ge(sem("ret_done"), l + 1)
            dve.wait_ge(sem("stored"), 16 * (7 * l + 3))
            dve.wait_ge(sem("rw_sums"), 2 * l + 1)
            for z in range(4):
                ins = nc.vector.tensor_scalar(w_L[:, z, :], ps[z][:, 0:T], 1e-24, None, ALU.max)
            ins.then_inc(sem("rw_norm"), 1)
            dve.wait_ge(sem("rw_root"), l + 1)
            link(nc.vector.reciprocal(flat(w_L), flat(w_L)))
            nc.vector.tensor_tensor(w_kk, w_kk, w_L, ALU.mult).then_inc(sem("rw_kk"), 1)
            dve.wait_ge(sem("rw_kk"), l + 1)
            for d in range(2):
                incl, excl = (w_L, w_LW) if d == 0 else (w_LW, w_L)
                dve.wait_ge(sem("rw_sig"), 2 * l + d + 1)
                for z in range(4):
                    ins = nc.vector.tensor_tensor_scan(w_L[:, z, :], K("carry"), w_LW[:, z, :], 0.0, ALU.mult, ALU.add)
                link(ins)
                if d == 0:
                    nc.vector.tensor_tensor(w_LW, w_L, w_LW, ALU.subtract).then_inc(sem("rw_L"), 1)
                else:
                    Lg = flat(w_L).rearrange("p (g t) -> p g t", t=C)
                    link(nc.vector.tensor_copy(w_tot, Lg[:, :, C - 1]))
                    link(nc.vector.tensor_tensor(Lg, w_tot.rearrange("p (g o) -> p g o", o=1).to_broadcast([P, 24, C]), Lg,
                                                 ALU.subtract))
                    nc.vector.tensor_tensor(w_LW, w_L, w_LW, ALU.add).then_inc(sem("rw_L"), 1)
                nc.vector.tensor_tensor(w_B[d], w_kk, w_E, ALU.mult)
                for z in range(4):
                    ins = nc.vector.tensor_scalar(w_K[d][:, z, :], w_E[:, z, :], -1.0, pcol("rwkv_k_a", z), ALU.add, ALU.mult)
                link(ins)
                link(nc.vector.scalar_tensor_tensor(flat(w_K[d]), flat(w_K[d]), 1.0, flat(k_), ALU.add, ALU.mult))
                dve.wait_ge(sem("rw_exp"), 2 * l + d + 1)
                nc.vector.tensor_tensor(w_QR[d][:, 0, :, :], w_kk, excl, ALU.mult)
                nc.vector.tensor_tensor(w_QR[d][:, 1, :, :], w_QR[d][:, 1, :, :], r_, ALU.mult)
                nc.vector.tensor_tensor(w_K[d], w_K[d], incl, ALU.mult)
                nc.vector.tensor_tensor(w_B[d], w_B[d], incl, ALU.mult).then_inc(sem("rw_prep"), 1)
                dve.wait_ge(sem("rw_prep"), 2 * l + d + 1)
            link(nc.vector.tensor_tensor(w_E, r_, k_, ALU.mult))
            for z in range(4):
                ins = nc.vector.tensor_scalar(w_E[:, z, :], w_E[:, z, :], pcol("rwkv_r_k", z), None, ALU.mult)
            ins.then_inc(sem("rw_sq"), 1)
            nc.vector.memset(u_S, 0.0)
            nc.vector.memset(w_Og, 0.0).then_inc(sem("rw_ready"), 1)
            dve.wait_ge(sem("rw_ready"), l + 1)
            for s, chunks in enumerate(STEPS):
                dve_rwkv_step(dve, link, l, NS * l + s, chunks)
                if s == 1:
                    dve.wait_ge(sem("rw_turn"), 2 * l + 2)
                    nc.vector.tensor_copy(u_S, ps[6][:, :]).then_inc(sem("rw_state"), 1)
            def wide(v):
                return v.rearrange("p (g o) -> p g o", o=1).to_broadcast([P, 24, C])
            link(nc.vector.tensor_reduce(w_tot, w_Og, X_AXIS, ALU.add))
            link(nc.vector.tensor_scalar(w_tot, w_tot, 1.0 / C, None, ALU.mult))
            link(nc.vector.tensor_tensor(w_Og, w_Og, wide(w_tot), ALU.subtract))
            link(nc.vector.tensor_tensor(w_sq, w_Og, w_Og, ALU.mult))
            link(nc.vector.tensor_reduce(w_tot, w_sq, X_AXIS, ALU.add))
            rsqrt(dve, link, nc.vector.tensor_scalar(w_tot, w_tot, 1.0 / C, None, ALU.mult), w_tot, RWKV_EPS, ALU.add)
            nc.vector.tensor_tensor(w_Og, w_Og, wide(w_tot), ALU.mult).then_inc(sem("rw_O"), 1)
            dve.wait_ge(sem("rw_sums"), 2 * l + 2)
            for z in range(4):
                ins = nc.vector.tensor_tensor(w_E[:, z, :], ps[4 + z][:, 0:T], v_[:, z, :], ALU.mult)
            ins.then_inc(sem("rw_bonus"), 1)
            dve.wait_ge(sem("rw_bonus"), l + 1)
            dve.wait_ge(sem("rw_affine"), l + 1)
            link(nc.vector.tensor_tensor(w_E, w_E, w_N, ALU.add))
            dve.wait_ge(sem("rw_gate"), l + 1)
            for z in range(4):
                ins = nc.vector.tensor_tensor(w_E[:, z, :], w_E[:, z, :], ps[4 + z][:, 0:T], ALU.mult)
            ins.then_inc(sem("rw_done"), 1)

        def dve_rwkv_step(dve, link, l, m, chunks):
            def part(u, d):
                return u[:, 256 * d:256 * (d + 1)].rearrange("p (z t) -> p z t", z=4)

            def scores(bank, x):
                return ps[bank][:, :].rearrange("p (z x t) -> p z x t", z=4, x=2)[:, :, x, :]
            dve.wait_ge(sem("rw_pairs"), 3 * m + 2)
            for d in range(2):
                nc.vector.tensor_tensor(part(u_G, d), scores(2 + d, 0), both("before", d), ALU.mult)
            for d in range(2):
                ins = nc.vector.tensor_tensor(part(u_RK, d), scores(2 + d, 1), both("upto", d), ALU.mult)
            ins.then_inc(sem("rw_masked"), 1)
            dve.wait_ge(sem("rw_tok"), 2 * m + 1)
            for d in range(2):
                ins = nc.vector.tensor_tensor(part(u_RB, d), scores(d, 1), both("upto", d), ALU.mult)
            ins.then_inc(sem("rw_masked"), 1)
            def masked(j):
                for d in range(2):
                    lv = K("levels")[:, P * j + 64 * d:P * j + 64 * d + 64].rearrange("p (o t) -> p o t", o=1)
                    nc.vector.tensor_tensor(part(u_Ms[j % 2], d), part(u_A, d), lv.to_broadcast([P, 4, 64]), ALU.mult)\
                        .then_inc(sem("rw_M"), 1)
            eye = K("eye64").rearrange("p (o t) -> p o t", o=1).to_broadcast([P, 4, 64])
            masked(0)
            for j in range(LEVELS):
                if 1 <= j < LEVELS - 1:
                    dve.wait_ge(sem("rw_T"), level(m, j - 1, 1))
                if j < LEVELS - 1:
                    masked(j + 1)
                for d in range(2):
                    def bank(at, d=d):
                        return ps[d][:, at:at + 256].rearrange("p (z t) -> p z t", z=4)
                    if j == 0:
                        dve.wait_ge(sem("rw_M"), level(m, 0, d))
                        nc.vector.tensor_tensor(part(u_Y, d), eye, part(u_M, d), ALU.subtract)
                        dve.wait_ge(sem("rw_T"), level(m, 0, d))
                        ins = nc.vector.tensor_tensor(part(u_X, d), eye, part(ps[(7, 3)[d]], d), ALU.subtract)
                    else:
                        dve.wait_ge(sem("rw_XY"), level(m, j - 1, d))
                        dve.wait_ge(sem("rw_XYp"), later(m, j, d))
                        ins = nc.vector.tensor_tensor(part(u_Y, d), part(u_Y, d), bank(0), ALU.subtract)
                        if j < LEVELS - 1:
                            ins = nc.vector.tensor_tensor(part(u_X, d), part(u_X, d), bank(256), ALU.subtract)
                    ins.then_inc(sem("rw_XY"), 1)
                if j == 0:
                    dve.wait_ge(sem("rw_XY"), level(m, 0, 1))
            dve.wait_ge(sem("rw_o"), m + 1)
            for d in range(2):
                o = w_Oc[:, chunks[d], :]
                link(nc.vector.tensor_tensor(o, o, ps[4][:, 256 * d:256 * (d + 1)], ALU.add))
            dve.wait_ge(sem("rw_S"), m + 1)
            link(nc.vector.tensor_tensor(u_X, u_S, ps[5][:, :], ALU.add))
            for d in range(2):
                e = w_ends[:, d, :, chunks[d]].rearrange("p (z o) -> p z o", o=1).to_broadcast([P, 4, 64])
                ins = nc.vector.tensor_tensor(part(u_S, d), part(u_X, d), e, ALU.mult)
            ins.then_inc(sem("rw_state"), 1)
            dve.wait_ge(sem("rw_state"), m + l + 1 + (1 if m % NS >= 2 else 0))

        g_T = arena[:, 0:24 * T].rearrange("p (z t) -> p z t", t=T)
        merged = arena[:, 24 * T:32 * T].rearrange("p (z t) -> p z t", t=T)
        m_tmp = [arena[:, TMP + T * b:TMP + T * (b + 1)] for b in range(2)]
        res_tmp = [[arena[:, at + 512 * b:at + 512 * (b + 1)] for b in range(2)] for at in (TMP + 1024, 0)]

        def pe_merge(pe, l):
            for z in range(24):
                if z % 4 == 0:
                    w = chunk_here(pe, l, 22 + z // 4)
                if z == 0:
                    pe.wait_ge(sem("rw_affine"), l + 1)
                if z >= 4:
                    pe.wait_ge(sem("gate_act"), 24 * l + z - 3)
                for k in range(KT):
                    ins = nc.tensor.matmul(ps[z % 4][:, 0:T], w[:, k, P * (z % 4):P * (z % 4) + P], hT[:, k, :],
                                           start=(k == 0), stop=(k == KT - 1))
                ins.then_inc(sem("gate_mm"), 1)
            pe.wait_ge(sem("rw_done"), l + 1)
            for b in range(3):
                w = chunk_here(pe, l, 28 + b)
                for z in range(8):
                    n = 8 * b + z
                    if n >= 4:
                        pe.wait_ge(sem("branch_dve"), 24 * l + n - 3)
                    for k in range(4):
                        ins = nc.tensor.matmul(ps[4 + n % 4][:, 0:T], w[:, k, P * z:P * (z + 1)], oT[:, b, k, :],
                                               start=(k == 0), stop=(k == 3))
                    ins.then_inc(sem("branch_mm"), 1)
            pe.wait_ge(sem("merged"), 8 * (l + 1))
            pe.wait_ge(sem("gate_act"), 24 * (l + 1))
            for c in range(2):
                w = chunk_here(pe, l, 31 + c)
                for t in range(NT):
                    n = NT * c + t
                    if n >= 4:
                        pe.wait_ge(sem("res_dve"), 6 * l + n - 3)
                    for k in range(KT):
                        ins = nc.tensor.matmul(ps[n % 4][:, :], merged[:, k, P * t:P * (t + 1)], w[:, k, :],
                                               start=(k == 0), stop=(k == KT - 1))
                    ins.then_inc(sem("out_mm"), 1)

        def act_merge(act, l):
            act.wait_ge(sem("rw_done"), l + 1)
            for z in range(24):
                act.wait_ge(sem("gate_mm"), 24 * l + z + 1)
                nc.scalar.activation(g_T[:, z, :], ps[z % 4][:, 0:T], ACT.Sigmoid).then_inc(sem("gate_act"), 1)
            act_norm_roots(act)

        def dve_merge(dve, link, l):
            for n in range(24):
                b, z = divmod(n, 8)
                dve.wait_ge(sem("branch_mm"), 24 * l + n + 1)
                dve.wait_ge(sem("gate_act"), 24 * l + n + 1)
                bank = ps[4 + n % 4][:, 0:T]
                if b == 0:
                    nc.vector.tensor_tensor(merged[:, z, :], bank, g_T[:, n, :], ALU.mult).then_inc(sem("branch_dve"), 1)
                    continue
                nc.vector.tensor_tensor(m_tmp[n % 2], bank, g_T[:, n, :], ALU.mult).then_inc(sem("branch_dve"), 1)
                dve.wait_ge(sem("branch_dve"), 24 * l + n + 1)
                ins = nc.vector.tensor_tensor(merged[:, z, :], merged[:, z, :], m_tmp[n % 2], ALU.add)
                if b == 2:
                    ins.then_inc(sem("merged"), 1)
                else:
                    link(ins)
            for n in range(6):
                c, t = divmod(n, NT)
                dve.wait_ge(sem("out_mm"), 6 * l + n + 1)
                dve_residual(dve, link, ps[n % 4], 0, t, c, "res_dve", 6 * l + n + 1)
            dve_out_norm(dve, link, l, 0)

        def dve_residual(dve, link, bank, which, t, c, done, value):
            cols = slice(512 * c, 512 * (c + 1))
            x = X[:, t, cols]
            tmp = res_tmp[which][(t + c) % 2]
            nc.vector.tensor_tensor(tmp, bank[:, :], gate[:, which, min(t, 1), cols], ALU.mult).then_inc(sem(done), 1)
            dve.wait_ge(sem(done), value)
            link(nc.vector.scalar_tensor_tensor(x, x, ALPHA, tmp, ALU.mult, ALU.add))

        def dve_out_norm(dve, link, l, which):
            n = 2 * l + which
            for t in range(NT):
                link(dve_layer_norm(dve, link, X[:, t, :], X[:, t, :]))
                if t == 0:
                    dve.wait_ge(sem("ln_in"), 32 * (n + 1))
                link(nc.vector.tensor_tensor(X[:, t, :], X[:, t, :], lnp[:, 0, :], ALU.mult))
                nc.vector.tensor_tensor(X[:, t, :], X[:, t, :], lnp[:, 1, :], ALU.add).then_inc(sem("x_done"), 1)
                dve.wait_ge(sem("x_done"), NT * n + t + 1)

        q_T = arena[:, 0:8 * T].rearrange("p (h t) -> p h t", t=T)
        keys_in = arena[:, 3072:4096].rearrange("p (h x) -> p h x", h=PH)
        keys_T = arena[:, 4096:5120].rearrange("p (h k) -> p h k", h=PH)
        sc = [arena[:, 5120 + 768 * b:5888 + 768 * b].rearrange("p (s t k) -> p s t k", s=2, t=NT) for b in range(2)]
        top_v = arena[:, 7168:7936].rearrange("p (t s h k) -> p t s h k", t=NT, s=2, h=PH)
        top_i = arena[:, 7936:8704].bitcast(U32).rearrange("p (t s h k) -> p t s h k", t=NT, s=2, h=PH)
        NCAND = FULL * TOPK + TOPK - FULL
        cand = arena[:, 9216:9216 + PH * NCAND].rearrange("p (h x) -> p h x", h=PH)
        TOP = 13312

        def tops(at, n, dt=F32):
            v = arena[:, TOP + at:TOP + at + n]
            return v if dt is F32 else v.bitcast(dt)
        tifs = [tops(at, 256).rearrange("p (s h k) -> p s h k", s=2, h=PH) for at in (512, 2304)]
        fs_ = tops(768, 128).rearrange("p (h k) -> p h k", h=PH)
        fp_ = tops(896, 128, U32).rearrange("p (h k) -> p h k", h=PH)
        fi_ = tops(1024, 256, U32).rearrange("p (s x) -> p s x", s=2)
        ff_ = tops(1280, 256).rearrange("p (s x) -> p s x", s=2)
        eqs = [[arena[:, 11264:13312], tops(2560, 2048)], [tops(4736, 2048), tops(6784, 2048)]]
        ijg = [tops(1536 + 384 * b, 384).rearrange("p (s x) -> p s x", s=3) for b in range(2)]
        fsum = small[:, 0:8]
        LOW = -3.0e38

        def pool_keys(pool, l):
            pool.wait_ge(sem("x_done"), NT * (2 * l + 1))
            pool.dma_start(keys_in.rearrange("p h (s d) -> p h s d", s=2),
                           a["peer_keys"][l].rearrange("h s k d -> k h s d")).then_inc(sem("keys_in"), 16)

        def pe_select(pe, l):
            pe.wait_ge(sem("h_ready"), 6 * (2 * l + 2))
            pe.wait_ge(sem("keys_in"), 16 * (l + 1))
            for h in range(PH):
                ins = nc.tensor.transpose(ps[h // 4][:, P * (h % 4):P * (h % 4) + P], keys_in[:, h, :], ident)
                if h % 4 == 3:
                    ins.then_inc(sem("keys_turned"), 1)

            def query(h):
                w = chunk_here(pe, l, 33 + h // 4)
                if h >= 2:
                    pe.wait_ge(sem("query_act"), 8 * l + h - 1)
                for k in range(KT):
                    ins = nc.tensor.matmul(ps[4 + h % 2][:, 0:T], w[:, k, P * (h % 4):P * (h % 4) + P], hT[:, k, :],
                                           start=(k == 0), stop=(k == KT - 1))
                ins.then_inc(sem("query_mm"), 1)

            def scores(h):
                pe.wait_ge(sem("query_act"), 8 * l + h + 1)
                if h == 0:
                    pe.wait_ge(sem("keys_act"), 2 * (l + 1))
                if h >= 2:
                    pe.wait_ge(sem("score_act"), 2 * (8 * l + h - 1))
                for s in range(2):
                    rows = slice(64 * s, 64 * s + 64)
                    for t in range(NT):
                        ins = nc.tensor.matmul(ps[2 * (h % 2) + s][:, P * t:P * (t + 1)], q_T[rows, h, P * t:P * (t + 1)],
                                               keys_T[rows, h, :], start=True, stop=True)
                    ins.then_inc(sem("score_mm"), 1)
            for h in range(PH + 1):
                if h < PH:
                    query(h)
                if h:
                    scores(h - 1)
            for t in range(NT):
                pe.wait_ge(sem("chosen"), NT * l + t + 1)
                pe.wait_ge(sem("picked"), 4 * l + min(2 * t + 2, 4))
                for i in range(3):
                    ins = nc.tensor.transpose(ps[5 + t][:, P * i:P * (i + 1)], ijg[t % 2][:, i, :], ident)
                ins.then_inc(sem("chosen_T"), 1)

        def act_select(act, l):
            act.wait_ge(sem("x_done"), NT * (2 * l + 1))
            for i in range(2):
                act.wait_ge(sem("keys_turned"), 2 * l + i + 1)
                nc.scalar.activation(keys_T[:, 4 * i:4 * i + 4, :].rearrange("p h k -> p (h k)"), ps[i][:, :], ACT.Copy)\
                    .then_inc(sem("keys_act"), 1)
            for h in range(PH + 1):
                if h < PH:
                    act.wait_ge(sem("query_mm"), 8 * l + h + 1)
                    nc.scalar.activation(q_T[:, h, :], ps[4 + h % 2][:, 0:T], ACT.Copy).then_inc(sem("query_act"), 1)
                if h:
                    if h >= 3:
                        act.wait_ge(sem("topped"), 8 * l + h - 2)
                    for s in range(2):
                        act.wait_ge(sem("score_mm"), 2 * (8 * l + h - 1) + s + 1)
                        nc.scalar.activation(sc[(h - 1) % 2][:, s, :, :].rearrange("p t k -> p (t k)"),
                                             ps[2 * ((h - 1) % 2) + s][:, 0:T], ACT.Copy).then_inc(sem("score_act"), 1)
            for t in range(NT):
                act_softmax(act, l, t)

        def act_softmax(act, l, t):
            act.wait_ge(sem("final_tops"), NT * l + t + 1)
            nc.scalar.activation(fs_, fs_, ACT.Exp).then_inc(sem("final_exp"), 1)
            act.wait_ge(sem("chosen_T"), NT * l + t + 1)
            tok = slice(P * t, P * (t + 1))
            nc.scalar.activation(chosen_ij[:, :, tok], ps[5 + t][:, 0:2 * P].rearrange("p (i n) -> p i n", i=2), ACT.Copy)
            nc.scalar.activation(chosen_g[:, tok], ps[5 + t][:, 2 * P:3 * P], ACT.Copy).then_inc(sem("ijg"), 1)

        def dve_top16(link, values, vals, idxs):
            n = len(values)
            for half in range(2):
                for i in range(n):
                    ins = nc.vector.max(vals[i][:, 8 * half:8 * half + 8], values[i])
                link(ins)
                for i in range(n):
                    ins = nc.vector.max_index(idxs[i][:, 8 * half:8 * half + 8], vals[i][:, 8 * half:8 * half + 8], values[i])
                if half == 0:
                    link(ins)
                    for i in range(n):
                        ins = nc.vector.match_replace(values[i], vals[i][:, 0:8], values[i], LOW)
                    link(ins)
            return ins

        def pick(engine, link, t, s):
            e3 = eqs[t % 2][s].rearrange("p (x a) -> p x a", a=TOPK)
            e4 = eqs[t % 2][s].rearrange("p (h k a) -> p h k a", h=PH, k=TOPK)
            link(engine.tensor_tensor(
                e4, e4, tifs[t % 2][:, s, :, :].rearrange("p h (o a) -> p h o a", o=1).to_broadcast([P, PH, TOPK, TOPK]),
                ALU.mult))
            n = TOPK // 2
            while n > 1:
                link(engine.tensor_tensor(e3[:, :, 0:n], e3[:, :, 0:n], e3[:, :, n:2 * n], ALU.add))
                n //= 2
            return engine.tensor_tensor(ijg[t % 2][:, s, :].rearrange("p (x o) -> p x o", o=1), e3[:, :, 0:1],
                                        e3[:, :, 1:2], ALU.add)

        def pool_select(pool, link, l):
            for t in range(2):
                for s in range(2):
                    pool.wait_ge(sem("places"), 2 * (NT * l + t) + s + 1)
                    pick(nc.gpsimd, link, t, s).then_inc(sem("picked"), 1)

        def dve_select(dve, link, l):
            for h in range(PH):
                dve.wait_ge(sem("score_act"), 2 * (8 * l + h + 1))
                groups = [(t, s) for t in range(NT) for s in range(2)]
                dve_top16(link, [sc[h % 2][:, s, t, :] for t, s in groups], [top_v[:, t, s, h, :] for t, s in groups],
                          [top_i[:, t, s, h, :] for t, s in groups]).then_inc(sem("topped"), 1)
            dve.wait_ge(sem("topped"), 8 * (l + 1))
            for t in range(NT):
                ts_ = top_v[:, t, :, :, :]
                nc.vector.tensor_copy(tifs[t % 2], top_i[:, t, :, :, :])
                nc.vector.tensor_tensor(
                    cand[:, :, 0:FULL * TOPK].rearrange("p h (a b) -> p h a b", a=FULL),
                    ts_[:, 0, :, 0:FULL].rearrange("p h (a o) -> p h a o", o=1).to_broadcast([P, PH, FULL, TOPK]),
                    ts_[:, 1, :, :].rearrange("p h (o b) -> p h o b", o=1).to_broadcast([P, PH, FULL, TOPK]), ALU.add)
                link(nc.vector.tensor_tensor(cand[:, :, FULL * TOPK:NCAND], ts_[:, 0, :, FULL:TOPK],
                                             ts_[:, 1, :, 0:1].to_broadcast([P, PH, TOPK - FULL]), ALU.add))
                link(dve_top16(link, [cand[:, h, :] for h in range(PH)],
                               [fs_[:, h, :] for h in range(PH)], [fp_[:, h, :] for h in range(PH)]))
                link(nc.vector.tensor_copy(fsum.rearrange("p (h o) -> p h o", o=1), fs_[:, :, 0:1]))
                nc.vector.tensor_tensor(fs_, fs_, fsum.rearrange("p (h o) -> p h o", o=1).to_broadcast([P, PH, TOPK]),
                                        ALU.subtract).then_inc(sem("final_tops"), 1)
                fpf = fp_.rearrange("p h k -> p (h k)")
                nc.vector.tensor_scalar(fi_[:, 0, :], fpf, 4, None, ALU.logical_shift_right)
                link(nc.vector.tensor_scalar(fi_[:, 1, :], fpf, 15, None, ALU.bitwise_and))
                link(nc.vector.tensor_copy(ff_, fi_))
                tail = tops(4608, P)
                link(nc.vector.scalar_tensor_tensor(tail, ff_[:, 0, :], float(FULL), ff_[:, 1, :], ALU.is_ge, ALU.mult))
                nc.vector.tensor_tensor(ff_[:, 0, :], ff_[:, 0, :], tail, ALU.add)
                link(nc.vector.tensor_tensor(ff_[:, 1, :], ff_[:, 1, :], tail, ALU.subtract))
                if t == 2:
                    dve.wait_ge(sem("picked"), 4 * l + 2)
                for s in range(2):
                    nc.vector.tensor_tensor(
                        eqs[t % 2][s].rearrange("p (x a) -> p x a", a=TOPK),
                        ff_[:, s, :].rearrange("p (x o) -> p x o", o=1).to_broadcast([P, P, TOPK]),
                        K("iota")[:, 0:TOPK].rearrange("p (o a) -> p o a", o=1).to_broadcast([P, P, TOPK]),
                        ALU.is_equal).then_inc(sem("places"), 1)
                out = ijg[t % 2]
                if t == 2:
                    dve.wait_ge(sem("chosen_T"), NT * l + 1)
                    dve.wait_ge(sem("places"), 6 * (l + 1))
                    for s in range(2):
                        link(pick(nc.vector, link, t, s))
                dve.wait_ge(sem("final_exp"), NT * l + t + 1)
                link(nc.vector.tensor_reduce(fsum, fs_, X_AXIS, ALU.add))
                link(nc.vector.reciprocal(fsum, fsum))
                nc.vector.tensor_tensor(out[:, 2, :].rearrange("p (h k) -> p h k", h=PH), fs_,
                                        fsum.rearrange("p (h o) -> p h o", o=1).to_broadcast([P, PH, TOPK]),
                                        ALU.mult).then_inc(sem("chosen"), 1)
                dve.wait_ge(sem("chosen"), NT * l + t + 1)
            dve.wait_ge(sem("ijg"), NT * (l + 1))
            g, rest = chosen_g, ge

            def part(k):
                return gate_parts[:, :, k]
            nc.vector.tensor_copy(iota_bf, K("iota"))
            link(nc.vector.tensor_copy(part(0), g))
            link(nc.vector.tensor_tensor(rest, g, part(0), ALU.subtract))
            link(nc.vector.tensor_copy(part(1), rest))
            link(nc.vector.tensor_tensor(rest, rest, part(1), ALU.subtract))
            nc.vector.tensor_copy(part(2), rest).then_inc(sem("select_done"), 1)

        def pe_gates(pe, s, b, bank):
            pe.wait_ge(sem("onehot_j"), s + 1)
            pe.wait_ge(sem("onehot_i"), s + 1)
            for n in range(SETN):
                for part in range(3):
                    ins = nc.tensor.matmul(bank[:, QUART * n:QUART * (n + 1)], E2[b][:, n, :], E1[b][:, n, part, :],
                                           start=(part == 0), stop=(part == 2))
            ins.then_inc(sem("gate_psum"), 1)

        def dve_onehot(dve, s, Q, n0, b, used=True):
            if used:
                dve.wait_ge(sem("gate_psum"), s - 1)
            nc.vector.tensor_tensor(
                hot_i[b], iota_bf[:, QUART * Q:QUART * (Q + 1)].rearrange("p (o i) -> p o i", o=1)
                .to_broadcast([P, SETN, QUART]),
                chosen_ij[:, 0, bass.ds(n0, SETN)].rearrange("p (n o) -> p n o", o=1).to_broadcast([P, SETN, QUART]),
                ALU.is_equal).then_inc(sem("hot_i"), 1)
            nc.vector.tensor_tensor(
                E2[b], iota_bf.rearrange("p (o j) -> p o j", o=1).to_broadcast([P, SETN, P]),
                chosen_ij[:, 1, bass.ds(n0, SETN)].rearrange("p (n o) -> p n o", o=1).to_broadcast([P, SETN, P]),
                ALU.is_equal).then_inc(sem("onehot_j"), 1)

        def pool_onehot(pool, s, n0, b, used=True):
            if used:
                pool.wait_ge(sem("gate_psum"), s - 1)
            pool.wait_ge(sem("hot_i"), s + 1)
            nc.gpsimd.tensor_tensor(
                E1[b], hot_i[b].rearrange("p n (o i) -> p n o i", o=1).to_broadcast([P, SETN, 3, QUART]),
                gate_parts[:, bass.ds(n0, SETN), :].rearrange("p n (k o) -> p n k o", o=1)
                .to_broadcast([P, SETN, 3, QUART]), ALU.mult).then_inc(sem("onehot_i"), 1)

        def pool_gates(pool, l):
            base = NKEYS * l
            pool.wait_ge(sem("select_done"), l + 1)
            for s in range(2):
                pool_onehot(pool, base + s, SETN * s, s, used=False)
            with pool.Fori(1, QUART // 2) as pair:
                for s in range(2):
                    pool_onehot(pool, pair * 2 + (base + s), pair * (2 * SETN) + SETN * s, s)
            for Q in range(1, NQ):
                with pool.Fori(0, QUART // 2) as pair:
                    for s in range(2):
                        pool_onehot(pool, pair * 2 + (base + QUART * Q + s), pair * (2 * SETN) + SETN * s, s)

        def act_store(act, s, Q, n0, bank):
            act.wait_ge(sem("gate_psum"), s + 1)
            nc.scalar.activation(G[:, QUART * (Q % 2):QUART * (Q % 2 + 1), bass.ds(n0, SETN)],
                                 bank[:, 0:T].rearrange("p (n i) -> p i n", i=QUART), ACT.Copy).then_inc(sem("gate_set"), 1)

        def pe_first_gates(pe, base):
            for s in range(2):
                pe_gates(pe, base + s, s, ps[6 + s])
            with pe.Fori(1, QUART // 2) as pair:
                for s in range(2):
                    pe.wait_ge(sem("gate_set"), pair * 2 + (base + s - 1))
                    pe_gates(pe, pair * 2 + (base + s), s, ps[6 + s])
            pe.wait_ge(sem("gate_set"), base + QUART)

        def dve_first_gates(dve, base):
            for s in range(2):
                dve_onehot(dve, base + s, 0, SETN * s, s, used=False)
            with dve.Fori(1, QUART // 2) as pair:
                for s in range(2):
                    dve_onehot(dve, pair * 2 + (base + s), 0, pair * (2 * SETN) + SETN * s, s)

        def act_first_gates(act, base):
            with act.Fori(0, QUART // 2) as pair:
                for s in range(2):
                    act_store(act, pair * 2 + (base + s), 0, pair * (2 * SETN) + SETN * s, ps[6 + s])

        def steps(eng, run):
            n = QUART // 2
            for Q in range(NQ):
                first, last = Q == 0, Q == NQ - 1
                if first:
                    run(Q, 0, 0)
                with eng.Fori(1 if first else 0, n - 1 if last else n) as pair:
                    run(Q, pair * 2, None)
                if last:
                    run(Q, QUART - 2, QUART - 2)

        def pe_experts(pe, base):
            def turn_a(g, b):
                pe.wait_ge(sem(f"u_in{b}"), g * 8 + (16 - 8 * b))
                for k in range(4):
                    ins = nc.tensor.transpose(ps[7][:, P * k:P * (k + 1)], ublk[b][:, P * k:P * (k + 1)], ident)
                ins.then_inc(sem("turn_a"), 1)

            def turn_b(g, b):
                pe.wait_ge(sem("uT_a"), g + 1)
                for k in range(4):
                    ins = nc.tensor.transpose(ps[7][:, P * k:P * (k + 1)], ublk[b][:, P * (k + 4):P * (k + 5)], ident)
                ins.then_inc(sem("u_used"), 1)

            def hidden(g, b, bank_used):
                pe.wait_ge(sem("uT_b"), g + 1)
                if bank_used:
                    pe.wait_ge(sem("gelu"), g)
                for k in range(KT):
                    ins = nc.tensor.matmul(ps[6][:, 0:T], uT[b][:, k, :], hT[:, k, :], start=(k == 0), stop=(k == KT - 1))
                ins.then_inc(sem("hidden"), 1)

            def value(b, part, start=False, stop=False):
                for t, c in ((0, 0), (0, 1), (1, 0), (1, 1), (2, 0), (2, 1))[3 * part:3 * part + 3]:
                    ins = nc.tensor.matmul(ps[2 * t + c][:, :], Wg[b][:, P * t:P * (t + 1)], vblk[b][:, 512 * c:512 * (c + 1)],
                                           start=start, stop=stop)
                return ins

            def value_ready(g, b):
                pe.wait_ge(sem(f"v_in{b}"), g * 8 + (16 - 8 * b))
                pe.wait_ge(sem("weighted"), g + 1)

            turn_a(base, 0)
            turn_b(base, 0)

            def run(Q, k, peeled):
                for j in range(2):
                    g = k + (base + QUART * Q + j)
                    begin = peeled == 0 and j == 0
                    end = peeled == QUART - 2 and j == 1
                    if not end:
                        if not begin and Q < NQ - 1:
                            pe.wait_ge(sem("gate_set"), g + QUART)
                        else:
                            if j == 0 and Q == NQ - 1:
                                pe.wait_ge(sem("gate_set"), base + NQ * QUART)
                            pe.wait_ge(sem("uT_b"), g + 1)
                        turn_a(g + 1, 1 - j)
                    hidden(g, j, not begin)
                    if not end:
                        turn_b(g + 1, 1 - j)
                    first = peeled == 0 and j == 1
                    if not begin:
                        value_ready(g - 1, 1 - j)
                        value(1 - j, 0, start=first)
                    if Q < NQ - 1:
                        pe.wait_ge(sem("uT_b"), g + 2)
                        pe_gates(pe, g + QUART, j, ps[7])
                    if not begin:
                        value(1 - j, 1, start=first).then_inc(sem("v_used"), 1)
            steps(pe, run)
            end = base + NKEYS - 1
            value_ready(end, 1)
            value(1, 0, stop=True)
            value(1, 1, stop=True).then_inc(sem("v_used"), 1)

        def act_experts(act, base):
            def turn(g, b, buffer_used):
                act.wait_ge(sem("turn_a"), g + 1)
                if buffer_used:
                    act.wait_ge(sem("hidden"), g - 1)
                nc.scalar.activation(uT[b][:, 0:4, :].rearrange("p k e -> p (k e)"), ps[7][:, :], ACT.Copy)\
                    .then_inc(sem("uT_a"), 1)

            turn(base, 0, False)

            def run(Q, k, peeled):
                for j in range(2):
                    g = k + (base + QUART * Q + j)
                    begin = peeled == 0 and j == 0
                    if not (peeled == QUART - 2 and j == 1):
                        turn(g + 1, 1 - j, not begin)
                    act.wait_ge(sem("hidden"), g + 1)
                    if not begin:
                        act.wait_ge(sem("weighted"), g)
                    nc.scalar.activation(ge, ps[6][:, 0:T], ACT.Gelu).then_inc(sem("gelu"), 1)
                    if Q < NQ - 1:
                        act_store(act, g + QUART, Q + 1, k * SETN + SETN * j, ps[7])
            steps(act, run)

        def dve_experts(dve, base):
            def turn(g, b, buffer_used):
                dve.wait_ge(sem("u_used"), g + 1)
                if buffer_used:
                    dve.wait_ge(sem("hidden"), g - 1)
                nc.vector.tensor_copy(uT[b][:, 4:8, :].rearrange("p k e -> p (k e)"), ps[7][:, :]).then_inc(sem("uT_b"), 1)

            turn(base, 0, False)

            def run(Q, k, peeled):
                for j in range(2):
                    g = k + (base + QUART * Q + j)
                    if Q < NQ - 1:
                        dve_onehot(dve, g + QUART, Q + 1, k * SETN + SETN * j, j)
                    if not (peeled == QUART - 2 and j == 1):
                        turn(g + 1, 1 - j, not (peeled == 0 and j == 0))
                    if j == 0:
                        dve.wait_ge(sem("gate_set"), base + QUART * (Q + 1))
                    dve.wait_ge(sem("gelu"), g + 1)
                    if not peeled == 0:
                        dve.wait_ge(sem("v_used"), g - 1)
                    i = bass.ds(k + (QUART * (Q % 2) + j), 1)
                    nc.vector.tensor_tensor(Wg[j].rearrange("p (o n) -> p o n", o=1), ge.rearrange("p (o n) -> p o n", o=1),
                                            G[:, i, :], ALU.mult).then_inc(sem("weighted"), 1)
            steps(dve, run)

        def pe_peer(pe, l):
            pe_select(pe, l)
            pe.wait_ge(sem("select_done"), l + 1)
            pe_first_gates(pe, NKEYS * l)
            pe_experts(pe, NKEYS * l)

        def act_peer(act, l):
            act_select(act, l)
            act.wait_ge(sem("select_done"), l + 1)
            act_first_gates(act, NKEYS * l)
            act_experts(act, NKEYS * l)
            act_norm_roots(act)

        def dve_peer(dve, link, l):
            dve_select(dve, link, l)
            dve.wait_ge(sem("select_done"), l + 1)
            dve_first_gates(dve, NKEYS * l)
            dve_experts(dve, NKEYS * l)
            dve.wait_ge(sem("v_used"), NKEYS * (l + 1))
            for n in range(6):
                t, c = divmod(n, 2)
                dve_residual(dve, link, ps[n], 1, t, c, "peer_res", 6 * l + n + 1)
            dve_out_norm(dve, link, l, 1)

        @block.sync
        def _(sp):
            sp.dma_start(const[:, :], a["consts"][:, 0:WHERE["reverse"].start]).then_inc(sem("const_in"), 16)
            sp.dma_start(X[:, 0, :], a["x_prompt"][0]).then_inc(sem("x_in"), 16)
            sp.dma_start(X[:, 1:3, :], a["x_sample"][0].rearrange("(t p) d -> p t d", p=P)).then_inc(sem("x_in"), 16)
            for l in range(DEPTH):
                for c in range(NCHUNK):
                    n = chunk_no(l, c)
                    if n >= 2:
                        chunk_released(sp, n - 2)
                    if l and c < 2:
                        sp.wait_ge(sem("v_used"), NKEYS * l)
                    src, k, w = chunk_source(l, c)
                    sp.dma_start(slot(n, k, w), src).then_inc(sem(f"chunk_in{n % 2}"), 16)
                sp_experts(sp, l)

        @block.gpsimd
        def _(pool):
            link = linker(pool, "pool")
            pool.dma_start(crow[0:8, :], a["c_ctx"].rearrange("(k p) -> k p", p=P)).then_inc(sem("c_in"), 16)
            pool.dma_start(crow[8:16, :], a["c"][0].rearrange("(k p) -> k p", p=P)).then_inc(sem("c_in"), 16)
            for l in range(DEPTH):
                if l:
                    pool.wait_ge(sem("v_used"), NKEYS * l)
                for nm, n in PARAMS:
                    pool.dma_start(prow[PAR[nm]:PAR[nm] + n, :], par_srcs[nm](l)).then_inc(sem("param_in"), 16)
                for s in range(2):
                    pool.dma_start(bmod[s:s + 1, :], a["b_mod"][l:l + 1, :]).then_inc(sem("param_in"), 16)
                pool_decays(pool, l)
                pool_na(pool, l)
                pool_na_out(pool, l)
                pool_ret(pool, l)
                pool_ret_out(pool, l)
                pool_rwkv(pool, l)
                pool_rwkv_out(pool, l)
                ln_rows(pool, l, "ln_a_g", "ln_a_b", 0)
                pool_keys(pool, l)
                ln_rows(pool, l, "ln_f_g", "ln_f_b", 1)
                pool_select(pool, link, l)
                pool_gates(pool, l)
            pool.wait_ge(sem("x_done"), 2 * DEPTH * NT)
            pool.dma_start(y_prompt[0], X[:, 0, :]).then_inc(sem("stored"), 16)
            pool.dma_start(y_sample[0].rearrange("(t p) d -> p t d", p=P), X[:, 1:3, :]).then_inc(sem("stored"), 16)
            pool.wait_ge(sem("stored"), 16 * (DEPTH * 7 + 2))

        @block.tensor
        def _(pe):
            pe_cond(pe)
            for l in range(DEPTH):
                pe_mod(pe, l)
                pe_norm(pe, 2 * l)
                pe_proj(pe, l)
                pe_ret(pe, l)
                pe_rwkv(pe, l)
                pe_merge(pe, l)
                pe_norm(pe, 2 * l + 1)
                pe_peer(pe, l)

        @block.scalar
        def _(act):
            link = linker(act, "act")
            act_cond(act)
            for l in range(DEPTH):
                act_norm(act, 2 * l)
                act_proj(act, l)
                act_ret(act, link, l)
                act_rwkv(act, link, l)
                act_merge(act, l)
                act_norm(act, 2 * l + 1)
                act_peer(act, l)

        @block.vector
        def _(dve):
            link = linker(dve, "dve")
            dve_cond(dve)
            for l in range(DEPTH):
                dve_mod(dve, l)
                dve_norm(dve, link, 2 * l)
                dve_proj(dve, link, l)
                dve_ret(dve, link, l)
                dve_rwkv(dve, link, l)
                dve_merge(dve, link, l)
                dve_norm(dve, link, 2 * l + 1)
                dve_peer(dve, link, l)


INS = ["x_prompt", "x_sample", "cache_na_k", "cache_na_v", "state_ret", "state_rwkv", "c", "c_ctx", "w_mod", "b_mod", "w_in",
       "na_rpb", "ret_decay_logit", "ret_gn_w", "ret_gn_b", "rwkv_mu", "rwkv_w0", "rwkv_w_up", "rwkv_a0", "rwkv_a_up",
       "rwkv_g_up", "rwkv_k_k", "rwkv_k_a", "rwkv_r_k", "rwkv_gn_w", "rwkv_gn_b", "w_br", "w_out", "ln_a_g", "ln_a_b",
       "ln_f_g", "ln_f_b", "peer_wq", "peer_keys", "peer_u", "peer_v"]
OUTS = [(1, 128, 1024), (1, 256, 1024), (1, 2, 8, 128, 64), (1, 2, 8, 128, 64), (1, 2, 2, 4, 64, 128), (1, 2, 2, 8, 64, 64)]


def kernel(**inputs):
    import concourse.bacc as bacc
    from concourse.bass_utils import run_bass_kernel_spmd

    nc = bacc.Bacc("TRN2", target_bir_lowering=False, num_devices=1)
    arrays, args = {}, {}
    for name in INS + ["consts"]:
        x = CONSTS if name == "consts" else np.ascontiguousarray(inputs[name])
        arrays[f"in_{name}"] = x
        args[name] = nc.dram_tensor(f"in_{name}", x.shape, mybir.dt.from_np(x.dtype), kind="ExternalInput").ap()
    outs = [nc.dram_tensor(f"out_{i}", s, F32, kind="ExternalOutput").ap() for i, s in enumerate(OUTS)]
    build(nc, args, outs)
    r = run_bass_kernel_spmd(nc, [arrays], core_ids=[0])
    return tuple(r.results[0][f"out_{i}"] for i in range(len(OUTS)))
```
